# Optimizing a Trainium2 kernel written in Bass

```python
import math
import jax, jax.numpy as jnp
from jax import lax
import numpy as np

D_MODEL = 1024
BATCH = 1
SEQ = 512
DEPTH = 2

GRID_W = 64
CTX_LEN = 256
HEAD_DIM = 64
ATTN_SCALE = HEAD_DIM ** -0.5
Q_BLOCK = 128
ROPE_BASE = 10000.0
ROPE_AXIS_DIM = HEAD_DIM // 2
ROPE_PAIRS_PER_AXIS = ROPE_AXIS_DIM // 2
EPS = 1e-6

POOL_WINDOWS = (2, 4, 8, 16)
POOL_GROUPS = len(POOL_WINDOWS)
POOL_WIDTH = D_MODEL // 2
POOL_GROUP_DIM = POOL_WIDTH // POOL_GROUPS

DIFF_HEADS = D_MODEL // 256
DIFF_WIDTH = DIFF_HEADS * 2 * HEAD_DIM

GQA_HEADS = D_MODEL // 128
GQA_KV_HEADS = GQA_HEADS // 4
GQA_GROUP = GQA_HEADS // GQA_KV_HEADS
GQA_WIDTH = GQA_HEADS * HEAD_DIM
GQA_KV_WIDTH = GQA_KV_HEADS * HEAD_DIM

N_BRANCH = 3
D_FF = 4 * D_MODEL

Q_SIDE_SPLITS = (POOL_WIDTH, POOL_WIDTH + DIFF_WIDTH, POOL_WIDTH + DIFF_WIDTH + GQA_WIDTH)
KV_OFF = POOL_WIDTH + DIFF_WIDTH + GQA_WIDTH + N_BRANCH * D_MODEL
KV_SPLITS = (DIFF_WIDTH, 2 * DIFF_WIDTH, 2 * DIFF_WIDTH + GQA_KV_WIDTH)
IN_WIDTH = KV_OFF + 2 * DIFF_WIDTH + 2 * GQA_KV_WIDTH

kernel_name = 'hybrid_pool_diffattn_gqa_prefix_dit_block'

def _rms_norm(x, g):
    xf = x.astype(jnp.float32)
    y = xf * lax.rsqrt(jnp.mean(xf * xf, axis=-1, keepdims=True) + EPS)
    return (y * g.astype(jnp.float32)).astype(x.dtype)

def _modulate(h, shift, scale):
    return h * (1 + scale) + shift

def _rope_tables(rows):
    row = jnp.repeat(jnp.arange(rows), GRID_W).astype(jnp.float32)
    col = jnp.tile(jnp.arange(GRID_W), rows).astype(jnp.float32)
    inv = 1.0 / (ROPE_BASE ** (jnp.arange(ROPE_PAIRS_PER_AXIS, dtype=jnp.float32) * 2.0 / ROPE_AXIS_DIM))
    ang = jnp.concatenate([row[:, None] * inv, col[:, None] * inv], axis=-1)
    return jnp.cos(ang), jnp.sin(ang)

def _rope(x, cos, sin):
    xf = x.astype(jnp.float32).reshape(x.shape[:-1] + (HEAD_DIM // 2, 2))
    x0, x1 = xf[..., 0], xf[..., 1]
    out = jnp.stack([x0 * cos - x1 * sin, x0 * sin + x1 * cos], axis=-1)
    return out.reshape(x.shape).astype(x.dtype)

def _heads(x, n):
    b, l, w = x.shape
    return x.reshape(b, l, n, w // n).transpose(0, 2, 1, 3)

def _merge_heads(o):
    b, h, l, d = o.shape
    return o.transpose(0, 2, 1, 3).reshape(b, l, h * d)

def _probs(s):
    return jax.nn.softmax(s.astype(jnp.float32) * ATTN_SCALE, axis=-1)

def _sweep_query_blocks(block_fn, queries):
    n = queries[0].shape[-2]
    nb = n // Q_BLOCK

    def split(q):
        q = q.reshape(q.shape[:-2] + (nb, Q_BLOCK, q.shape[-1]))
        return jnp.moveaxis(q, -3, 0)

    out = lax.map(lambda blk: block_fn(*blk), tuple(split(q) for q in queries))
    out = jnp.moveaxis(out, 0, -3)
    return out.reshape(out.shape[:-3] + (n, out.shape[-1]))

def _pool_mixer(z, w_grp, scale):
    b, l, _ = z.shape
    zg = z.reshape(b, l, POOL_GROUPS, POOL_GROUP_DIM)
    zf = zg.astype(jnp.float32)
    cs = jnp.concatenate([jnp.zeros((b, 1, POOL_GROUPS, POOL_GROUP_DIM), jnp.float32),
                          jnp.cumsum(zf, axis=1)], axis=1)
    t = jnp.arange(l)
    means = []
    for g, w in enumerate(POOL_WINDOWS):
        lo = jnp.clip(t - w // 2, 0, l)
        hi = jnp.clip(t + w // 2, 0, l)
        cnt = (hi - lo).astype(jnp.float32)[None, :, None]
        means.append((cs[:, hi, g] - cs[:, lo, g]) / cnt)
    pooled = (jnp.stack(means, axis=2) - zf).astype(z.dtype)
    mixed = jnp.einsum('blgc,gcd->blgd', pooled, w_grp)
    return mixed.reshape(b, l, POOL_WIDTH) * scale

def _diff_lambda(lq1, lk1, lq2, lk2, lam_init):
    def e(a, b):
        return jnp.exp(jnp.sum(a.astype(jnp.float32) * b.astype(jnp.float32)))
    return e(lq1, lk1) - e(lq2, lk2) + lam_init

def _diff_attention(q1, q2, k1, k2, v, lam, sub_gain, lam_init):
    def block(a, b):
        p = (_probs(jnp.einsum('bhqd,bhkd->bhqk', a, k1))
             - lam * _probs(jnp.einsum('bhqd,bhkd->bhqk', b, k2)))
        return jnp.einsum('bhqk,bhkd->bhqd', p.astype(v.dtype), v)

    o = _sweep_query_blocks(block, (q1, q2))
    o = _rms_norm(o, sub_gain) * (1.0 - lam_init)
    return _merge_heads(o)

def _gq_attention(q, k, v):
    b, h, l, d = q.shape
    qg = q.reshape(b, GQA_KV_HEADS, GQA_GROUP, l, d)

    def block(a):
        p = _probs(jnp.einsum('bhgqd,bhkd->bhgqk', a, k))
        return jnp.einsum('bhgqk,bhkd->bhgqd', p.astype(v.dtype), v)

    o = _sweep_query_blocks(block, (qg,))
    return _merge_heads(o.reshape(b, h, l, d))

def _kv_heads(kv_part, k_gain, cos, sin):
    dk, dv, gk, gv = jnp.split(kv_part, KV_SPLITS, axis=-1)
    dk = _heads(dk, DIFF_HEADS)
    k1, k2 = dk[..., :HEAD_DIM], dk[..., HEAD_DIM:]
    dv = _heads(dv, DIFF_HEADS)
    gk = _rms_norm(_heads(gk, GQA_KV_HEADS), k_gain)
    gv = _heads(gv, GQA_KV_HEADS)
    if cos is not None:
        k1, k2, gk = _rope(k1, cos, sin), _rope(k2, cos, sin), _rope(gk, cos, sin)
    return (k1, k2, dv, gk, gv)

def _mix(q_part, keys, lp, lam, lam_init, cos, sin):
    pool_in, dq, gq, gates = jnp.split(q_part, Q_SIDE_SPLITS, axis=-1)
    k1, k2, dv, gk, gv = keys
    dq = _heads(dq, DIFF_HEADS)
    q1, q2 = dq[..., :HEAD_DIM], dq[..., HEAD_DIM:]
    gq = _rms_norm(_heads(gq, GQA_HEADS), lp['gqa_q_norm'])
    if cos is not None:
        q1, q2, gq = _rope(q1, cos, sin), _rope(q2, cos, sin), _rope(gq, cos, sin)
    pool_out = _pool_mixer(pool_in, lp['w_pool_grp'], lp['pool_scale'])
    diff_out = _diff_attention(q1, q2, k1, k2, dv, lam, lp['diff_subln'], lam_init)
    gqa_out = _gq_attention(gq, gk, gv)
    b, l, _ = gates.shape
    g = jax.nn.sigmoid(gates.reshape(b, l, N_BRANCH, D_MODEL))
    merged = (g[:, :, 0] * (pool_out @ lp['w_pool_out'])
              + g[:, :, 1] * (diff_out @ lp['w_diff_out'])
              + g[:, :, 2] * (gqa_out @ lp['w_gqa_out']))
    return merged @ lp['w_o']

def _mlp(h, w1, w2):
    return jnp.square(jax.nn.relu(h @ w1)) @ w2

def _layer(x, ctx, c, c_ctx, lp, lam_init, cos, sin, update_ctx):
    sh_a, sc_a, gt_a, sh_f, sc_f, gt_f = jnp.split(
        (jax.nn.silu(c) @ lp['w_mod'] + lp['b_mod'])[:, None, :], 6, axis=-1)
    csh_a, csc_a, cgt_a, csh_f, csc_f, cgt_f = jnp.split(
        jax.nn.silu(c_ctx) @ lp['w_mod'] + lp['b_mod'], 6, axis=-1)
    lam = _diff_lambda(lp['lambda_q1'], lp['lambda_k1'], lp['lambda_q2'], lp['lambda_k2'], lam_init)

    h_lat = _modulate(_rms_norm(x, lp['g_pre_mix']), sh_a, sc_a)
    h_ctx = _modulate(_rms_norm(ctx, lp['g_pre_mix']), csh_a, csc_a)

    p_lat = h_lat @ lp['w_in']
    p_ctx = h_ctx @ lp['w_in'] if update_ctx else h_ctx @ lp['w_in'][:, KV_OFF:]
    ctx_kv = _kv_heads(p_ctx[..., -(IN_WIDTH - KV_OFF):], lp['gqa_k_norm'], None, None)
    lat_kv = _kv_heads(p_lat[..., KV_OFF:], lp['gqa_k_norm'], cos, sin)
    keys = tuple(jnp.concatenate([kc, kl], axis=2) for kc, kl in zip(ctx_kv, lat_kv))

    y_lat = _mix(p_lat[..., :KV_OFF], keys, lp, lam, lam_init, cos, sin)
    x = x + gt_a * _rms_norm(y_lat, lp['g_post_mix'])
    hf = _modulate(_rms_norm(x, lp['g_pre_ffn']), sh_f, sc_f)
    x = x + gt_f * _rms_norm(_mlp(hf, lp['w_ff1'], lp['w_ff2']), lp['g_post_ffn'])

    if update_ctx:
        y_ctx = _mix(p_ctx[..., :KV_OFF], ctx_kv, lp, lam, lam_init, None, None)
        ctx = ctx + cgt_a * _rms_norm(y_ctx, lp['g_post_mix'])
        hc = _modulate(_rms_norm(ctx, lp['g_pre_ffn']), csh_f, csc_f)
        ctx = ctx + cgt_f * _rms_norm(_mlp(hc, lp['w_ff1'], lp['w_ff2']), lp['g_post_ffn'])
    return x, ctx

def setup_inputs(seed: int = 0) -> dict:
    key = jax.random.key(seed)
    ks = jax.random.split(key, 32)

    def nrm(k, shape, scale):
        return jax.random.normal(k, shape, jnp.float32) * scale

    def gain(k, shape):
        return 1.0 + 0.02 * jax.random.normal(k, shape, jnp.float32)

    return {
        'x': nrm(ks[0], (BATCH, SEQ, D_MODEL), 1.0),
        'c': nrm(ks[1], (BATCH, D_MODEL), 1.0),
        'ctx': nrm(ks[2], (BATCH, CTX_LEN, D_MODEL), 1.0),
        'c_ctx': nrm(ks[3], (D_MODEL,), 1.0),
        'w_mod': nrm(ks[4], (DEPTH, D_MODEL, 6 * D_MODEL), D_MODEL ** -0.5),
        'b_mod': nrm(ks[5], (DEPTH, 6 * D_MODEL), 0.01),
        'g_pre_mix': gain(ks[6], (DEPTH, D_MODEL)),
        'g_post_mix': gain(ks[7], (DEPTH, D_MODEL)),
        'g_pre_ffn': gain(ks[8], (DEPTH, D_MODEL)),
        'g_post_ffn': gain(ks[9], (DEPTH, D_MODEL)),
        'w_in': nrm(ks[10], (DEPTH, D_MODEL, IN_WIDTH), D_MODEL ** -0.5),
        'w_pool_grp': nrm(ks[11], (DEPTH, POOL_GROUPS, POOL_GROUP_DIM, POOL_GROUP_DIM), POOL_GROUP_DIM ** -0.5),
        'pool_scale': gain(ks[12], (DEPTH, POOL_WIDTH)),
        'lambda_q1': nrm(ks[13], (DEPTH, HEAD_DIM), 0.1),
        'lambda_k1': nrm(ks[14], (DEPTH, HEAD_DIM), 0.1),
        'lambda_q2': nrm(ks[15], (DEPTH, HEAD_DIM), 0.1),
        'lambda_k2': nrm(ks[16], (DEPTH, HEAD_DIM), 0.1),
        'diff_subln': gain(ks[17], (DEPTH, 2 * HEAD_DIM)),
        'gqa_q_norm': gain(ks[18], (DEPTH, HEAD_DIM)),
        'gqa_k_norm': gain(ks[19], (DEPTH, HEAD_DIM)),
        'w_pool_out': nrm(ks[20], (DEPTH, POOL_WIDTH, D_MODEL), POOL_WIDTH ** -0.5),
        'w_diff_out': nrm(ks[21], (DEPTH, DIFF_WIDTH, D_MODEL), DIFF_WIDTH ** -0.5),
        'w_gqa_out': nrm(ks[22], (DEPTH, GQA_WIDTH, D_MODEL), GQA_WIDTH ** -0.5),
        'w_o': nrm(ks[23], (DEPTH, D_MODEL, D_MODEL), D_MODEL ** -0.5),
        'w_ff1': nrm(ks[24], (DEPTH, D_MODEL, D_FF), D_MODEL ** -0.5),
        'w_ff2': nrm(ks[25], (DEPTH, D_FF, D_MODEL), D_FF ** -0.5),
    }

def reference(x, c, ctx, c_ctx, w_mod, b_mod, g_pre_mix, g_post_mix, g_pre_ffn, g_post_ffn,
              w_in, w_pool_grp, pool_scale, lambda_q1, lambda_k1, lambda_q2, lambda_k2,
              diff_subln, gqa_q_norm, gqa_k_norm, w_pool_out, w_diff_out, w_gqa_out, w_o,
              w_ff1, w_ff2):
    rows = x.shape[1] // GRID_W
    cos, sin = _rope_tables(rows)
    for i in range(DEPTH):
        lp = {
            'w_mod': w_mod[i], 'b_mod': b_mod[i],
            'g_pre_mix': g_pre_mix[i], 'g_post_mix': g_post_mix[i],
            'g_pre_ffn': g_pre_ffn[i], 'g_post_ffn': g_post_ffn[i],
            'w_in': w_in[i], 'w_pool_grp': w_pool_grp[i], 'pool_scale': pool_scale[i],
            'lambda_q1': lambda_q1[i], 'lambda_k1': lambda_k1[i],
            'lambda_q2': lambda_q2[i], 'lambda_k2': lambda_k2[i],
            'diff_subln': diff_subln[i], 'gqa_q_norm': gqa_q_norm[i], 'gqa_k_norm': gqa_k_norm[i],
            'w_pool_out': w_pool_out[i], 'w_diff_out': w_diff_out[i], 'w_gqa_out': w_gqa_out[i],
            'w_o': w_o[i], 'w_ff1': w_ff1[i], 'w_ff2': w_ff2[i],
        }
        lam_init = 0.8 - 0.6 * math.exp(-0.3 * i)
        x, ctx = _layer(x, ctx, c, c_ctx, lp, lam_init, cos, sin, i < DEPTH - 1)
    return x


_drawn_inputs = setup_inputs


def setup_inputs(seed=0):
    import zlib

    import numpy as np

    out = dict(_drawn_inputs(seed))
    spreads = {}
    factors = {'b_mod': 2.859,
     'g_pre_mix': 4.054,
     'g_post_mix': 4.201,
     'g_pre_ffn': 4.488,
     'g_post_ffn': 4.542,
     'pool_scale': 5.723,
     'lambda_q1': 5.231,
     'lambda_k1': 5.468,
     'lambda_q2': 4.392,
     'lambda_k2': 5.17,
     'diff_subln': 48.589,
     'gqa_q_norm': 8.0,
     'gqa_k_norm': 8.0}
    for name, (base, spread) in spreads.items():
        noise = np.random.default_rng([zlib.crc32(name.encode()), seed]).standard_normal(out[name].shape)
        drawn = base * np.exp(spread * noise) if base else spread * noise
        out[name] = __import__('jax').numpy.asarray(drawn.astype(out[name].dtype))
    for name, factor in factors.items():
        out[name] = (out[name] * factor).astype(out[name].dtype)
    return out
```

```python
import math
from contextlib import ExitStack

import concourse.bass as bass
from concourse import mybir

F32 = mybir.dt.float32
F32R = mybir.dt.float32r
ALU = mybir.AluOpType
ACT = mybir.ActivationFunctionType
AX = mybir.AxisListType

P = 128
D = 1024
KT = D // P
SEQ, CTX = 512, 256
T = SEQ + CTX
TT = T // P
CTX_TILES = CTX // P
DEPTH = 2
HD = 64
SCALE = HD ** -0.5
EPS = 1e-6
POOL_WINDOWS = (2, 4, 8, 16)
POOL_W = DIFF_W = GQA_W = 512
DIFF_HEADS, GQA_HEADS, KV_HEADS = 4, 8, 2
GROUP = GQA_HEADS // KV_HEADS
GATE_OFF = POOL_W + DIFF_W + GQA_W
KV_OFF = GATE_OFF + 3 * D
DK_OFF, DV_OFF = KV_OFF, KV_OFF + DIFF_W
GK_OFF = KV_OFF + 2 * DIFF_W
GV_OFF = GK_OFF + KV_HEADS * HD
D_FF = 4 * D
FB = 512
NB = D_FF // FB
NPANEL = DIFF_HEADS + KV_HEADS
RING, RAW = 4, 4
UNIT = KT * P
CH = 256
NCH = T // CH
ZPAD = 8
R_C, R_CC, R_GPM, R_GQM, R_GPF, R_GQF = range(0, 48, 8)
R_BMOD, R_PSC, R_SUB, ROWS = 48, 96, 100, 101


def lambda_init(layer):
    return 0.8 - 0.6 * math.exp(-0.3 * layer)


class Units:

    def __init__(self):
        self.n = 0
        self.used = 0
        self.landed = [0] * RAW
        self.in_slot, self.in_raw = {}, {}

    def phase(self, slots, raws, iters=1, dmas=None):
        return Phase(self, slots, raws, iters, dmas or [1] * len(slots))


class Phase:

    def __init__(self, units, slots, raws, iters, dmas):
        self.slots, self.raws, self.B = slots, raws, len(slots)
        self.base, self.used0 = units.n, units.used
        self.land0 = list(units.landed)
        self.per = [sum(16 * d for r, d in zip(raws, dmas) if r == q) for q in range(RAW)]
        seen = [0] * RAW
        self.rank = []
        for r, d in zip(raws, dmas):
            seen[r] += 16 * d
            self.rank.append(seen[r])
        self.first_slot, self.first_raw = dict(units.in_slot), dict(units.in_raw)
        for j in range(self.B):
            units.in_slot[slots[j]] = units.used + self.B * (iters - 1) + j + 1
            units.in_raw[raws[j]] = units.n + self.B * (iters - 1) + j + 1
        self.iters = iters
        units.n += self.B * iters
        units.used += self.B * iters
        for q in range(RAW):
            units.landed[q] += self.per[q] * iters

    def landed(self, j, i):
        r = self.raws[j]
        return i * self.per[r] + (self.land0[r] + self.rank[j])

    def index(self, j, i):
        return i * self.B + (self.base + j)

    def _free(self, slots, first, base, j, i):
        earlier = [q for q in range(j) if slots[q] == slots[j]]
        if earlier:
            return i * self.B + (base + earlier[-1] + 1)
        if self.iters == 1:
            return first[slots[j]]
        return i * self.B + (base + 1 - self.B + max(q for q in range(self.B) if slots[q] == slots[j]))

    def raw_free(self, j, i):
        return self._free(self.raws, self.first_raw, self.base, j, i)

    def slot_free(self, j, i):
        return self._free(self.slots, self.first_slot, self.used0, j, i)


def build(nc, a, out):
    top = ExitStack()
    with top:
        def sb(name, shape, dt=F32, ctx=top):
            return ctx.enter_context(nc.sbuf_tensor(name, shape, dt))

        def sem(name):
            return top.enter_context(nc.semaphore(name))

        raw = [sb(f"raw{s}", [P, UNIT]) for s in range(RAW)]
        whi3 = sb("whi3", [P, 3, KT, P], F32R)
        wlo3 = sb("wlo3", [P, 3, KT, P], F32R)
        Hhi = sb("Hhi", [P, KT, T], F32R)
        Hlo = sb("Hlo", [P, KT, T], F32R)
        A = sb("A", [P, KT, T])
        ident = sb("ident", [P, P])
        ones = sb("ones", [P, P])
        cosT = sb("cosT", [P, SEQ // P, HD])
        sinT = sb("sinT", [P, SEQ // P, HD])
        vec = sb("vec", [P, ROWS])
        mod = sb("mod", [P, 6 * KT, 2])
        csil = sb("csil", [P, KT, 2])
        preA = sb("preA", [P, KT, 2])
        postA = sb("postA", [P, KT, 2])
        preF = sb("preF", [P, KT, 2])
        postF = sb("postF", [P, KT, 2])
        headG = sb("headG", [P, GROUP + 1, HD])
        subg = sb("subg", [P, 1])
        lams = sb("lams", [P, 2])
        lame = sb("lame", [P, 2])
        lam = sb("lam", [P, 1])
        mhalf = sb("mhalf", [P, 8])
        xdram = nc.dram_tensor("x_spill", [P, KT * T], F32, kind="Internal").ap()

        psum = top.enter_context(nc.psum_tensor("psum", [P, 8, 512], F32))

        landed = [sem(f"landed{s}") for s in range(RAW)]
        hi_ready, lo_ready, unit_used = sem("hi_ready"), sem("lo_ready"), sem("unit_used")
        setup_in, setup_step, setup_pool = sem("setup_in"), sem("setup_step"), sem("setup_pool")
        units = Units()

        def whi(j):
            return whi3[:, j] if j < 3 else whi_x[0][:]

        def wlo(j):
            return wlo3[:, j] if j < 3 else wlo_x[0][:]

        whi_x, wlo_x = [None], [None]

        def fourth_slot(ctx, tag):
            whi_x[0] = sb(f"whi_{tag}", [P, KT, P], F32R, ctx)
            wlo_x[0] = sb(f"wlo_{tag}", [P, KT, P], F32R, ctx)

        def split_hi(act, ph, j, i, wait_slot=True):
            act.wait_ge(landed[ph.raws[j]], ph.landed(j, i))
            if wait_slot:
                act.wait_ge(unit_used, ph.slot_free(j, i))
            dst = whi(ph.slots[j]).rearrange("p k n -> p (k n)")
            nc.scalar.activation(dst, raw[ph.raws[j]][:], ACT.Copy).then_inc(hi_ready, 1)

        def split_lo(dve, ph, j, i):
            dve.wait_ge(hi_ready, ph.index(j, i) + 1)
            dst = wlo(ph.slots[j]).rearrange("p k n -> p (k n)")
            hi = whi(ph.slots[j]).rearrange("p k n -> p (k n)").bitcast(F32)
            nc.vector.tensor_tensor(dst, raw[ph.raws[j]][:], hi, ALU.subtract).then_inc(lo_ready, 1)

        def load_unit(sp, ph, j, i, pieces):
            sp.wait_ge(lo_ready, ph.raw_free(j, i))
            for dst, src in pieces:
                sp.dma_start(dst, src).then_inc(landed[ph.raws[j]], 16)

        def slot_view(s, k=KT):
            return raw[s][:].rearrange("p (k n) -> p k n", k=k)

        def three_terms(out_ap, w_h, w_l, x_h, x_l, chunks, first, last):
            mm = None
            for n, (w, x) in enumerate(((w_h, x_h), (w_h, x_l), (w_l, x_h))):
                for bank, c0, cn in chunks:
                    mm = nc.tensor.matmul(out_ap[:, bank, 0:cn], w, x[:, c0:c0 + cn],
                                          start=first and n == 0, stop=last and n == 2)
            return mm

        with ExitStack() as z:
            xt = sb("x_rows", [P, TT, D], F32, z)
            x_in, x_turned, x_kept = sem("x_in"), sem("x_turned"), sem("x_kept")
            block = z.enter_context(nc.Block())

            @block.sync
            def _(sp):
                sp.dma_start(ident[:], a["identity"]).then_inc(setup_in, 16)
                sp.dma_start(xt[:, 0:CTX_TILES], a["ctx"].rearrange("b (t p) d -> p (b t) d", p=P)).then_inc(x_in, 16)
                sp.dma_start(xt[:, CTX_TILES:TT], a["x"].rearrange("b (t p) d -> p (b t) d", p=P)).then_inc(x_in, 16)
                sp.dma_start(cosT[:], a["cos"].rearrange("(t p) d -> p t d", p=P)).then_inc(setup_in, 16)
                sp.dma_start(sinT[:], a["sin"].rearrange("(t p) d -> p t d", p=P)).then_inc(setup_in, 16)
                sp.wait_ge(setup_in, 48)

            @block.gpsimd
            def _(pool):
                nc.gpsimd.memset(ones[:], 1.0).then_inc(setup_pool, 1)
                nc.gpsimd.memset(mhalf[:], -0.5).then_inc(setup_pool, 1)

            @block.tensor
            def _(pe):
                pe.wait_ge(setup_in, 48)
                pe.wait_ge(x_in, 32)
                for t in range(TT):
                    for h in range(2):
                        g = 2 * t + h
                        if g >= 8:
                            pe.wait_ge(x_kept, g - 7)
                        for k in range(4):
                            f = 4 * h + k
                            mm = nc.tensor.transpose(psum[:, g % 8, k * P:(k + 1) * P],
                                                     xt[:, t, f * P:(f + 1) * P], ident[:])
                        mm.then_inc(x_turned, 1)

            @block.vector
            def _(dve):
                for g in range(2 * TT):
                    t, h = g // 2, g % 2
                    dve.wait_ge(x_turned, g + 1)
                    nc.vector.tensor_copy(A[:, 4 * h:4 * h + 4, t * P:(t + 1) * P],
                                          psum[:, g % 8].rearrange("p (k n) -> p k n", k=4)).then_inc(x_kept, 1)

        MU, MS = 12, 3
        m_in, m_vec, m_loaded = sem("m_in"), sem("m_vec"), [sem(f"m_loaded{s}") for s in range(MS)]
        m_turned, m_step, m_sig, m_exp = sem("m_turned"), sem("m_step"), sem("m_sig"), sem("m_exp")

        def modulation(layer):
            with ExitStack() as z:
                rows = sb(f"rows{layer}", [P, P], F32, z)
                lamv = sb(f"lamv{layer}", [P, 4, HD], F32, z)
                lamp = sb(f"lamp{layer}", [P, 2, HD], F32, z)
                sg = sb(f"sg{layer}", [P, 2 * KT], F32, z)
                wm = [sb(f"wm{layer}_{s}", [P, KT, 512], F32, z) for s in range(MS)]
                block = z.enter_context(nc.Block())
                lin = 16 * 9 * (layer + 1)
                l0 = MU // MS * 16 * layer
                used0 = units.used
                units.used += MU

                @block.sync
                def _(sp):
                    for r, src in ((R_C, a["c"].rearrange("b (k p) -> (b k) p", p=P)),
                                   (R_CC, a["c_ctx"].rearrange("(k p) -> k p", p=P)),
                                   (R_GPM, a["g_pre_mix"][layer].rearrange("(k p) -> k p", p=P)),
                                   (R_GQM, a["g_post_mix"][layer].rearrange("(k p) -> k p", p=P)),
                                   (R_GPF, a["g_pre_ffn"][layer].rearrange("(k p) -> k p", p=P)),
                                   (R_GQF, a["g_post_ffn"][layer].rearrange("(k p) -> k p", p=P)),
                                   (R_BMOD, a["b_mod"][layer].rearrange("(k p) -> k p", p=P)),
                                   (R_PSC, a["pool_scale"][layer].rearrange("(k p) -> k p", p=P)),
                                   (R_SUB, a["diff_subln"][layer].rearrange("(k p) -> k p", p=P))):
                        sp.dma_start(rows[r:r + src.shape[0], :], src).then_inc(m_vec, 16)
                    src = a["w_mod"][layer].rearrange("(k p) n -> p k n", p=P)
                    for s in range(MS):
                        sp.dma_start(wm[s][:], src[:, :, s * 512:(s + 1) * 512]).then_inc(m_loaded[s], 16)
                    with sp.Fori(1, MU // MS) as i:
                        for s in range(MS):
                            off = sp.snap(i * (MS * 512) + s * 512)
                            done = sp.snap(i * MS + (used0 + s + 1 - MS))
                            sp.wait_ge(unit_used, done)
                            sp.dma_start(wm[s][:], src[:, :, bass.ds(off, 512)]).then_inc(m_loaded[s], 16)

                @block.gpsimd
                def _(pool):
                    for g in range(GROUP + 1):
                        g_dram = a["gqa_q_norm" if g < GROUP else "gqa_k_norm"][layer]
                        pool.dma_start(headG[:, g, :], g_dram.rearrange("(o d) -> o d", o=1).broadcast_to([P, HD])
                                       ).then_inc(m_in, 16)
                    for n, name in enumerate(("lambda_q1", "lambda_k1", "lambda_q2", "lambda_k2")):
                        pool.dma_start(lamv[:, n, :], a[name][layer].rearrange("(o d) -> o d", o=1)
                                       .broadcast_to([P, HD])).then_inc(m_in, 16)

                @block.scalar
                def _(act):
                    act.wait_ge(m_step, 11 * layer + 1)
                    nc.scalar.activation(sg[:], vec[:, 0:2 * KT], ACT.Sigmoid).then_inc(m_sig, 1)
                    act.wait_ge(m_step, 11 * layer + 4)
                    nc.scalar.activation(lame[:], lams[:], ACT.Exp).then_inc(m_exp, 1)

                @block.tensor
                def _(pe):
                    pe.wait_ge(m_vec, 16 * 9 * (layer + 1))
                    nc.tensor.transpose(psum[:, 1, 0:ROWS], rows[0:ROWS, :], ident[0:ROWS, 0:ROWS]).then_inc(m_turned, 1)
                    pe.wait_ge(m_step, 11 * layer + 2)
                    with pe.Fori(0, MU // MS) as i:
                        for s in range(MS):
                            pe.wait_ge(m_loaded[s], i * 16 + (l0 + 16))
                            for q in range(4):
                                for k in range(KT):
                                    mm = nc.tensor.matmul(psum[:, 0, bass.ds(i * (MS * 8) + (s * 8 + q * 2), 2)],
                                                          wm[s][:, k, q * P:(q + 1) * P], csil[:, k, :],
                                                          start=k == 0, stop=k == KT - 1)
                            mm.then_inc(unit_used, 1)

                @block.vector
                def _(dve):
                    s0 = 11 * layer
                    dve.wait_ge(m_turned, layer + 1)
                    nc.vector.tensor_copy(vec[:], psum[:, 1, 0:ROWS]).then_inc(m_step, 1)
                    dve.wait_ge(m_sig, layer + 1)
                    nc.vector.tensor_tensor(csil[:].rearrange("p k s -> p s k"),
                                            vec[:, 0:2 * KT].rearrange("p (s k) -> p s k", s=2),
                                            sg[:].rearrange("p (s k) -> p s k", s=2), ALU.mult).then_inc(m_step, 1)
                    dve.wait_ge(m_in, lin)
                    nc.vector.tensor_tensor(lamp[:], lamv[:].rearrange("p (n q) d -> p q n d", q=2)[:, 0],
                                            lamv[:].rearrange("p (n q) d -> p q n d", q=2)[:, 1],
                                            ALU.mult).then_inc(m_step, 1)
                    dve.wait_ge(m_step, s0 + 3)
                    nc.vector.tensor_reduce(lams[:], lamp[:], AX.X, ALU.add).then_inc(m_step, 1)
                    dve.wait_ge(m_exp, layer + 1)
                    nc.vector.scalar_tensor_tensor(lam[:], lame[:, 0:1], lambda_init(layer), lame[:, 1:2],
                                                   ALU.add, ALU.subtract).then_inc(m_step, 1)
                    nc.vector.tensor_scalar(subg[:], vec[:, R_SUB:R_SUB + 1], 1.0 - lambda_init(layer), None,
                                            ALU.mult).then_inc(m_step, 1)
                    dve.wait_ge(unit_used, used0 + MU)
                    nc.vector.tensor_tensor(mod[:], psum[:, 0, 0:12 * KT].rearrange("p (k s) -> p k s", s=2),
                                            vec[:, R_BMOD:R_BMOD + 6 * KT].rearrange("p (k o) -> p k o", o=1)
                                            .broadcast_to([P, 6 * KT, 2]), ALU.add).then_inc(m_step, 1)
                    dve.wait_ge(m_step, s0 + 7)

                    def gain(r):
                        return vec[:, r:r + KT].rearrange("p (k o) -> p k o", o=1).broadcast_to([P, KT, 2])

                    nc.vector.scalar_tensor_tensor(preA[:], mod[:, KT:2 * KT], 1.0, gain(R_GPM), ALU.add, ALU.mult
                                                   ).then_inc(m_step, 1)
                    nc.vector.tensor_tensor(postA[:], mod[:, 2 * KT:3 * KT], gain(R_GQM), ALU.mult).then_inc(m_step, 1)
                    nc.vector.scalar_tensor_tensor(preF[:], mod[:, 4 * KT:5 * KT], 1.0, gain(R_GPF), ALU.add, ALU.mult
                                                   ).then_inc(m_step, 1)
                    nc.vector.tensor_tensor(postF[:], mod[:, 5 * KT:6 * KT], gain(R_GQF), ALU.mult).then_inc(m_step, 1)

        n_sq, n_acc, n_ss, n_var, n_pow, n_diag, n_bc, n_sc, n_x, n_aff, n_hi, n_lo = (
            sem(n) for n in ("n_sq", "n_acc", "n_ss", "n_var", "n_pow", "n_diag", "n_bc", "n_sc", "n_x", "n_aff",
                             "n_hi", "n_lo"))
        n_spill, n_reload = sem("n_spill"), sem("n_reload")
        count = {"r": 0, "x": 0, "h": 0, "spill": 0, "reload": 0}

        def norms(tag, chunks, X, gains=None, shift_at=0, Y=None, post=None, X_out=None, spill=False, reload=False):
            X_out = X if X_out is None else X_out
            with ExitStack() as z:
                sq = sb(f"sq_{tag}", [P, KT, CH], F32, z)
                t1 = sb(f"t1_{tag}", [P, KT, CH], F32, z)
                t2 = sb(f"t2_{tag}", [P, KT, CH], F32, z)
                acc = sb(f"acc_{tag}", [P, CH], F32, z)
                var = sb(f"var_{tag}", [P, 2], F32, z)
                rstd = sb(f"rstd_{tag}", [P, 2], F32, z)
                diag = sb(f"diag_{tag}", [P, 2, P], F32, z)
                passes = [(c, what) for c in chunks for what in (["Y"] if Y is not None else []) +
                          (["x"] if gains is not None else [])]
                r0, x0, h0 = count["r"], count["x"], count["h"]
                rl0, sp0 = count["reload"], count["spill"]
                count["r"] += len(passes)
                if Y is not None:
                    count["x"] += len(chunks)
                if gains is not None:
                    count["h"] += len(chunks)
                count["spill"] += 16 if spill else 0
                count["reload"] += 16 if reload else 0
                block = z.enter_context(nc.Block())

                def cols(c):
                    return slice(c * CH, (c + 1) * CH)

                def stream(c):
                    return 1 if c * CH < CTX else 0

                @block.sync
                def _(sp):
                    if reload:
                        sp.dma_start(X[:].rearrange("p k t -> p (k t)"), xdram).then_inc(n_reload, 16)
                    if spill:
                        sp.dma_start(xdram, X[:].rearrange("p k t -> p (k t)")).then_inc(n_spill, 16)
                        sp.wait_ge(n_spill, sp0 + 16)

                @block.scalar
                def _(act):
                    x, h = x0, h0
                    for n, (c, what) in enumerate(passes):
                        r = r0 + n
                        src = Y if what == "Y" else X_out
                        if what == "Y":
                            x += 1
                        elif Y is not None:
                            act.wait_ge(n_x, x)
                        if n:
                            act.wait_ge(n_acc, r)
                        nc.scalar.activation(sq[:], src[:, :, cols(c)], ACT.Square).then_inc(n_sq, 1)
                        if what == "x":
                            h += 1
                            act.wait_ge(n_sc, r + 1)
                            if h > h0 + 1:
                                act.wait_ge(n_lo, h - 1)
                            s = stream(c)
                            for k in range(KT):
                                aff = nc.scalar.activation(t2[:, k], t1[:, k], ACT.Identity,
                                                           bias=mod[:, shift_at + k, s:s + 1],
                                                           scale=gains[:, k, s:s + 1])
                            aff.then_inc(n_aff, 1)
                            act.wait_ge(n_aff, h)
                            nc.scalar.activation(Hhi[:, :, cols(c)], t2[:], ACT.Copy).then_inc(n_hi, 1)

                @block.vector
                def _(dve):
                    x, h = x0, h0
                    if reload:
                        dve.wait_ge(n_reload, rl0 + 16)
                    for n, (c, what) in enumerate(passes):
                        r = r0 + n
                        dve.wait_ge(n_sq, r + 1)
                        if n:
                            dve.wait_ge(n_ss, r)
                        nc.vector.tensor_reduce(acc[:], sq[:].rearrange("p k t -> p t k"), AX.X, ALU.add
                                                ).then_inc(n_acc, 1)
                        dve.wait_ge(n_ss, r + 1)
                        if n:
                            dve.wait_ge(n_pow, r)
                        nc.vector.tensor_scalar(var[:], psum[:, 0, 0:4].rearrange("p (t o) -> p t o", o=2)[:, :, 0],
                                                1.0 / D, EPS, ALU.mult, ALU.add).then_inc(n_var, 1)
                        dve.wait_ge(n_pow, r + 1)
                        if n:
                            dve.wait_ge(n_bc, r)
                        for t in range(2):
                            dg = nc.vector.tensor_scalar(diag[:, t], ident[:], rstd[:, t:t + 1], None, ALU.mult)
                        dg.then_inc(n_diag, 1)
                        dve.wait_ge(n_bc, r + 1)
                        src = Y if what == "Y" else X_out
                        if n:
                            dve.wait_ge(n_aff, h)
                        nc.vector.tensor_tensor(t1[:], src[:, :, cols(c)],
                                                psum[:, 1, 0:CH].rearrange("p (o t) -> p o t", o=1)
                                                .broadcast_to([P, KT, CH]), ALU.mult).then_inc(n_sc, 1)
                        s = stream(c)
                        if what == "Y":
                            x += 1
                            dve.wait_ge(n_sc, r + 1)
                            for k in range(KT):
                                up = nc.vector.scalar_tensor_tensor(X_out[:, k, cols(c)], t1[:, k],
                                                                    post[:, k, s:s + 1], X[:, k, cols(c)], ALU.mult,
                                                                    ALU.add)
                            up.then_inc(n_x, 1)
                        else:
                            h += 1
                            dve.wait_ge(n_hi, h)
                            nc.vector.tensor_tensor(Hlo[:, :, cols(c)], t2[:], Hhi[:, :, cols(c)].bitcast(F32),
                                                    ALU.subtract).then_inc(n_lo, 1)

                @block.gpsimd
                def _(pool):
                    for n in range(len(passes)):
                        r = r0 + n
                        pool.wait_ge(n_var, r + 1)
                        if n:
                            pool.wait_ge(n_diag, r)
                        nc.gpsimd.tensor_tensor(rstd[:], var[:], mhalf[:, 0:2], ALU.pow).then_inc(n_pow, 1)

                @block.tensor
                def _(pe):
                    for n in range(len(passes)):
                        r = r0 + n
                        pe.wait_ge(n_acc, r + 1)
                        if n:
                            pe.wait_ge(n_var, r)
                        for t in range(2):
                            mm = nc.tensor.matmul(psum[:, 0, 2 * t:2 * t + 2], acc[:, t * P:(t + 1) * P],
                                                  ones[:, 0:2], start=True, stop=True)
                        mm.then_inc(n_ss, 1)
                        pe.wait_ge(n_diag, r + 1)
                        if n:
                            pe.wait_ge(n_sc, r)
                        nc.tensor.matmul(psum[:, 1, 0:CH], ones[:], diag[:].rearrange("p t n -> p (t n)"),
                                         start=True, stop=True).then_inc(n_bc, 1)

        GEMM, SBANK, TR, OB = 0, 1, 5, 7

        def attention(layer):
            q_tiles = range(TT) if layer < DEPTH - 1 else range(CTX_TILES, TT)
            w_in = a["w_in"][layer].rearrange("(k p) n -> p k n", p=P)
            ph = units.phase([0, 1, 2] * NPANEL, [n % RAW for n in range(3 * NPANEL)], 1,
                             [1, 1, 1] * DIFF_HEADS + [1, 1, 2] * KV_HEADS)
            units.used -= 3 * NPANEL
            units.in_slot = {s: units.used for s in range(RING)}

            def sm(n):
                return sem(f"{n}_{layer}")

            gemm_done, act_read, dve_read = sm("gemm_done"), sm("act_read"), sm("dve_read")
            sq_done, head_var, head_pow = sm("sq_done"), sm("head_var"), sm("head_pow")
            roped, stack_hi, stack_lo, stacks_in = sm("roped"), sm("stack_hi"), sm("stack_lo"), sm("stacks_in")
            scores, negmax, exped, probs = sm("scores"), sm("negmax"), sm("exped"), sm("probs")
            turned, pt_hi, pt_lo, pv_done = sm("turned"), sm("pt_hi"), sm("pt_lo"), sm("pv_done")
            o_read, o_sq, o_var, o_pow, o_norm, o_out = (sm("o_read"), sm("o_sq"), sm("o_var"), sm("o_pow"),
                                                         sm("o_norm"), sm("o_out"))
            dchain = sm("dchain")

            class Prep:

                def __init__(s, g):
                    s.g, s.p, s.t = g, g // TT, g % TT
                    s.diff = s.p < DIFF_HEADS
                    s.q = s.t in q_tiles
                    s.nq = 2 if s.diff else GROUP
                    s.nk = 2 if s.diff else 1
                    s.vd = 2 * HD if s.diff else HD
                    s.g0 = 0 if s.q else s.nq
                    s.g1 = s.nq + s.nk
                    s.stacks = list(range(s.g0, 6))
                    s.uses = [s.stacks[i:i + 3] for i in range(0, len(s.stacks), 3)]
                    s.rope = s.t >= CTX_TILES

            class Item:

                def __init__(s, p, t, j):
                    s.p, s.t, s.j = p, t, j
                    s.diff = p < DIFF_HEADS
                    s.nkt = CTX_TILES if t < CTX_TILES else TT
                    s.keys = s.nkt * P
                    s.last = s.diff or j == GROUP - 1

            preps = [Prep(g) for g in range(NPANEL * TT)]
            items, slots = [], []
            for t in range(TT):
                slots.append(dict(preps=[preps[t]], item=None))
            for p in range(NPANEL):
                mine = [Item(p, t, j) for t in q_tiles for j in range(1 if p < DIFF_HEADS else GROUP)]
                nxt = preps[(p + 1) * TT:(p + 2) * TT]
                for n, it in enumerate(mine):
                    got = nxt[n * len(nxt) // len(mine):(n + 1) * len(nxt) // len(mine)]
                    slots.append(dict(preps=got, item=it))
                items += mine
            slots += [dict(preps=[], item=None) for _ in range(2)]
            n_score = n_use = n_ptuse = n_stuse = n_out = n_norm = n_dsq = 0
            readers = []
            for i, it in enumerate(items):
                it.i, it.scores = i, []
                for _ in range(2 if it.diff else 1):
                    it.scores.append(n_score)
                    n_score += 1
            for n, sl in enumerate(slots):
                sl["next"] = items[0] if n == TT - 1 else None
                if sl["item"] is not None and sl["item"].i + 1 < len(items):
                    sl["next"] = items[sl["item"].i + 1]
                nx = sl["next"]
                sl["urgent"] = any(nx is not None and nx.p == q.p for q in sl["preps"])
                sl["outs"] = []
            for n, sl in enumerate(slots):
                if sl["item"] is not None and sl["item"].last:
                    later = n + (2 if sl["item"].diff else 1)
                    slots[later]["outs"].append(sl["item"])
            for sl in slots:
                it = sl["item"]

                def stack_uses():
                    nonlocal n_use, n_stuse
                    for q in sl["preps"]:
                        q.use0, q.st0 = n_use, n_stuse
                        for _ in q.uses:
                            n_stuse += 1
                            readers.append((stacks_in, n_stuse))
                            n_use += 1

                if it is not None:
                    it.use0, it.pt0 = n_use, n_ptuse
                    it.ptuses = [list(range(k, min(k + 3, it.nkt))) for k in range(0, it.nkt, 3)]
                    for _ in it.ptuses:
                        n_ptuse += 1
                        readers.append((pt_lo, n_ptuse))
                        n_use += 1
                stack_uses()
                sl["stack_first"] = sl["urgent"] or it is None
                for o in sl["outs"]:
                    o.ouse = n_use
                    o.n_out = n_out
                    n_out += 1
                    readers.append((o_out, n_out))
                    n_use += 1
            kept = []
            for it in items:
                it.before = kept[n_norm - 2] if n_norm >= 2 else None
                if it.last:
                    kept.append(it)
                it.nrm = n_norm
                n_norm += it.last
                if it.diff:
                    it.dsq = n_dsq
                    n_dsq += 1
            gq = [q for q in preps if not q.diff]
            for n, q in enumerate(gq):
                q.hn = n

            with ExitStack() as z:
                qk = [sb(f"qk{b}_{layer}", [P, 6, T], F32R, z) for b in range(2)]
                vhi = [sb(f"vhi{b}_{layer}", [P, TT, 2 * HD], F32R, z) for b in range(2)]
                vlo = [sb(f"vlo{b}_{layer}", [P, TT, 2 * HD], F32R, z) for b in range(2)]
                e = [[sb(f"e{b}{s}_{layer}", [P, T], F32, z) for s in range(2)] for b in range(2)]
                pth = [sb(f"pth{b}_{layer}", [P, TT, P], F32R, z) for b in range(2)]
                ptl = [sb(f"ptl{b}_{layer}", [P, TT, P], F32R, z) for b in range(2)]
                ra = sb(f"ra_{layer}", [P, 5, HD], F32, z)
                rb = sb(f"rb_{layer}", [P, 5, HD], F32, z)
                rc = sb(f"rc_{layer}", [P, 5, HD], F32, z)
                st = sb(f"st_{layer}", [P, 6, 2 * HD], F32R, z)
                hsq = sb(f"hsq_{layer}", [P, 5, HD], F32, z)
                rd = sb(f"rd_{layer}", [P, 5, HD], F32, z)
                hss = sb(f"hss_{layer}", [P, 5], F32, z)
                hvar = sb(f"hvar_{layer}", [P, 5], F32, z)
                hpow = sb(f"hpow_{layer}", [P, 5], F32, z)
                mx = sb(f"mx_{layer}", [P, 2], F32, z)
                nmx = sb(f"nmx_{layer}", [P, 2, 2], F32, z)
                esum = sb(f"esum_{layer}", [P, 2, 2], F32, z)
                rec = sb(f"rec_{layer}", [P, 2, 2], F32, z)
                rlam = sb(f"rlam_{layer}", [P, 1], F32, z)
                osb = sb(f"osb_{layer}", [P, 2, P], F32, z)
                osq = sb(f"osq_{layer}", [P, P], F32, z)
                oss = sb(f"oss_{layer}", [P, 1], F32, z)
                ovar = sb(f"ovar_{layer}", [P, 1], F32, z)
                opow = sb(f"opow_{layer}", [P, 1], F32, z)
                onrm = sb(f"onrm_{layer}", [P, 2, 2 * P], F32, z)
                block = z.enter_context(nc.Block())

                @block.sync
                def _(sp):
                    for n in range(3 * NPANEL):
                        p, m = n // 3, n % 3
                        v = slot_view(ph.raws[n])
                        if p < DIFF_HEADS:
                            c = (POOL_W, DK_OFF, DV_OFF)[m] + p * 2 * HD
                            pieces = [(v, w_in[:, :, c:c + P])]
                        elif m < 2:
                            c = POOL_W + DIFF_W + (p - DIFF_HEADS) * GROUP * HD + m * P
                            pieces = [(v, w_in[:, :, c:c + P])]
                        else:
                            ck, cv = GK_OFF + (p - DIFF_HEADS) * HD, GV_OFF + (p - DIFF_HEADS) * HD
                            pieces = [(v[:, :, 0:HD], w_in[:, :, ck:ck + HD]), (v[:, :, HD:P], w_in[:, :, cv:cv + HD])]
                        if n >= RAW:
                            sp.wait_ge(lo_ready, ph.base + n - RAW + 1)
                        for dst, src in pieces:
                            sp.dma_start(dst, src).then_inc(landed[ph.raws[n]], 16)

                def panel_units(p):
                    return range(3 * p, 3 * p + 3) if p < NPANEL else ()

                def after_panel(sl):
                    return [q.p for q in sl["preps"] if q.t == TT - 1]

                @block.tensor
                def _(pe):
                    def gemm(q):
                        pe.wait_ge(lo_ready, ph.base + 3 * q.p + 3)
                        if q.g:
                            pe.wait_ge(act_read, q.g)
                            pe.wait_ge(dve_read, q.g)
                        u0 = 0 if q.q else (1 if q.diff else 2)
                        o = psum[:, GEMM, u0 * P:3 * P]
                        tok = slice(q.t * P, (q.t + 1) * P)
                        for k in range(KT):
                            for n, (x, w) in enumerate(((Hhi, whi3), (Hhi, wlo3), (Hlo, whi3))):
                                mm = nc.tensor.matmul(o, x[:, k, tok], w[:, u0:3, k, :],
                                                      start=k == 0 and n == 0, stop=k == KT - 1 and n == 2)
                        mm.then_inc(gemm_done, 1)

                    def bank(use):
                        if use >= 2:
                            pe.wait_ge(*readers[use - 2])
                        return psum[:, TR + use % 2]

                    def turn_stacks(q):
                        pe.wait_ge(stack_hi, q.g + 1)
                        pe.wait_ge(stack_lo, q.g + 1)
                        for u, group in enumerate(q.uses):
                            b = bank(q.use0 + u)
                            for n, sx in enumerate(group):
                                mm = nc.tensor.transpose(b[:, n * P:(n + 1) * P], st[:, sx, :].bitcast(F32), ident[:])
                            mm.then_inc(turned, 1)

                    def score(it):
                        b = qk[it.p % 2]
                        pe.wait_ge(stacks_in, preps[it.p * TT + TT - 1].st0 + len(preps[it.p * TT + TT - 1].uses))
                        tok = slice(it.t * P, (it.t + 1) * P)
                        for s, n in enumerate(it.scores):
                            if n >= 2:
                                pe.wait_ge(exped, n - 1)
                            qs = s if it.diff else it.j
                            ks = (2 + s, 4 + s) if it.diff else (4, 5)
                            for c in range((it.keys + 383) // 384):
                                w = min(384, it.keys)
                                for m in range(2):
                                    mm = nc.tensor.matmul(psum[:, SBANK + 2 * (n % 2) + c, 0:w], b[:, qs, tok],
                                                          b[:, ks[m], c * 384:c * 384 + w], start=m == 0, stop=m == 1)
                            mm.then_inc(scores, 1)

                    def turn_probs(it):
                        pe.wait_ge(probs, it.i + 1)
                        for u, kts in enumerate(it.ptuses):
                            b = bank(it.use0 + u)
                            for n, kt in enumerate(kts):
                                mm = nc.tensor.transpose(b[:, n * P:(n + 1) * P],
                                                         e[it.i % 2][0][:, kt * P:(kt + 1) * P], ident[:])
                            mm.then_inc(turned, 1)

                    def weigh(it):
                        vd = 2 * HD if it.diff else HD
                        pe.wait_ge(pt_hi, it.pt0 + len(it.ptuses))
                        pe.wait_ge(pt_lo, it.pt0 + len(it.ptuses))
                        if it.i:
                            pe.wait_ge(o_read, it.i)
                        x, y = pth[it.i % 2], ptl[it.i % 2]
                        vh, vl = vhi[it.p % 2], vlo[it.p % 2]
                        for kt in range(it.nkt):
                            for n, (w, v) in enumerate(((x, vh), (x, vl), (y, vh))):
                                mm = nc.tensor.matmul(psum[:, OB, 0:vd], w[:, kt, :], v[:, kt, 0:vd],
                                                      start=kt == 0 and n == 0, stop=kt == it.nkt - 1 and n == 2)
                        mm.then_inc(pv_done, 1)

                    def turn_out(it):
                        if it.diff:
                            pe.wait_ge(o_norm, it.dsq + 1)
                        else:
                            pe.wait_ge(o_read, it.i + 1)
                        b = bank(it.ouse)
                        for n in range(1 if it.diff else 2):
                            mm = nc.tensor.transpose(b[:, n * P:(n + 1) * P], onrm[:, it.nrm % 2, n * P:(n + 1) * P],
                                                     ident[:])
                        mm.then_inc(turned, 1)

                    for sl in slots:
                        for q in sl["preps"][:1]:
                            gemm(q)
                        if sl["item"] is not None:
                            turn_probs(sl["item"])
                        for n, q in enumerate(sl["preps"]):
                            if n:
                                gemm(q)
                            if sl["stack_first"]:
                                turn_stacks(q)
                        if sl["next"] is not None:
                            score(sl["next"])
                        if sl["item"] is not None:
                            weigh(sl["item"])
                        if not sl["stack_first"]:
                            for q in sl["preps"]:
                                turn_stacks(q)
                        for o in sl["outs"]:
                            turn_out(o)

                @block.scalar
                def _(act):
                    def hi_of_panel(p):
                        for n in panel_units(p):
                            act.wait_ge(landed[ph.raws[n]], ph.landed(n, 0))
                            if p:
                                act.wait_ge(gemm_done, TT * p)
                            nc.scalar.activation(whi3[:, n % 3].rearrange("p k n -> p (k n)"), raw[ph.raws[n]][:],
                                                 ACT.Copy).then_inc(hi_ready, 1)

                    def read_projection(q):
                        act.wait_ge(gemm_done, q.g + 1)
                        if not q.diff:
                            if q.hn:
                                act.wait_ge(head_var, q.hn)
                            nc.scalar.activation(hsq[:, q.g0:q.g1].rearrange("p g d -> p (g d)"),
                                                 psum[:, GEMM, q.g0 * HD:q.g1 * HD], ACT.Square).then_inc(sq_done, 1)
                        nc.scalar.activation(vhi[q.p % 2][:, q.t, 0:q.vd], psum[:, GEMM, 3 * P - q.vd:3 * P], ACT.Copy
                                             ).then_inc(act_read, 1)

                    def stack_his(q):
                        act.wait_ge(roped, q.g + 1)
                        if q.g:
                            last = preps[q.g - 1]
                            act.wait_ge(turned, last.use0 + len(last.uses))
                        if q.q:
                            nc.scalar.activation(st[:, 0:q.nq, 0:HD], rc[:, 0:q.nq], ACT.Copy)
                        k0 = q.nq
                        src = rc[:, q.nq:q.g1].rearrange("p g (o d) -> p g o d", o=1).broadcast_to([P, q.nk, 2, HD])
                        nc.scalar.activation(st[:, k0:k0 + q.nk].rearrange("p s (o d) -> p s o d", o=2), src, ACT.Copy
                                             ).then_inc(stack_hi, 1)

                    def keep_stacks(q):
                        for u, group in enumerate(q.uses):
                            act.wait_ge(turned, q.use0 + u + 1)
                            nc.scalar.activation(qk[q.p % 2][:, group[0]:group[-1] + 1, q.t * P:(q.t + 1) * P],
                                                 psum[:, TR + (q.use0 + u) % 2, 0:len(group) * P]
                                                 .rearrange("p (s n) -> p s n", n=P), ACT.Copy).then_inc(stacks_in, 1)

                    def exps(it):
                        for s, n in enumerate(it.scores):
                            act.wait_ge(negmax, n + 1)
                            src = psum[:, SBANK + 2 * (n % 2):SBANK + 2 * (n % 2) + 2, 0:384]
                            dst = e[it.i % 2][s][:].rearrange("p (c w) -> p c w", c=2)
                            if it.keys < T:
                                src, dst = psum[:, SBANK + 2 * (n % 2), 0:it.keys], e[it.i % 2][s][:, 0:it.keys]
                            nc.scalar.activation(dst, src, ACT.Exp, bias=nmx[:, it.i % 2, s:s + 1], scale=SCALE,
                                                 accum_out=esum[:, it.i % 2, s:s + 1]).then_inc(exped, 1)

                    def keep_probs(it):
                        for u, kts in enumerate(it.ptuses):
                            act.wait_ge(turned, it.use0 + u + 1)
                            nc.scalar.activation(pth[it.i % 2][:, kts[0]:kts[-1] + 1, :],
                                                 psum[:, TR + (it.use0 + u) % 2, 0:len(kts) * P]
                                                 .rearrange("p (s n) -> p s n", n=P), ACT.Copy).then_inc(pt_hi, 1)

                    hi_of_panel(0)
                    for sl in slots:
                        for q in sl["preps"][:1]:
                            read_projection(q)
                        if sl["item"] is not None:
                            keep_probs(sl["item"])
                        for n, q in enumerate(sl["preps"]):
                            if n:
                                read_projection(q)
                            stack_his(q)
                            if sl["stack_first"]:
                                keep_stacks(q)
                        if sl["next"] is not None:
                            exps(sl["next"])
                        if not sl["stack_first"]:
                            for q in sl["preps"]:
                                keep_stacks(q)
                        for p in after_panel(sl):
                            hi_of_panel(p + 1)
                        if sl["item"] is not None and sl["item"].diff:
                            it = sl["item"]
                            act.wait_ge(o_read, it.i + 1)
                            if it.dsq:
                                act.wait_ge(o_var, it.dsq)
                            nc.scalar.activation(osq[:], osb[:, it.i % 2], ACT.Square, accum_out=oss[:]
                                                 ).then_inc(o_sq, 1)

                @block.vector
                def _(dve):
                    steps = [0]

                    def link(ins):
                        steps[0] += 1
                        ins.then_inc(dchain, 1)
                        dve.wait_ge(dchain, steps[0])

                    def lo_of_panel(p):
                        for n in panel_units(p):
                            dve.wait_ge(hi_ready, ph.base + n + 1)
                            nc.vector.tensor_tensor(wlo3[:, n % 3].rearrange("p k n -> p (k n)"), raw[ph.raws[n]][:],
                                                    whi3[:, n % 3].rearrange("p k n -> p (k n)").bitcast(F32),
                                                    ALU.subtract).then_inc(lo_ready, 1)

                    def shape_heads(q):
                        dve.wait_ge(act_read, q.g + 1)
                        if q.g:
                            dve.wait_ge(stack_hi, q.g)
                        g0, g1 = q.g0, q.g1
                        ng = g1 - g0

                        def values_lo():
                            nc.vector.tensor_tensor(vlo[q.p % 2][:, q.t, 0:q.vd], psum[:, GEMM, 3 * P - q.vd:3 * P],
                                                    vhi[q.p % 2][:, q.t, 0:q.vd].bitcast(F32), ALU.subtract
                                                    ).then_inc(dve_read, 1)

                        def rotate(x, last_read):
                            def table(tab, first, step):
                                y = tab[:, q.t - CTX_TILES, first::step].rearrange("p (o d) -> p o d", o=1)
                                return y.broadcast_to([P, ng, HD // step])

                            nc.vector.tensor_tensor(ra[:, g0:g1], x, table(cosT, 0, 1), ALU.mult)
                            nc.vector.tensor_tensor(rd[:, g0:g1, 0::2], x[:, :, 1::2], table(sinT, 0, 2), ALU.mult)
                            sw = nc.vector.tensor_tensor(rd[:, g0:g1, 1::2], x[:, :, 0::2], table(sinT, 1, 2), ALU.mult)
                            if last_read:
                                values_lo()
                                dve.wait_ge(dve_read, q.g + 1)
                            else:
                                link(sw)
                            nc.vector.tensor_tensor(rc[:, g0:g1], ra[:, g0:g1], rd[:, g0:g1], ALU.add
                                                    ).then_inc(roped, 1)

                        x = psum[:, GEMM, g0 * HD:g1 * HD].rearrange("p (g d) -> p g d", d=HD)
                        if q.diff and q.rope:
                            rotate(x, True)
                        elif q.diff:
                            nc.vector.tensor_copy(rc[:, g0:g1], x).then_inc(roped, 1)
                            values_lo()
                        else:
                            dve.wait_ge(sq_done, q.hn + 1)
                            link(nc.vector.tensor_reduce(hss[:, g0:g1], hsq[:, g0:g1], AX.X, ALU.add))
                            nc.vector.tensor_scalar(hvar[:, g0:g1], hss[:, g0:g1], 1.0 / HD, EPS, ALU.mult, ALU.add
                                                    ).then_inc(head_var, 1)
                            dve.wait_ge(head_pow, q.hn + 1)
                            r = hpow[:, g0:g1].rearrange("p (g o) -> p g o", o=1).broadcast_to([P, ng, HD])
                            nc.vector.tensor_tensor(ra[:, g0:g1], x, r, ALU.mult)
                            values_lo()
                            dve.wait_ge(dve_read, q.g + 1)
                            if q.rope:
                                link(nc.vector.tensor_tensor(rb[:, g0:g1], ra[:, g0:g1], headG[:, g0:g1], ALU.mult))
                                rotate(rb[:, g0:g1], False)
                            else:
                                nc.vector.tensor_tensor(rc[:, g0:g1], ra[:, g0:g1], headG[:, g0:g1], ALU.mult
                                                        ).then_inc(roped, 1)

                    def stack_los(q):
                        dve.wait_ge(stack_hi, q.g + 1)
                        if q.q:
                            nc.vector.tensor_tensor(st[:, 0:q.nq, HD:2 * HD], rc[:, 0:q.nq],
                                                    st[:, 0:q.nq, 0:HD].bitcast(F32), ALU.subtract)
                        ka, kb = q.nq, q.nq + q.nk
                        src = rc[:, q.nq:q.g1].rearrange("p g (o d) -> p g o d", o=1).broadcast_to([P, q.nk, 2, HD])
                        nc.vector.tensor_tensor(st[:, kb:kb + q.nk].rearrange("p s (o d) -> p s o d", o=2), src,
                                                st[:, ka:ka + q.nk].bitcast(F32)
                                                .rearrange("p s (o d) -> p s o d", o=2), ALU.subtract
                                                ).then_inc(stack_lo, 1)

                    def maxima(it):
                        for s, n in enumerate(it.scores):
                            dve.wait_ge(scores, n + 1)
                            if it.keys < T:
                                link(nc.vector.tensor_reduce(mx[:, s:s + 1], psum[:, SBANK + 2 * (n % 2), 0:it.keys],
                                                             AX.X, ALU.max))
                            else:
                                link(nc.vector.tensor_reduce(
                                    mx[:, s:s + 1], psum[:, SBANK + 2 * (n % 2):SBANK + 2 * (n % 2) + 2, 0:384],
                                    AX.XY, ALU.max))
                            nc.vector.tensor_scalar(nmx[:, it.i % 2, s:s + 1], mx[:, s:s + 1], -SCALE, None, ALU.mult
                                                    ).then_inc(negmax, 1)

                    def normalise(it):
                        b = it.i % 2
                        ns = len(it.scores)
                        dve.wait_ge(exped, it.scores[-1] + 1)
                        if not it.diff:
                            nc.vector.reciprocal(rec[:, b, 0:1], esum[:, b, 0:1]).then_inc(probs, 1)
                            return
                        link(nc.vector.reciprocal(rec[:, b, 0:ns], esum[:, b, 0:ns]))
                        link(nc.vector.tensor_scalar(rlam[:], rec[:, b, 1:2], lam[:, 0:1], None, ALU.mult))
                        link(nc.vector.tensor_scalar(e[b][1][:, 0:it.keys], e[b][1][:, 0:it.keys], rlam[:, 0:1], None,
                                                     ALU.mult))
                        nc.vector.scalar_tensor_tensor(e[b][0][:, 0:it.keys], e[b][0][:, 0:it.keys], rec[:, b, 0:1],
                                                       e[b][1][:, 0:it.keys], ALU.mult, ALU.subtract
                                                       ).then_inc(probs, 1)

                    def probs_lo(it):
                        for u, kts in enumerate(it.ptuses):
                            dve.wait_ge(pt_hi, it.pt0 + u + 1)
                            sl_ = slice(kts[0], kts[-1] + 1)
                            nc.vector.tensor_tensor(ptl[it.i % 2][:, sl_, :],
                                                    psum[:, TR + (it.use0 + u) % 2, 0:len(kts) * P]
                                                    .rearrange("p (s n) -> p s n", n=P),
                                                    pth[it.i % 2][:, sl_, :].bitcast(F32), ALU.subtract
                                                    ).then_inc(pt_lo, 1)

                    def read_output(it):
                        dve.wait_ge(pv_done, it.i + 1)
                        if it.diff:
                            nc.vector.tensor_copy(osb[:, it.i % 2], psum[:, OB, 0:P]).then_inc(o_read, 1)
                        else:
                            if it.j == 0 and it.before is not None:
                                dve.wait_ge(turned, it.before.ouse + 1)
                            nc.vector.tensor_scalar(onrm[:, it.nrm % 2, it.j * HD:(it.j + 1) * HD],
                                                    psum[:, OB, 0:HD], rec[:, it.i % 2, 0:1], None, ALU.mult
                                                    ).then_inc(o_read, 1)

                    def output_var(it):
                        dve.wait_ge(o_sq, it.dsq + 1)
                        if it.dsq:
                            dve.wait_ge(o_pow, it.dsq)
                        nc.vector.tensor_scalar(ovar[:], oss[:], 1.0 / (2 * HD), EPS, ALU.mult, ALU.add
                                                ).then_inc(o_var, 1)

                    def output_norm(it):
                        dve.wait_ge(o_pow, it.dsq + 1)
                        if it.before is not None:
                            dve.wait_ge(turned, it.before.ouse + 1)
                        nc.vector.tensor_scalar(onrm[:, it.nrm % 2, 0:P], osb[:, it.i % 2], opow[:, 0:1], None,
                                                ALU.mult).then_inc(o_norm, 1)

                    def keep_output(it):
                        dve.wait_ge(turned, it.ouse + 1)
                        b = psum[:, TR + it.ouse % 2]
                        tok = slice(it.t * P, (it.t + 1) * P)
                        if it.diff:
                            nc.vector.tensor_scalar(A[:, it.p, tok], b[:, 0:P], subg[:, 0:1], None, ALU.mult
                                                    ).then_inc(o_out, 1)
                        else:
                            f = DIFF_HEADS + 2 * (it.p - DIFF_HEADS)
                            nc.vector.tensor_copy(A[:, f:f + 2, tok], b[:, 0:2 * P].rearrange("p (s n) -> p s n", n=P)
                                                  ).then_inc(o_out, 1)

                    lo_of_panel(0)
                    for n, sl in enumerate(slots):
                        it = sl["item"]
                        if it is not None:
                            probs_lo(it)
                        for q in sl["preps"]:
                            shape_heads(q)
                            stack_los(q)
                        if sl["next"] is not None:
                            maxima(sl["next"])
                        before = slots[n - 1]["item"] if n else None
                        if before is not None and before.diff:
                            output_norm(before)
                        if it is not None:
                            read_output(it)
                        if sl["next"] is not None:
                            normalise(sl["next"])
                        for p in after_panel(sl):
                            lo_of_panel(p + 1)
                        if it is not None and it.diff:
                            output_var(it)
                        for o in sl["outs"]:
                            keep_output(o)

                @block.gpsimd
                def _(pool):
                    for n, sl in enumerate(slots):
                        for q in sl["preps"]:
                            if not q.diff:
                                pool.wait_ge(head_var, q.hn + 1)
                                if q.g:
                                    pool.wait_ge(dve_read, q.g)
                                nc.gpsimd.tensor_tensor(hpow[:, q.g0:q.g1], hvar[:, q.g0:q.g1],
                                                        mhalf[:, q.g0:q.g1], ALU.pow).then_inc(head_pow, 1)
                        it = sl["item"]
                        if it is not None and it.diff:
                            pool.wait_ge(o_var, it.dsq + 1)
                            if it.dsq:
                                pool.wait_ge(o_norm, it.dsq)
                            nc.gpsimd.tensor_tensor(opow[:], ovar[:], mhalf[:, 0:1], ALU.pow).then_inc(o_pow, 1)

        def wide(layer):
            if layer < DEPTH - 1:
                return [(0, 0, 384), (1, 384, 384)], 0
            return [(0, CTX, SEQ)], CTX

        def grid(ap, layer):
            chunks, t0 = wide(layer)
            return ap[:, t0:T].rearrange("p (c w) -> p c w", c=len(chunks))

        def pair(u, layer):
            chunks, _ = wide(layer)
            return psum[:, 2 * (u % 4):2 * (u % 4) + len(chunks), 0:chunks[0][2]]

        po_step, po_hi, po_lo, po_mm, po_out, po_table, o_hi, o_lo = (
            sem(n) for n in ("po_step", "po_hi", "po_lo", "po_mm", "po_out", "po_table", "o_hi", "o_lo"))
        gate_done, z_done, sig_done, z_read, mix_step, me_hi, me_lo, y_kept = (
            sem(n) for n in ("gate_done", "z_done", "sig_done", "z_read", "mix_step", "me_hi", "me_lo", "y_kept"))
        relu_done, hid_hi, hid_sq, hid_lo, y_done, y_added = (
            sem(n) for n in ("relu_done", "hid_hi", "hid_sq", "hid_lo", "y_done", "y_added"))

        def pooling(layer, Ohi, Olo):
            chunks, t0 = wide(layer)
            w_in = a["w_in"][layer].rearrange("(k p) n -> p k n", p=P)
            grp = a["w_pool_grp"][layer].rearrange("g c d -> c g d")
            G, W2 = len(POOL_WINDOWS), T + 4 * ZPAD
            parts = [(o, q, n) for o, q, n in ((ZPAD, 0, CTX), (CTX + 3 * ZPAD, CTX, SEQ)) if q + n > t0]
            per_layer = 1 + sum(g + 4 for g in range(G))

            def step(g):
                return layer * per_layer + 1 + sum(q + 4 for q in range(g))

            ph = units.phase([0, 1, 2, 0, 1], [2, 3, 0, 1, 2])
            with ExitStack() as z:
                zp = sb(f"zp{layer}", [P, W2], F32, z)
                sums = [sb(f"sum{b}_{layer}", [P, W2], F32, z) for b in range(2)]
                inv = sb(f"inv{layer}", [P, T], F32, z)
                block = z.enter_context(nc.Block())

                @block.sync
                def _(sp):
                    for j in range(G):
                        sp.dma_start(slot_view(ph.raws[j]), w_in[:, :, j * P:(j + 1) * P]).then_inc(landed[ph.raws[j]], 16)
                    sp.wait_ge(lo_ready, ph.base + 1)
                    sp.dma_start(slot_view(ph.raws[G])[:, 0:G], grp).then_inc(landed[ph.raws[G]], 16)
                    for g in range(G):
                        if g:
                            sp.wait_ge(po_step, step(g) - 1)
                        sp.dma_start(inv[:], a["inv_count"][g:g + 1, :].broadcast_to([P, T])).then_inc(po_table, 16)

                @block.scalar
                def _(act):
                    for j in range(G + 1):
                        act.wait_ge(landed[ph.raws[j]], ph.landed(j, 0))
                        if j >= 3:
                            act.wait_ge(unit_used, ph.used0 + j - 2)
                        n = UNIT if j < G else G * P
                        dst = whi(ph.slots[j]).rearrange("p k n -> p (k n)")
                        nc.scalar.activation(dst[:, 0:n], raw[ph.raws[j]][:, 0:n], ACT.Copy).then_inc(hi_ready, 1)
                        for k in ((), (0, 1), (2, 3), (4, 5), (6, 7))[j]:
                            nc.scalar.activation(Ohi[:, 4 + k, t0:T], A[:, k, t0:T], ACT.Copy).then_inc(o_hi, 1)
                    for g in range(G):
                        act.wait_ge(po_step, step(g + 1))
                        nc.scalar.activation(Ohi[:, g, t0:T], A[:, 4 + g, t0:T], ACT.Copy).then_inc(po_hi, 1)
                    for g in range(G):
                        act.wait_ge(*((po_mm, layer * (G - 1) + g + 1) if g < G - 1 else (unit_used, ph.used0 + G + 1)))
                        nc.scalar.activation(grid(A[:, g], layer), pair(g, layer), ACT.Identity,
                                             scale=vec[:, R_PSC + g:R_PSC + g + 1]).then_inc(po_out, 1)
                        act.wait_ge(po_out, layer * G + g + 1)
                        nc.scalar.activation(Ohi[:, g, t0:T], A[:, g, t0:T], ACT.Copy).then_inc(po_hi, 1)

                @block.tensor
                def _(pe):
                    for g in range(G):
                        pe.wait_ge(lo_ready, ph.base + g + 1)
                        s = ph.slots[g]
                        for k in range(KT):
                            mm = three_terms(pair(g, layer), whi(s)[:, k], wlo(s)[:, k], Hhi[:, k], Hlo[:, k],
                                             chunks, k == 0, k == KT - 1)
                        mm.then_inc(unit_used, 1)
                    pe.wait_ge(lo_ready, ph.base + G + 1)
                    s = ph.slots[G]
                    for g in range(G):
                        pe.wait_ge(po_lo, layer * 2 * G + g + 1)
                        mm = three_terms(pair(g, layer), whi(s)[:, g], wlo(s)[:, g], Ohi[:, g], Olo[:, g],
                                         chunks, True, True)
                        mm.then_inc(po_mm if g < G - 1 else unit_used, 1)

                @block.vector
                def _(dve):
                    nc.vector.memset(zp[:], 0.0).then_inc(po_step, 1)
                    for j in range(G + 1):
                        dve.wait_ge(hi_ready, ph.index(j, 0) + 1)
                        n = UNIT if j < G else G * P
                        dst = wlo(ph.slots[j]).rearrange("p k n -> p (k n)")
                        hi = whi(ph.slots[j]).rearrange("p k n -> p (k n)").bitcast(F32)
                        nc.vector.tensor_tensor(dst[:, 0:n], raw[ph.raws[j]][:, 0:n], hi[:, 0:n], ALU.subtract
                                                ).then_inc(lo_ready, 1)
                        for k in ((), (0, 1), (2, 3), (4, 5), (6, 7))[j]:
                            dve.wait_ge(o_hi, 8 * layer + k + 1)
                            nc.vector.tensor_tensor(Olo[:, 4 + k, t0:T], A[:, k, t0:T],
                                                    Ohi[:, 4 + k, t0:T].bitcast(F32), ALU.subtract).then_inc(o_lo, 1)
                    for g in range(G):
                        n = step(g)
                        dve.wait_ge(po_step, n)
                        dve.wait_ge(unit_used, ph.used0 + g + 1)
                        for o, q, ln in parts:
                            for bank, c0, cn in chunks:
                                u, v = max(q, c0), min(q + ln, c0 + cn)
                                if u < v:
                                    ins = nc.vector.tensor_copy(zp[:, o + u - q:o + v - q],
                                                                pair(g, layer)[:, bank, u - c0:v - c0])
                        ins.then_inc(po_step, 1)
                        dve.wait_ge(po_step, n + 1)
                        src, left, right = zp, 0, 0
                        for m in range(g + 1):
                            back, ahead = (1, 0) if m == 0 else (2 ** (m - 1), 2 ** (m - 1))
                            left, right = left + back, right + ahead
                            nc.vector.tensor_tensor(sums[m % 2][:, left:W2 - right],
                                                    src[:, left - back:W2 - right - back],
                                                    src[:, left + ahead:W2 - right + ahead], ALU.add
                                                    ).then_inc(po_step, 1)
                            dve.wait_ge(po_step, n + 2 + m)
                            src = sums[m % 2]
                        mean = sums[(g + 1) % 2]
                        dve.wait_ge(po_table, 16 * (layer * G + g + 1))
                        for o, q, ln in parts:
                            ins = nc.vector.tensor_tensor(mean[:, o:o + ln], src[:, o:o + ln], inv[:, q:q + ln], ALU.mult)
                        ins.then_inc(po_step, 1)
                        dve.wait_ge(po_step, n + 3 + g)
                        dve.wait_ge(o_lo, 8 * layer + 8)
                        for o, q, ln in parts:
                            ins = nc.vector.tensor_tensor(A[:, 4 + g, q:q + ln], mean[:, o:o + ln], zp[:, o:o + ln],
                                                          ALU.subtract)
                        ins.then_inc(po_step, 1)
                        dve.wait_ge(po_hi, layer * 2 * G + g + 1)
                        nc.vector.tensor_tensor(Olo[:, g, t0:T], A[:, 4 + g, t0:T], Ohi[:, g, t0:T].bitcast(F32),
                                                ALU.subtract).then_inc(po_lo, 1)
                    for g in range(G):
                        dve.wait_ge(po_hi, layer * 2 * G + G + g + 1)
                        nc.vector.tensor_tensor(Olo[:, g, t0:T], A[:, g, t0:T], Ohi[:, g, t0:T].bitcast(F32),
                                                ALU.subtract).then_inc(po_lo, 1)

        def merge(layer, Ohi, Olo):
            chunks, t0 = wide(layer)
            w_in = a["w_in"][layer].rearrange("(k p) n -> p k n", p=P)
            w_out = [a[n][layer].rearrange("(k p) n -> p k n", p=P) for n in ("w_pool_out", "w_diff_out", "w_gqa_out")]
            w_o = a["w_o"][layer].rearrange("(k p) n -> p k n", p=P)
            HK = KT // 2
            pg = units.phase([0, 1, 2, 3, 0, 1, 2, 3, 0, 1], [3, 0, 1, 2, 3, 0, 1, 2, 3, 0], KT // 2,
                             [1, 1, 1, 2, 1] * 2)
            po = units.phase([0, 1, 2, 3] * 2, [3, 0, 1, 2] * 2)
            m0 = KT * layer

            with ExitStack() as z:
                fourth_slot(z, f"mix{layer}")
                sig = [sb(f"sig{b}_{layer}", [P, T], F32, z) for b in range(3)]
                block = z.enter_context(nc.Block())

                def pg_used(j, i):
                    return i * pg.B + (pg.used0 + j + 1)

                def A_tile(i, mm):
                    flat = A[:].rearrange("p k t -> p (k t)")
                    n = T - t0
                    ap = flat[:, bass.ds(i * (2 * T) + (mm * T + t0), n)]
                    return ap.rearrange("p (c w) -> p c w", c=len(chunks))

                @block.sync
                def _(sp):
                    with sp.Fori(0, KT // 2) as i:
                        for j in range(pg.B):
                            mm, u = j // 5, j % 5
                            v = slot_view(pg.raws[j])
                            if u < 3:
                                src = [(v, w_in, GATE_OFF + u * D + mm * P)]
                            elif u == 3:
                                src = [(v[:, 0:HK], w_out[0], mm * P), (v[:, HK:KT], w_out[1], mm * P)]
                            else:
                                src = [(v[:, 0:HK], w_out[2], mm * P)]
                            sp.wait_ge(lo_ready, pg.raw_free(j, i))
                            for dst, w, c in src:
                                off = (i * 2 + mm) * P + (c - mm * P) if u < 3 else (i * P + mm * (P // 2)) * 2
                                sp.dma_start(dst, w[:, :, bass.ds(off, P)]).then_inc(landed[pg.raws[j]], 16)
                    for j in range(KT):
                        sp.wait_ge(lo_ready, po.raw_free(j, 0))
                        sp.dma_start(slot_view(po.raws[j]), w_o[:, :, j * P:(j + 1) * P]).then_inc(landed[po.raws[j]], 16)

                @block.tensor
                def _(pe):
                    def branch(b, slot, half, u):
                        for k in range(HK):
                            mm_ = three_terms(pair(u, layer), whi(slot)[:, half * HK + k], wlo(slot)[:, half * HK + k],
                                              Ohi[:, 4 * b + k], Olo[:, 4 * b + k], chunks, k == 0, k == HK - 1)
                        return mm_

                    with pe.Fori(0, KT // 2) as i:
                        for j in range(pg.B):
                            mm, u = j // 5, j % 5
                            s = pg.slots[j]
                            pe.wait_ge(lo_ready, pg.index(j, i) + 1)
                            if u == 0:
                                pe.wait_ge(sig_done, i * 6 + (3 * m0 + 3 * mm))
                            elif u == 1:
                                pe.wait_ge(z_read, i * 6 + (3 * m0 + 3 * mm))
                            elif u == 3:
                                pe.wait_ge(sig_done, i * 6 + (3 * m0 + 3 * mm + 2))
                            if u < 3:
                                for k in range(KT):
                                    last = three_terms(pair(mm * 6 + u, layer), whi(s)[:, k], wlo(s)[:, k], Hhi[:, k],
                                                       Hlo[:, k], chunks, k == 0, k == KT - 1)
                                last.then_inc(unit_used, 1)
                            elif u == 3:
                                branch(0, s, 0, mm * 6 + 3).then_inc(z_done, 1)
                                branch(1, s, 1, mm * 6 + 4).then_inc(unit_used, 1)
                            else:
                                branch(2, s, 0, mm * 6 + 5).then_inc(unit_used, 1)
                    pe.wait_ge(z_read, 3 * (m0 + KT))
                    for j in range(KT):
                        s = po.slots[j]
                        pe.wait_ge(lo_ready, po.base + j + 1)
                        if j >= 4:
                            pe.wait_ge(y_kept, m0 + j - 3)
                        for k in range(KT):
                            if j == 0:
                                pe.wait_ge(me_lo, m0 + k + 1)
                            mm_ = three_terms(pair(j, layer), whi(s)[:, k], wlo(s)[:, k], Hhi[:, k], Hlo[:, k],
                                              chunks, k == 0, k == KT - 1)
                        mm_.then_inc(unit_used, 1)

                @block.scalar
                def _(act):
                    split_hi(act, pg, 0, 0, wait_slot=False)
                    with act.Fori(0, KT // 2) as i:
                        for j in range(pg.B):
                            mm, u = j // 5, j % 5
                            split_hi(act, pg, (j + 1) % pg.B, i + (j + 1) // pg.B if j + 1 == pg.B else i)
                            if u < 3:
                                act.wait_ge(unit_used, pg_used(j, i))
                                act.wait_ge(z_read, i * 6 + (3 * m0 + 3 * mm))
                                act.wait_ge(mix_step, i * 4 + (2 * m0 + 2 * mm))
                                nc.scalar.activation(grid(sig[u], layer), pair(mm * 6 + u, layer), ACT.Sigmoid
                                                     ).then_inc(sig_done, 1)
                    act.wait_ge(unit_used, po.used0)
                    for k in range(KT):
                        act.wait_ge(mix_step, 2 * (m0 + k + 1))
                        nc.scalar.activation(Hhi[:, k, t0:T], A[:, k, t0:T], ACT.Copy).then_inc(me_hi, 1)
                    for j in range(KT):
                        if j + 1 < KT:
                            split_hi(act, po, j + 1, 0)
                        act.wait_ge(unit_used, po.used0 + j + 1)
                        if j == 0:
                            act.wait_ge(me_lo, m0 + KT)
                        nc.scalar.activation(grid(A[:, j], layer), pair(j, layer), ACT.Copy).then_inc(y_kept, 1)

                @block.vector
                def _(dve):
                    split_lo(dve, pg, 0, 0)
                    with dve.Fori(0, KT // 2) as i:
                        for j in range(pg.B):
                            mm, u = j // 5, j % 5
                            split_lo(dve, pg, (j + 1) % pg.B, i + (j + 1) // pg.B if j + 1 == pg.B else i)
                            if u < 3:
                                continue
                            n3, n2 = i * 6 + (3 * m0 + 3 * mm), i * 4 + (2 * m0 + 2 * mm)
                            dst = A_tile(i, mm)
                            for b in ((0, 1) if u == 3 else (2,)):
                                src = pair(mm * 6 + 3 + b, layer)
                                if b == 0:
                                    dve.wait_ge(z_done, i * 2 + (m0 + mm + 1))
                                else:
                                    dve.wait_ge(unit_used, pg_used(j, i))
                                dve.wait_ge(sig_done, n3 + (b + 1))
                                g = grid(sig[b], layer)
                                nc.vector.tensor_tensor(dst if b == 0 else g, src, g, ALU.mult).then_inc(z_read, 1)
                                if b:
                                    dve.wait_ge(z_read, n3 + (b + 1))
                                    if b == 2:
                                        dve.wait_ge(mix_step, n2 + 1)
                                    nc.vector.tensor_tensor(dst, dst, g, ALU.add).then_inc(mix_step, 1)
                    for k in range(KT):
                        dve.wait_ge(me_hi, m0 + k + 1)
                        nc.vector.tensor_tensor(Hlo[:, k, t0:T], A[:, k, t0:T], Hhi[:, k, t0:T].bitcast(F32),
                                                ALU.subtract).then_inc(me_lo, 1)
                    for j in range(KT - 1):
                        split_lo(dve, po, j + 1, 0)

        def mlp(layer):
            chunks, t0 = wide(layer)
            w1 = a["w_ff1"][layer].rearrange("(k p) n -> p k n", p=P)
            w2 = a["w_ff2"][layer].rearrange("(r p) n -> p r n", p=P)
            MB = FB // P
            HK = MB
            ring = [0, 1, 2, 3]
            rr = [3, 0, 1, 2]
            pa = units.phase(ring, rr)
            pb = units.phase(ring * 4, rr * 4, NB // 2 - 1)
            pc = units.phase(ring * 3, rr * 3)
            h0, y0 = NB * MB * layer, (NB + 1) * KT * layer

            with ExitStack() as z:
                fourth_slot(z, f"mlp{layer}")
                hhi = [sb(f"hhi{b}_{layer}", [P, MB, T], F32R, z) for b in range(2)]
                hlo = [sb(f"hlo{b}_{layer}", [P, MB, T], F32R, z) for b in range(2)]
                rt = [sb(f"rt{b}_{layer}", [P, T], F32, z) for b in range(2)]
                h2 = sb(f"h2_{layer}", [P, T], F32, z)
                block = z.enter_context(nc.Block())

                def up(ph, j0, blk):
                    return [(ph, j0 + m, "up", blk, m) for m in range(MB)]

                def down(ph, j0, blk):
                    return [(ph, j0 + m, "down", blk, m) for m in range(KT // 2)]

                plan_a = up(pa, 0, (0, 0))
                plan_b = up(pb, 0, (2, 1)) + down(pb, 4, (2, 0)) + up(pb, 8, (2, 2)) + down(pb, 12, (2, 1))
                plan_c = up(pc, 0, (0, NB - 1)) + down(pc, 4, (0, NB - 2)) + down(pc, 8, (0, NB - 1))

                def run(eng, body):
                    body(0, plan_a, (pb, 0, 0))
                    with eng.Fori(0, NB // 2 - 1) as i:
                        body(i, plan_b, (pb, 0, 1))
                    body(0, plan_c, None)

                def at(i, lin):
                    return i * lin[0] + lin[1] if lin[0] else lin[1]

                def parity(blk):
                    return blk[1] % 2

                def pair_uses(plan):
                    n, got = 0, []
                    for _, _, kind, _, _ in plan:
                        got.append(n)
                        n += 1 if kind == "up" else 2
                    return got

                @block.sync
                def _(sp):
                    def body(i, plan, _):
                        for ph, j, kind, blk, m in plan:
                            s = ph.raws[j]
                            if kind == "up":
                                off, dst, src, n = at(i, (blk[0] * FB, blk[1] * FB + m * P)), slot_view(s), w1, P
                            else:
                                off, dst, src, n = at(i, (blk[0] * HK, blk[1] * HK)), slot_view(s, HK), w2, HK
                            sp.wait_ge(lo_ready, ph.raw_free(j, i))
                            src = src[:, :, bass.ds(off, P)] if kind == "up" else \
                                src[:, bass.ds(off, HK), m * 2 * P:(m + 1) * 2 * P]
                            sp.dma_start(dst, src).then_inc(landed[s], 16)
                    run(sp, body)

                @block.tensor
                def _(pe):
                    def body(i, plan, _):
                        for (ph, j, kind, blk, m), u in zip(plan, pair_uses(plan)):
                            s = ph.slots[j]
                            pe.wait_ge(lo_ready, ph.index(j, i) + 1)
                            if kind == "up":
                                if blk != (0, 0):
                                    pe.wait_ge(relu_done, at(i, (blk[0] * MB, h0 + (blk[1] - 1) * MB + m + 1)))
                                    pe.wait_ge(y_added, at(i, (blk[0] * KT, y0 + (blk[1] - 1) * KT + KT // 2 + m + 1)))
                                for k in range(KT):
                                    mm = three_terms(pair(u, layer), whi(s)[:, k], wlo(s)[:, k], Hhi[:, k], Hlo[:, k],
                                                     chunks, k == 0, k == KT - 1)
                                mm.then_inc(unit_used, 1)
                                continue
                            hh, hl = hhi[parity(blk)], hlo[parity(blk)]
                            if m == 0:
                                pe.wait_ge(hid_lo, at(i, (blk[0] * MB, h0 + (blk[1] + 1) * MB)))
                            w_h = whi(s).rearrange("p k n -> p (k n)").rearrange("p (k n) -> p k n", k=HK)
                            w_l = wlo(s).rearrange("p k n -> p (k n)").rearrange("p (k n) -> p k n", k=HK)
                            for q in range(2):
                                n = 2 * m + q
                                if m < 2 and blk != (0, NB - 1):
                                    pe.wait_ge(relu_done, at(i, (blk[0] * MB, h0 + (blk[1] + 1) * MB + n + 1)))
                                else:
                                    pe.wait_ge(y_added, at(i, (blk[0] * KT, y0 + (blk[1] + 1) * KT + n - 3)))
                                for k in range(HK):
                                    mm = three_terms(pair(u + q, layer), w_h[:, k, q * P:(q + 1) * P],
                                                     w_l[:, k, q * P:(q + 1) * P], hh[:, k], hl[:, k], chunks,
                                                     k == 0, k == HK - 1)
                                mm.then_inc(y_done if q == 0 else unit_used, 1)
                    run(pe, body)

                def prefetch(i, plan, n, follow):
                    if n + 1 < len(plan):
                        return plan[n + 1][0], plan[n + 1][1], i
                    if follow is None:
                        return None
                    ph, j, ahead = follow
                    return ph, j, i + 1 if ahead else 0

                @block.scalar
                def _(act):
                    def body(i, plan, follow):
                        for n, ((ph, j, kind, blk, m), u) in enumerate(zip(plan, pair_uses(plan))):
                            nxt = prefetch(i, plan, n, follow)
                            if nxt is not None:
                                split_hi(act, *nxt)
                            if kind == "down":
                                continue
                            h = at(i, (blk[0] * MB, h0 + blk[1] * MB + m))
                            r = rt[m % 2]
                            act.wait_ge(unit_used, i * ph.B + (ph.used0 + j + 1))
                            if m >= 2 or blk != (0, 0):
                                act.wait_ge(hid_sq, at(i, (blk[0] * MB, h0 + blk[1] * MB + m - 1)))
                            nc.scalar.activation(grid(r, layer), pair(u, layer), ACT.Relu).then_inc(relu_done, 1)
                            act.wait_ge(relu_done, h + 1)
                            nc.scalar.activation(hhi[parity(blk)][:, m, t0:T], r[:, t0:T], ACT.Square
                                                 ).then_inc(hid_hi, 1)
                    split_hi(act, pa, 0, 0)
                    run(act, body)

                @block.vector
                def _(dve):
                    def body(i, plan, follow):
                        for n, ((ph, j, kind, blk, m), u) in enumerate(zip(plan, pair_uses(plan))):
                            nxt = prefetch(i, plan, n, follow)
                            if nxt is not None:
                                split_lo(dve, *nxt)
                            if kind == "up":
                                r = rt[m % 2]
                                h = at(i, (blk[0] * MB, h0 + blk[1] * MB + m))
                                dve.wait_ge(relu_done, h + 1)
                                if m or blk != (0, 0):
                                    dve.wait_ge(hid_lo, h)
                                nc.vector.tensor_tensor(h2[:, t0:T], r[:, t0:T], r[:, t0:T], ALU.mult
                                                        ).then_inc(hid_sq, 1)
                                dve.wait_ge(hid_sq, h + 1)
                                dve.wait_ge(hid_hi, h + 1)
                                nc.vector.tensor_tensor(hlo[parity(blk)][:, m, t0:T], h2[:, t0:T],
                                                        hhi[parity(blk)][:, m, t0:T].bitcast(F32), ALU.subtract
                                                        ).then_inc(hid_lo, 1)
                                continue
                            for q in range(2):
                                k = 2 * m + q
                                if q == 0:
                                    dve.wait_ge(y_done, at(i, (blk[0] * KT // 2, y_done0 + blk[1] * (KT // 2) + m + 1)))
                                else:
                                    dve.wait_ge(unit_used, i * ph.B + (ph.used0 + j + 1))
                                dve.wait_ge(y_added, at(i, (blk[0] * KT, y0 + blk[1] * KT + k + 1)))
                                dst = grid(A[:, k], layer)
                                nc.vector.tensor_tensor(dst, pair(u + q, layer), dst, ALU.add).then_inc(y_added, 1)
                    y_done0 = NB * (KT // 2) * layer
                    split_lo(dve, pa, 0, 0)
                    for k in range(KT):
                        nc.vector.memset(A[:, k, t0:T], 0.0).then_inc(y_added, 1)
                    run(dve, body)

        for layer in range(DEPTH):
            tiles = range(NCH) if layer < DEPTH - 1 else range(CTX // CH, NCH)
            modulation(layer)
            norms(f"pre{layer}", range(NCH), A, preA, 0, spill=True)
            attention(layer)
            with ExitStack() as outs:
                Ohi = sb(f"Ohi{layer}", [P, 12, T], F32R, outs)
                Olo = sb(f"Olo{layer}", [P, 12, T], F32R, outs)
                pooling(layer, Ohi, Olo)
                merge(layer, Ohi, Olo)
            with ExitStack() as xs:
                B = sb(f"B{layer}", [P, KT, T], F32, xs)
                norms(f"mid{layer}", tiles, B, preF, 3 * KT, Y=A, post=postA, reload=True)
                mlp(layer)
                norms(f"end{layer}", tiles, B, Y=A, post=postF, X_out=A)

        with ExitStack() as z:
            rows = sb("out_rows", [P, SEQ // P, D], F32, z)
            out_turned, out_kept, out_left = sem("out_turned"), sem("out_kept"), sem("out_left")
            block = z.enter_context(nc.Block())

            @block.tensor
            def _(pe):
                for t in range(SEQ // P):
                    for h in range(2):
                        g = 2 * t + h
                        for k in range(4):
                            f = 4 * h + k
                            mm = nc.tensor.transpose(psum[:, g, k * P:(k + 1) * P],
                                                     A[:, f, CTX + t * P:CTX + (t + 1) * P], ident[:])
                        mm.then_inc(out_turned, 1)

            @block.vector
            def _(dve):
                for g in range(2 * SEQ // P):
                    dve.wait_ge(out_turned, g + 1)
                    nc.vector.tensor_copy(rows[:, g // 2, (g % 2) * 512:(g % 2 + 1) * 512], psum[:, g]
                                          ).then_inc(out_kept, 1)

            @block.sync
            def _(sp):
                dst = out.rearrange("b (t p) d -> p (b t) d", p=P)
                for t in range(SEQ // P):
                    sp.wait_ge(out_kept, 2 * t + 2)
                    sp.dma_start(dst[:, t], rows[:, t]).then_inc(out_left, 16)
                sp.wait_ge(out_left, 16 * (SEQ // P))


_INS = ["x", "c", "ctx", "c_ctx", "w_mod", "b_mod", "g_pre_mix", "g_post_mix", "g_pre_ffn", "g_post_ffn", "w_in",
        "w_pool_grp", "pool_scale", "lambda_q1", "lambda_k1", "lambda_q2", "lambda_k2", "diff_subln", "gqa_q_norm",
        "gqa_k_norm", "w_pool_out", "w_diff_out", "w_gqa_out", "w_o", "w_ff1", "w_ff2"]


def _constants():
    import numpy as np
    grid_w, pairs = 64, HD // 4
    row = np.repeat(np.arange(SEQ // grid_w), grid_w).astype(np.float32)
    col = np.tile(np.arange(grid_w), SEQ // grid_w).astype(np.float32)
    inv = (1.0 / (np.float32(10000.0) ** (np.arange(pairs, dtype=np.float32) * np.float32(2.0) / np.float32(HD // 2)))
           ).astype(np.float32)
    ang = np.concatenate([row[:, None] * inv, col[:, None] * inv], axis=-1).astype(np.float32)
    cos, sin = np.cos(ang), np.sin(ang)
    inv_count = np.zeros((len(POOL_WINDOWS), T), np.float32)
    for g, w in enumerate(POOL_WINDOWS):
        at = 0
        for n in (CTX, SEQ):
            t = np.arange(n)
            count = np.clip(t + w // 2, 0, n) - np.clip(t - w // 2, 0, n)
            inv_count[g, at:at + n] = 1.0 / count
            at += n
    return {"cos": np.repeat(cos, 2, axis=1).astype(np.float32),
            "sin": np.stack([-sin, sin], axis=-1).reshape(SEQ, HD).astype(np.float32),
            "inv_count": inv_count, "identity": np.eye(P, dtype=np.float32)}


def kernel(**inputs):
    import numpy as _np
    import concourse.bacc as _bacc
    from concourse import mybir as _mybir
    from concourse.bass_utils import run_bass_kernel_spmd as _run

    nc = _bacc.Bacc("TRN2", target_bir_lowering=False, num_devices=1)
    arrays, args = {}, {}
    data = {name: inputs[name] for name in _INS}
    data.update(_constants())
    for name, value in data.items():
        v = _np.ascontiguousarray(value)
        arrays[f"in_{name}"] = v
        args[name] = nc.dram_tensor(f"in_{name}", v.shape, _mybir.dt.from_np(v.dtype), kind="ExternalInput").ap()
    out = nc.dram_tensor("out_0", (1, SEQ, D), _mybir.dt.float32, kind="ExternalOutput").ap()
    build(nc, args, out)
    r = _run(nc, [arrays], core_ids=[0])
    return r.results[0]["out_0"]
```

```python
import math
from contextlib import ExitStack

import concourse.bass as bass
from concourse import mybir

F32 = mybir.dt.float32
F32R = mybir.dt.float32r
ALU = mybir.AluOpType
ACT = mybir.ActivationFunctionType
AX = mybir.AxisListType

P = 128
D = 1024
KT = D // P
SEQ, CTX = 512, 256
T = SEQ + CTX
TT = T // P
CTX_TILES = CTX // P
DEPTH = 2
HD = 64
SCALE = HD ** -0.5
EPS = 1e-6
POOL_WINDOWS = (2, 4, 8, 16)
POOL_W = DIFF_W = GQA_W = 512
DIFF_HEADS, GQA_HEADS, KV_HEADS = 4, 8, 2
GROUP = GQA_HEADS // KV_HEADS
GATE_OFF = POOL_W + DIFF_W + GQA_W
KV_OFF = GATE_OFF + 3 * D
DK_OFF, DV_OFF = KV_OFF, KV_OFF + DIFF_W
GK_OFF = KV_OFF + 2 * DIFF_W
GV_OFF = GK_OFF + KV_HEADS * HD
D_FF = 4 * D
FB = 512
NB = D_FF // FB
NPANEL = DIFF_HEADS + KV_HEADS
RING, RAW = 4, 4
UNIT = KT * P
CH = 256
NCH = T // CH
ZPAD = 8
R_C, R_CC, R_GPM, R_GQM, R_GPF, R_GQF = range(0, 48, 8)
R_BMOD, R_PSC, R_SUB, ROWS = 48, 96, 100, 101


def lambda_init(layer):
    return 0.8 - 0.6 * math.exp(-0.3 * layer)


class Units:

    def __init__(self):
        self.n = 0
        self.used = 0
        self.landed = [0] * RAW
        self.in_slot, self.in_raw = {}, {}

    def phase(self, slots, raws, iters=1, dmas=None):
        return Phase(self, slots, raws, iters, dmas or [1] * len(slots))


class Phase:

    def __init__(self, units, slots, raws, iters, dmas):
        self.slots, self.raws, self.B = slots, raws, len(slots)
        self.base, self.used0 = units.n, units.used
        self.land0 = list(units.landed)
        self.per = [sum(16 * d for r, d in zip(raws, dmas) if r == q) for q in range(RAW)]
        seen = [0] * RAW
        self.rank = []
        for r, d in zip(raws, dmas):
            seen[r] += 16 * d
            self.rank.append(seen[r])
        self.first_slot, self.first_raw = dict(units.in_slot), dict(units.in_raw)
        for j in range(self.B):
            units.in_slot[slots[j]] = units.used + self.B * (iters - 1) + j + 1
            units.in_raw[raws[j]] = units.n + self.B * (iters - 1) + j + 1
        self.iters = iters
        units.n += self.B * iters
        units.used += self.B * iters
        for q in range(RAW):
            units.landed[q] += self.per[q] * iters

    def landed(self, j, i):
        r = self.raws[j]
        return i * self.per[r] + (self.land0[r] + self.rank[j])

    def index(self, j, i):
        return i * self.B + (self.base + j)

    def _free(self, slots, first, base, j, i):
        earlier = [q for q in range(j) if slots[q] == slots[j]]
        if earlier:
            return i * self.B + (base + earlier[-1] + 1)
        if self.iters == 1:
            return first[slots[j]]
        return i * self.B + (base + 1 - self.B + max(q for q in range(self.B) if slots[q] == slots[j]))

    def raw_free(self, j, i):
        return self._free(self.raws, self.first_raw, self.base, j, i)

    def slot_free(self, j, i):
        return self._free(self.slots, self.first_slot, self.used0, j, i)


def build(nc, a, out):
    top = ExitStack()
    with top:
        def sb(name, shape, dt=F32, ctx=top):
            return ctx.enter_context(nc.sbuf_tensor(name, shape, dt))

        def sem(name):
            return top.enter_context(nc.semaphore(name))

        raw = [sb(f"raw{s}", [P, UNIT]) for s in range(RAW)]
        whi3 = sb("whi3", [P, 3, KT, P], F32R)
        wlo3 = sb("wlo3", [P, 3, KT, P], F32R)
        Hhi = sb("Hhi", [P, KT, T], F32R)
        Hlo = sb("Hlo", [P, KT, T], F32R)
        A = sb("A", [P, KT, T])
        ident = sb("ident", [P, P])
        ones = sb("ones", [P, P])
        cosT = sb("cosT", [P, SEQ // P, HD])
        sinT = sb("sinT", [P, SEQ // P, HD])
        vec = sb("vec", [P, ROWS])
        mod = sb("mod", [P, 6 * KT, 2])
        csil = sb("csil", [P, KT, 2])
        preA = sb("preA", [P, KT, 2])
        postA = sb("postA", [P, KT, 2])
        preF = sb("preF", [P, KT, 2])
        postF = sb("postF", [P, KT, 2])
        headG = sb("headG", [P, GROUP + 1, HD])
        subg = sb("subg", [P, 1])
        lams = sb("lams", [P, 2])
        lame = sb("lame", [P, 2])
        lam = sb("lam", [P, 1])
        mhalf = sb("mhalf", [P, 8])
        xdram = nc.dram_tensor("x_spill", [P, KT * T], F32, kind="Internal").ap()

        psum = top.enter_context(nc.psum_tensor("psum", [P, 8, 512], F32))

        landed = [sem(f"landed{s}") for s in range(RAW)]
        hi_ready, lo_ready, unit_used = sem("hi_ready"), sem("lo_ready"), sem("unit_used")
        setup_in, setup_step, setup_pool = sem("setup_in"), sem("setup_step"), sem("setup_pool")
        units = Units()

        def whi(j):
            return whi3[:, j] if j < 3 else whi_x[0][:]

        def wlo(j):
            return wlo3[:, j] if j < 3 else wlo_x[0][:]

        whi_x, wlo_x = [None], [None]

        def fourth_slot(ctx, tag):
            whi_x[0] = sb(f"whi_{tag}", [P, KT, P], F32R, ctx)
            wlo_x[0] = sb(f"wlo_{tag}", [P, KT, P], F32R, ctx)

        def split_hi(act, ph, j, i, wait_slot=True):
            act.wait_ge(landed[ph.raws[j]], ph.landed(j, i))
            if wait_slot:
                act.wait_ge(unit_used, ph.slot_free(j, i))
            dst = whi(ph.slots[j]).rearrange("p k n -> p (k n)")
            nc.scalar.activation(dst, raw[ph.raws[j]][:], ACT.Copy).then_inc(hi_ready, 1)

        def split_lo(dve, ph, j, i):
            dve.wait_ge(hi_ready, ph.index(j, i) + 1)
            dst = wlo(ph.slots[j]).rearrange("p k n -> p (k n)")
            hi = whi(ph.slots[j]).rearrange("p k n -> p (k n)").bitcast(F32)
            nc.vector.tensor_tensor(dst, raw[ph.raws[j]][:], hi, ALU.subtract).then_inc(lo_ready, 1)

        def load_unit(sp, ph, j, i, pieces):
            sp.wait_ge(lo_ready, ph.raw_free(j, i))
            for dst, src in pieces:
                sp.dma_start(dst, src).then_inc(landed[ph.raws[j]], 16)

        def slot_view(s, k=KT):
            return raw[s][:].rearrange("p (k n) -> p k n", k=k)

        def three_terms(out_ap, w_h, w_l, x_h, x_l, chunks, first, last):
            mm = None
            for n, (w, x) in enumerate(((w_h, x_h), (w_h, x_l), (w_l, x_h))):
                for bank, c0, cn in chunks:
                    mm = nc.tensor.matmul(out_ap[:, bank, 0:cn], w, x[:, c0:c0 + cn],
                                          start=first and n == 0, stop=last and n == 2)
            return mm

        with ExitStack() as z:
            xt = sb("x_rows", [P, TT, D], F32, z)
            x_in, x_turned, x_kept = sem("x_in"), sem("x_turned"), sem("x_kept")
            block = z.enter_context(nc.Block())

            @block.sync
            def _(sp):
                sp.dma_start(ident[:], a["identity"]).then_inc(setup_in, 16)
                sp.dma_start(xt[:, 0:CTX_TILES], a["ctx"].rearrange("b (t p) d -> p (b t) d", p=P)).then_inc(x_in, 16)
                sp.dma_start(xt[:, CTX_TILES:TT], a["x"].rearrange("b (t p) d -> p (b t) d", p=P)).then_inc(x_in, 16)
                sp.dma_start(cosT[:], a["cos"].rearrange("(t p) d -> p t d", p=P)).then_inc(setup_in, 16)
                sp.dma_start(sinT[:], a["sin"].rearrange("(t p) d -> p t d", p=P)).then_inc(setup_in, 16)
                sp.wait_ge(setup_in, 48)

            @block.gpsimd
            def _(pool):
                nc.gpsimd.memset(ones[:], 1.0).then_inc(setup_pool, 1)
                nc.gpsimd.memset(mhalf[:], -0.5).then_inc(setup_pool, 1)

            @block.tensor
            def _(pe):
                pe.wait_ge(setup_in, 48)
                pe.wait_ge(x_in, 32)
                for t in range(TT):
                    for h in range(2):
                        g = 2 * t + h
                        if g >= 8:
                            pe.wait_ge(x_kept, g - 7)
                        for k in range(4):
                            f = 4 * h + k
                            mm = nc.tensor.transpose(psum[:, g % 8, k * P:(k + 1) * P],
                                                     xt[:, t, f * P:(f + 1) * P], ident[:])
                        mm.then_inc(x_turned, 1)

            @block.vector
            def _(dve):
                for g in range(2 * TT):
                    t, h = g // 2, g % 2
                    dve.wait_ge(x_turned, g + 1)
                    nc.vector.tensor_copy(A[:, 4 * h:4 * h + 4, t * P:(t + 1) * P],
                                          psum[:, g % 8].rearrange("p (k n) -> p k n", k=4)).then_inc(x_kept, 1)

        MU, MS = 12, 3
        m_in, m_vec, m_loaded = sem("m_in"), sem("m_vec"), [sem(f"m_loaded{s}") for s in range(MS)]
        m_turned, m_step, m_sig, m_exp = sem("m_turned"), sem("m_step"), sem("m_sig"), sem("m_exp")

        def modulation(layer):
            with ExitStack() as z:
                rows = sb(f"rows{layer}", [P, P], F32, z)
                lamv = sb(f"lamv{layer}", [P, 4, HD], F32, z)
                lamp = sb(f"lamp{layer}", [P, 2, HD], F32, z)
                sg = sb(f"sg{layer}", [P, 2 * KT], F32, z)
                wm = [sb(f"wm{layer}_{s}", [P, KT, 512], F32, z) for s in range(MS)]
                block = z.enter_context(nc.Block())
                lin = 16 * 9 * (layer + 1)
                l0 = MU // MS * 16 * layer
                used0 = units.used
                units.used += MU

                @block.sync
                def _(sp):
                    for r, src in ((R_C, a["c"].rearrange("b (k p) -> (b k) p", p=P)),
                                   (R_CC, a["c_ctx"].rearrange("(k p) -> k p", p=P)),
                                   (R_GPM, a["g_pre_mix"][layer].rearrange("(k p) -> k p", p=P)),
                                   (R_GQM, a["g_post_mix"][layer].rearrange("(k p) -> k p", p=P)),
                                   (R_GPF, a["g_pre_ffn"][layer].rearrange("(k p) -> k p", p=P)),
                                   (R_GQF, a["g_post_ffn"][layer].rearrange("(k p) -> k p", p=P)),
                                   (R_BMOD, a["b_mod"][layer].rearrange("(k p) -> k p", p=P)),
                                   (R_PSC, a["pool_scale"][layer].rearrange("(k p) -> k p", p=P)),
                                   (R_SUB, a["diff_subln"][layer].rearrange("(k p) -> k p", p=P))):
                        sp.dma_start(rows[r:r + src.shape[0], :], src).then_inc(m_vec, 16)
                    src = a["w_mod"][layer].rearrange("(k p) n -> p k n", p=P)
                    for s in range(MS):
                        sp.dma_start(wm[s][:], src[:, :, s * 512:(s + 1) * 512]).then_inc(m_loaded[s], 16)
                    with sp.Fori(1, MU // MS) as i:
                        for s in range(MS):
                            off = sp.snap(i * (MS * 512) + s * 512)
                            done = sp.snap(i * MS + (used0 + s + 1 - MS))
                            sp.wait_ge(unit_used, done)
                            sp.dma_start(wm[s][:], src[:, :, bass.ds(off, 512)]).then_inc(m_loaded[s], 16)

                @block.gpsimd
                def _(pool):
                    for g in range(GROUP + 1):
                        g_dram = a["gqa_q_norm" if g < GROUP else "gqa_k_norm"][layer]
                        pool.dma_start(headG[:, g, :], g_dram.rearrange("(o d) -> o d", o=1).broadcast_to([P, HD])
                                       ).then_inc(m_in, 16)
                    for n, name in enumerate(("lambda_q1", "lambda_k1", "lambda_q2", "lambda_k2")):
                        pool.dma_start(lamv[:, n, :], a[name][layer].rearrange("(o d) -> o d", o=1)
                                       .broadcast_to([P, HD])).then_inc(m_in, 16)

                @block.scalar
                def _(act):
                    act.wait_ge(m_step, 11 * layer + 1)
                    nc.scalar.activation(sg[:], vec[:, 0:2 * KT], ACT.Sigmoid).then_inc(m_sig, 1)
                    act.wait_ge(m_step, 11 * layer + 4)
                    nc.scalar.activation(lame[:], lams[:], ACT.Exp).then_inc(m_exp, 1)

                @block.tensor
                def _(pe):
                    pe.wait_ge(m_vec, 16 * 9 * (layer + 1))
                    nc.tensor.transpose(psum[:, 1, 0:ROWS], rows[0:ROWS, :], ident[0:ROWS, 0:ROWS]).then_inc(m_turned, 1)
                    pe.wait_ge(m_step, 11 * layer + 2)
                    with pe.Fori(0, MU // MS) as i:
                        for s in range(MS):
                            pe.wait_ge(m_loaded[s], i * 16 + (l0 + 16))
                            for q in range(4):
                                for k in range(KT):
                                    mm = nc.tensor.matmul(psum[:, 0, bass.ds(i * (MS * 8) + (s * 8 + q * 2), 2)],
                                                          wm[s][:, k, q * P:(q + 1) * P], csil[:, k, :],
                                                          start=k == 0, stop=k == KT - 1)
                            mm.then_inc(unit_used, 1)

                @block.vector
                def _(dve):
                    s0 = 11 * layer
                    dve.wait_ge(m_turned, layer + 1)
                    nc.vector.tensor_copy(vec[:], psum[:, 1, 0:ROWS]).then_inc(m_step, 1)
                    dve.wait_ge(m_sig, layer + 1)
                    nc.vector.tensor_tensor(csil[:].rearrange("p k s -> p s k"),
                                            vec[:, 0:2 * KT].rearrange("p (s k) -> p s k", s=2),
                                            sg[:].rearrange("p (s k) -> p s k", s=2), ALU.mult).then_inc(m_step, 1)
                    dve.wait_ge(m_in, lin)
                    nc.vector.tensor_tensor(lamp[:], lamv[:].rearrange("p (n q) d -> p q n d", q=2)[:, 0],
                                            lamv[:].rearrange("p (n q) d -> p q n d", q=2)[:, 1],
                                            ALU.mult).then_inc(m_step, 1)
                    dve.wait_ge(m_step, s0 + 3)
                    nc.vector.tensor_reduce(lams[:], lamp[:], AX.X, ALU.add).then_inc(m_step, 1)
                    dve.wait_ge(m_exp, layer + 1)
                    nc.vector.scalar_tensor_tensor(lam[:], lame[:, 0:1], lambda_init(layer), lame[:, 1:2],
                                                   ALU.add, ALU.subtract).then_inc(m_step, 1)
                    nc.vector.tensor_scalar(subg[:], vec[:, R_SUB:R_SUB + 1], 1.0 - lambda_init(layer), None,
                                            ALU.mult).then_inc(m_step, 1)
                    dve.wait_ge(unit_used, used0 + MU)
                    nc.vector.tensor_tensor(mod[:], psum[:, 0, 0:12 * KT].rearrange("p (k s) -> p k s", s=2),
                                            vec[:, R_BMOD:R_BMOD + 6 * KT].rearrange("p (k o) -> p k o", o=1)
                                            .broadcast_to([P, 6 * KT, 2]), ALU.add).then_inc(m_step, 1)
                    dve.wait_ge(m_step, s0 + 7)

                    def gain(r):
                        return vec[:, r:r + KT].rearrange("p (k o) -> p k o", o=1).broadcast_to([P, KT, 2])

                    nc.vector.scalar_tensor_tensor(preA[:], mod[:, KT:2 * KT], 1.0, gain(R_GPM), ALU.add, ALU.mult
                                                   ).then_inc(m_step, 1)
                    nc.vector.tensor_tensor(postA[:], mod[:, 2 * KT:3 * KT], gain(R_GQM), ALU.mult).then_inc(m_step, 1)
                    nc.vector.scalar_tensor_tensor(preF[:], mod[:, 4 * KT:5 * KT], 1.0, gain(R_GPF), ALU.add, ALU.mult
                                                   ).then_inc(m_step, 1)
                    nc.vector.tensor_tensor(postF[:], mod[:, 5 * KT:6 * KT], gain(R_GQF), ALU.mult).then_inc(m_step, 1)

        n_sq, n_acc, n_ss, n_var, n_pow, n_diag, n_bc, n_sc, n_x, n_aff, n_hi, n_lo = (
            sem(n) for n in ("n_sq", "n_acc", "n_ss", "n_var", "n_pow", "n_diag", "n_bc", "n_sc", "n_x", "n_aff",
                             "n_hi", "n_lo"))
        n_spill, n_reload = sem("n_spill"), sem("n_reload")
        count = {"r": 0, "x": 0, "h": 0, "spill": 0, "reload": 0}

        def norms(tag, chunks, X, gains=None, shift_at=0, Y=None, post=None, X_out=None, spill=False, reload=False):
            X_out = X if X_out is None else X_out
            with ExitStack() as z:
                sq = sb(f"sq_{tag}", [P, KT, CH], F32, z)
                t1 = sb(f"t1_{tag}", [P, KT, CH], F32, z)
                t2 = sb(f"t2_{tag}", [P, KT, CH], F32, z)
                acc = sb(f"acc_{tag}", [P, CH], F32, z)
                var = sb(f"var_{tag}", [P, 2], F32, z)
                rstd = sb(f"rstd_{tag}", [P, 2], F32, z)
                diag = sb(f"diag_{tag}", [P, 2, P], F32, z)
                passes = [(c, what) for c in chunks for what in (["Y"] if Y is not None else []) +
                          (["x"] if gains is not None else [])]
                r0, x0, h0 = count["r"], count["x"], count["h"]
                rl0, sp0 = count["reload"], count["spill"]
                count["r"] += len(passes)
                if Y is not None:
                    count["x"] += len(chunks)
                if gains is not None:
                    count["h"] += len(chunks)
                count["spill"] += 16 if spill else 0
                count["reload"] += 16 if reload else 0
                block = z.enter_context(nc.Block())

                def cols(c):
                    return slice(c * CH, (c + 1) * CH)

                def stream(c):
                    return 1 if c * CH < CTX else 0

                @block.sync
                def _(sp):
                    if reload:
                        sp.dma_start(X[:].rearrange("p k t -> p (k t)"), xdram).then_inc(n_reload, 16)
                    if spill:
                        sp.dma_start(xdram, X[:].rearrange("p k t -> p (k t)")).then_inc(n_spill, 16)
                        sp.wait_ge(n_spill, sp0 + 16)

                @block.scalar
                def _(act):
                    x, h = x0, h0
                    for n, (c, what) in enumerate(passes):
                        r = r0 + n
                        src = Y if what == "Y" else X_out
                        if what == "Y":
                            x += 1
                        elif Y is not None:
                            act.wait_ge(n_x, x)
                        if n:
                            act.wait_ge(n_acc, r)
                        nc.scalar.activation(sq[:], src[:, :, cols(c)], ACT.Square).then_inc(n_sq, 1)
                        if what == "x":
                            h += 1
                            act.wait_ge(n_sc, r + 1)
                            if h > h0 + 1:
                                act.wait_ge(n_lo, h - 1)
                            s = stream(c)
                            for k in range(KT):
                                aff = nc.scalar.activation(t2[:, k], t1[:, k], ACT.Identity,
                                                           bias=mod[:, shift_at + k, s:s + 1],
                                                           scale=gains[:, k, s:s + 1])
                            aff.then_inc(n_aff, 1)
                            act.wait_ge(n_aff, h)
                            nc.scalar.activation(Hhi[:, :, cols(c)], t2[:], ACT.Copy).then_inc(n_hi, 1)

                @block.vector
                def _(dve):
                    x, h = x0, h0
                    if reload:
                        dve.wait_ge(n_reload, rl0 + 16)
                    for n, (c, what) in enumerate(passes):
                        r = r0 + n
                        dve.wait_ge(n_sq, r + 1)
                        if n:
                            dve.wait_ge(n_ss, r)
                        nc.vector.tensor_reduce(acc[:], sq[:].rearrange("p k t -> p t k"), AX.X, ALU.add
                                                ).then_inc(n_acc, 1)
                        dve.wait_ge(n_ss, r + 1)
                        if n:
                            dve.wait_ge(n_pow, r)
                        nc.vector.tensor_scalar(var[:], psum[:, 0, 0:4].rearrange("p (t o) -> p t o", o=2)[:, :, 0],
                                                1.0 / D, EPS, ALU.mult, ALU.add).then_inc(n_var, 1)
                        dve.wait_ge(n_pow, r + 1)
                        if n:
                            dve.wait_ge(n_bc, r)
                        for t in range(2):
                            dg = nc.vector.tensor_scalar(diag[:, t], ident[:], rstd[:, t:t + 1], None, ALU.mult)
                        dg.then_inc(n_diag, 1)
                        dve.wait_ge(n_bc, r + 1)
                        src = Y if what == "Y" else X_out
                        if n:
                            dve.wait_ge(n_aff, h)
                        nc.vector.tensor_tensor(t1[:], src[:, :, cols(c)],
                                                psum[:, 1, 0:CH].rearrange("p (o t) -> p o t", o=1)
                                                .broadcast_to([P, KT, CH]), ALU.mult).then_inc(n_sc, 1)
                        s = stream(c)
                        if what == "Y":
                            x += 1
                            dve.wait_ge(n_sc, r + 1)
                            for k in range(KT):
                                up = nc.vector.scalar_tensor_tensor(X_out[:, k, cols(c)], t1[:, k],
                                                                    post[:, k, s:s + 1], X[:, k, cols(c)], ALU.mult,
                                                                    ALU.add)
                            up.then_inc(n_x, 1)
                        else:
                            h += 1
                            dve.wait_ge(n_hi, h)
                            nc.vector.tensor_tensor(Hlo[:, :, cols(c)], t2[:], Hhi[:, :, cols(c)].bitcast(F32),
                                                    ALU.subtract).then_inc(n_lo, 1)

                @block.gpsimd
                def _(pool):
                    for n in range(len(passes)):
                        r = r0 + n
                        pool.wait_ge(n_var, r + 1)
                        if n:
                            pool.wait_ge(n_diag, r)
                        nc.gpsimd.tensor_tensor(rstd[:], var[:], mhalf[:, 0:2], ALU.pow).then_inc(n_pow, 1)

                @block.tensor
                def _(pe):
                    for n in range(len(passes)):
                        r = r0 + n
                        pe.wait_ge(n_acc, r + 1)
                        if n:
                            pe.wait_ge(n_var, r)
                        for t in range(2):
                            mm = nc.tensor.matmul(psum[:, 0, 2 * t:2 * t + 2], acc[:, t * P:(t + 1) * P],
                                                  ones[:, 0:2], start=True, stop=True)
                        mm.then_inc(n_ss, 1)
                        pe.wait_ge(n_diag, r + 1)
                        if n:
                            pe.wait_ge(n_sc, r)
                        nc.tensor.matmul(psum[:, 1, 0:CH], ones[:], diag[:].rearrange("p t n -> p (t n)"),
                                         start=True, stop=True).then_inc(n_bc, 1)

        GEMM, SBANK, TR, NTR, OB = 0, 1, 5, 2, 7

        def attention(layer):
            q_tiles = range(TT) if layer < DEPTH - 1 else range(CTX_TILES, TT)
            w_in = a["w_in"][layer].rearrange("(k p) n -> p k n", p=P)
            ph = units.phase([0, 1, 2] * NPANEL, [n % RAW for n in range(3 * NPANEL)], 1,
                             [1, 1, 1] * DIFF_HEADS + [1, 1, 2] * KV_HEADS)
            units.used -= 3 * NPANEL
            units.in_slot = {s: units.used for s in range(RING)}

            def sm(n):
                return sem(f"{n}_{layer}")

            gemm_done, act_read, dve_read = sm("gemm_done"), sm("act_read"), sm("dve_read")
            sq_done, head_var, head_pow = sm("sq_done"), sm("head_var"), sm("head_pow")
            normed, roped, stack_hi, stack_lo, stacks_in = sm("normed"), sm("roped"), sm("stack_hi"), sm("stack_lo"), sm("stacks_in")
            scores, negmax, exped, probs = sm("scores"), sm("negmax"), sm("exped"), sm("probs")
            turned, pt_hi, pt_lo, pv_done = sm("turned"), sm("pt_hi"), sm("pt_lo"), sm("pv_done")
            o_read, o_sq, o_var, o_pow, o_norm, o_out = (sm("o_read"), sm("o_sq"), sm("o_var"), sm("o_pow"),
                                                         sm("o_norm"), sm("o_out"))
            dchain = sm("dchain")

            class Prep:

                def __init__(s, g):
                    s.g, s.p, s.t = g, g // TT, g % TT
                    s.diff = s.p < DIFF_HEADS
                    s.q = s.t in q_tiles
                    s.nq = 2 if s.diff else GROUP
                    s.nk = 2 if s.diff else 1
                    s.vd = 2 * HD if s.diff else HD
                    s.g0 = 0 if s.q else s.nq
                    s.g1 = s.nq + s.nk
                    s.stacks = list(range(s.g0, 6))
                    s.uses = [s.stacks[i:i + 3] for i in range(0, len(s.stacks), 3)]
                    s.rope = s.t >= CTX_TILES

            class Item:

                def __init__(s, p, t, j):
                    s.p, s.t, s.j = p, t, j
                    s.diff = p < DIFF_HEADS
                    s.nkt = CTX_TILES if t < CTX_TILES else TT
                    s.keys = s.nkt * P
                    s.last = s.diff or j == GROUP - 1

            preps = [Prep(g) for g in range(NPANEL * TT)]
            items = [Item(p, t, j) for p in range(NPANEL) for t in q_tiles
                     for j in range(1 if p < DIFF_HEADS else GROUP)]
            lead = TT + 1
            slots = [dict(preps=[], late=[], outs=[], finish=None) for _ in range(lead + len(items) + 4)]
            for t in range(TT):
                slots[t]["preps"] = [preps[t]]
            for p in range(NPANEL - 1):
                first = lead + sum(it.p < p for it in items)
                count = sum(it.p == p for it in items)
                for t in range(TT):
                    at = (t * count // TT - 1) if count <= TT else max(0, (t + 1) * count // TT - 3)
                    slots[first + at]["preps"].append(preps[(p + 1) * TT + t])
            for n, sl in enumerate(slots):
                if sl["preps"]:
                    q = sl["preps"][-1]
                    scored = lead + sum(it.p < q.p for it in items)
                    relaxed = not q.diff and not slots[n + 1]["preps"] and n + 2 < scored
                    slots[n + 2 if relaxed else n + 1]["late"] = [q]
                    slots[n + 1 if relaxed else n]["finish"] = q
            for sl in slots:
                sl["at_once"], sl["between"] = [], []
            for p in range(1, NPANEL):
                end = [n for n, sl in enumerate(slots) if any(q.p == p - 1 for q in sl["preps"])][-1]
                start = [n for n, sl in enumerate(slots) if any(q.p == p for q in sl["preps"])][0]
                for u in range(3):
                    if start == end + 1:
                        slots[end]["at_once"].append(3 * p + u)
                    else:
                        slots[end + u * (start - end) // 3]["between"].append(3 * p + u)

            def nth(n):
                return items[n] if 0 <= n < len(items) else None

            for n, sl in enumerate(slots):
                sl["score"], sl["turn"], sl["weigh"], sl["weighed"] = (nth(n - lead - lag) for lag in range(4))
                if sl["weigh"] is not None and sl["weigh"].last:
                    slots[n + (2 if sl["weigh"].diff else 1)]["outs"].append(sl["weigh"])
            n_score = n_use = n_ptuse = n_stuse = n_out = n_norm = n_dsq = 0
            readers = []
            for i, it in enumerate(items):
                it.i, it.scores = i, []
                for _ in range(2 if it.diff else 1):
                    it.scores.append(n_score)
                    n_score += 1
            for sl in slots:
                for o in sl["outs"]:
                    o.ouse = n_use
                    n_out += 1
                    readers.append((o_out, n_out))
                    n_use += 1
                it = sl["turn"]
                if it is not None:
                    it.use0, it.pt0 = n_use, n_ptuse
                    it.ptuses = [list(range(k, min(k + 3, it.nkt))) for k in range(0, it.nkt, 3)]
                    for _ in it.ptuses:
                        n_ptuse += 1
                        readers.append((pt_lo, n_ptuse))
                        n_use += 1
                for q in sl["late"] + sl["preps"][:-1]:
                    q.use0, q.st0 = n_use, n_stuse
                    for _ in q.uses:
                        n_stuse += 1
                        readers.append((stacks_in, n_stuse))
                        n_use += 1
            kept = []
            for it in items:
                it.before = kept[n_norm - 2] if n_norm >= 2 else None
                if it.last:
                    kept.append(it)
                it.nrm = n_norm
                n_norm += it.last
                if it.diff:
                    it.dsq = n_dsq
                    n_dsq += 1
            gq = [q for q in preps if not q.diff]
            for n, q in enumerate(gq):
                q.hn, q.roped_before = n, sum(x.rope for x in gq[:n])

            with ExitStack() as z:
                qk = [sb(f"qk{b}_{layer}", [P, 6, T], F32R, z) for b in range(2)]
                vhi = [sb(f"vhi{b}_{layer}", [P, TT, 2 * HD], F32R, z) for b in range(3)]
                vlo = [sb(f"vlo{b}_{layer}", [P, TT, 2 * HD], F32R, z) for b in range(3)]
                e = [[sb(f"e{b}{s}_{layer}", [P, T], F32, z) for s in range(2)] for b in range(2)]
                pth = [sb(f"pth{b}_{layer}", [P, TT, P], F32R, z) for b in range(2)]
                ptl = [sb(f"ptl{b}_{layer}", [P, TT, P], F32R, z) for b in range(2)]
                ra = sb(f"ra_{layer}", [P, 5, HD], F32, z)
                rc = sb(f"rc_{layer}", [P, 5, HD], F32, z)
                st = sb(f"st_{layer}", [P, 6, 2 * HD], F32R, z)
                hsq = sb(f"hsq_{layer}", [P, 5, HD], F32, z)
                rd = sb(f"rd_{layer}", [P, 5, HD], F32, z)
                hss = sb(f"hss_{layer}", [P, 5], F32, z)
                hvar = sb(f"hvar_{layer}", [P, 5], F32, z)
                hpow = sb(f"hpow_{layer}", [P, 5], F32, z)
                mx = sb(f"mx_{layer}", [P, 2], F32, z)
                nmx = sb(f"nmx_{layer}", [P, 2, 2], F32, z)
                esum = sb(f"esum_{layer}", [P, 2, 2], F32, z)
                rec = sb(f"rec_{layer}", [P, 3, 2], F32, z)
                rlam = sb(f"rlam_{layer}", [P, 1], F32, z)
                osb = sb(f"osb_{layer}", [P, 2, P], F32, z)
                osq = sb(f"osq_{layer}", [P, P], F32, z)
                oss = sb(f"oss_{layer}", [P, 1], F32, z)
                ovar = sb(f"ovar_{layer}", [P, 1], F32, z)
                opow = sb(f"opow_{layer}", [P, 1], F32, z)
                onrm = sb(f"onrm_{layer}", [P, 2, 2 * P], F32, z)
                block = z.enter_context(nc.Block())

                @block.sync
                def _(sp):
                    for n in range(3 * NPANEL):
                        p, m = n // 3, n % 3
                        v = slot_view(ph.raws[n])
                        if p < DIFF_HEADS:
                            c = (POOL_W, DK_OFF, DV_OFF)[m] + p * 2 * HD
                            pieces = [(v, w_in[:, :, c:c + P])]
                        elif m < 2:
                            c = POOL_W + DIFF_W + (p - DIFF_HEADS) * GROUP * HD + m * P
                            pieces = [(v, w_in[:, :, c:c + P])]
                        else:
                            ck, cv = GK_OFF + (p - DIFF_HEADS) * HD, GV_OFF + (p - DIFF_HEADS) * HD
                            pieces = [(v[:, :, 0:HD], w_in[:, :, ck:ck + HD]), (v[:, :, HD:P], w_in[:, :, cv:cv + HD])]
                        if n >= RAW:
                            sp.wait_ge(lo_ready, ph.base + n - RAW + 1)
                        for dst, src in pieces:
                            sp.dma_start(dst, src).then_inc(landed[ph.raws[n]], 16)

                @block.tensor
                def _(pe):
                    def gemm(q):
                        pe.wait_ge(lo_ready, ph.base + 3 * q.p + 3)
                        if q.g:
                            pe.wait_ge(act_read, q.g)
                            pe.wait_ge(dve_read, q.g)
                        u0 = 0 if q.q else (1 if q.diff else 2)
                        o = psum[:, GEMM, u0 * P:3 * P]
                        tok = slice(q.t * P, (q.t + 1) * P)
                        for k in range(KT):
                            for n, (x, w) in enumerate(((Hhi, whi3), (Hhi, wlo3), (Hlo, whi3))):
                                mm = nc.tensor.matmul(o, x[:, k, tok], w[:, u0:3, k, :],
                                                      start=k == 0 and n == 0, stop=k == KT - 1 and n == 2)
                        mm.then_inc(gemm_done, 1)

                    def bank(use):
                        if use >= NTR:
                            pe.wait_ge(*readers[use - NTR])
                        return psum[:, TR + use % NTR]

                    def turn_stacks(q):
                        pe.wait_ge(stack_hi, q.g + 1)
                        pe.wait_ge(stack_lo, q.g + 1)
                        for u, group in enumerate(q.uses):
                            b = bank(q.use0 + u)
                            for n, sx in enumerate(group):
                                mm = nc.tensor.transpose(b[:, n * P:(n + 1) * P], st[:, sx, :].bitcast(F32), ident[:])
                            mm.then_inc(turned, 1)

                    def score(it):
                        b = qk[it.p % 2]
                        pe.wait_ge(stacks_in, preps[it.p * TT + TT - 1].st0 + len(preps[it.p * TT + TT - 1].uses))
                        tok = slice(it.t * P, (it.t + 1) * P)
                        for s, n in enumerate(it.scores):
                            if n >= 2:
                                pe.wait_ge(exped, n - 1)
                            qs = s if it.diff else it.j
                            ks = (2 + s, 4 + s) if it.diff else (4, 5)
                            for c in range((it.keys + 383) // 384):
                                w = min(384, it.keys)
                                for m in range(2):
                                    mm = nc.tensor.matmul(psum[:, SBANK + 2 * (n % 2) + c, 0:w], b[:, qs, tok],
                                                          b[:, ks[m], c * 384:c * 384 + w], start=m == 0, stop=m == 1)
                            mm.then_inc(scores, 1)

                    def turn_probs(it):
                        pe.wait_ge(probs, it.i + 1)
                        for u, kts in enumerate(it.ptuses):
                            b = bank(it.use0 + u)
                            for n, kt in enumerate(kts):
                                mm = nc.tensor.transpose(b[:, n * P:(n + 1) * P],
                                                         e[it.i % 2][0][:, kt * P:(kt + 1) * P], ident[:])
                            mm.then_inc(turned, 1)

                    def weigh(it):
                        pe.wait_ge(pt_hi, it.pt0 + len(it.ptuses))
                        pe.wait_ge(pt_lo, it.pt0 + len(it.ptuses))
                        if it.i:
                            pe.wait_ge(o_read, it.i)
                        x, y = pth[it.i % 2], ptl[it.i % 2]
                        vh, vl = vhi[it.p % 3], vlo[it.p % 3]
                        for kt in range(it.nkt):
                            terms = (((x, vh, 2 * HD), (x, vl, 2 * HD), (y, vh, 2 * HD)) if it.diff else
                                     ((x, vh, 2 * HD), (y, vh, HD)))
                            for n, (w, v, wd) in enumerate(terms):
                                mm = nc.tensor.matmul(psum[:, OB, 0:wd], w[:, kt, :], v[:, kt, 0:wd],
                                                      start=kt == 0 and n == 0,
                                                      stop=kt == it.nkt - 1 and n == len(terms) - 1)
                        mm.then_inc(pv_done, 1)

                    def turn_out(it):
                        if it.diff:
                            pe.wait_ge(o_norm, it.dsq + 1)
                        else:
                            pe.wait_ge(o_read, it.i + 1)
                        b = bank(it.ouse)
                        for n in range(1 if it.diff else 2):
                            mm = nc.tensor.transpose(b[:, n * P:(n + 1) * P], onrm[:, it.nrm % 2, n * P:(n + 1) * P],
                                                     ident[:])
                        mm.then_inc(turned, 1)

                    for sl in slots:
                        if sl["preps"]:
                            gemm(sl["preps"][0])
                        for o in sl["outs"]:
                            turn_out(o)
                        if sl["score"] is not None:
                            score(sl["score"])
                        if sl["turn"] is not None:
                            turn_probs(sl["turn"])
                        if sl["weigh"] is not None:
                            weigh(sl["weigh"])
                        for q in sl["late"]:
                            turn_stacks(q)
                        if len(sl["preps"]) > 1:
                            gemm(sl["preps"][1])
                            turn_stacks(sl["preps"][0])

                @block.scalar
                def _(act):
                    def weight_hi(n):
                        act.wait_ge(landed[ph.raws[n]], ph.landed(n, 0))
                        if n >= 3:
                            act.wait_ge(gemm_done, TT * (n // 3))
                        nc.scalar.activation(whi3[:, n % 3].rearrange("p k n -> p (k n)"), raw[ph.raws[n]][:],
                                             ACT.Copy).then_inc(hi_ready, 1)

                    def read_projection(q):
                        act.wait_ge(gemm_done, q.g + 1)
                        if not q.diff:
                            if q.hn:
                                act.wait_ge(head_var, q.hn)
                            nc.scalar.activation(hsq[:, q.g0:q.g1].rearrange("p g d -> p (g d)"),
                                                 psum[:, GEMM, q.g0 * HD:q.g1 * HD], ACT.Square).then_inc(sq_done, 1)
                        nc.scalar.activation(vhi[q.p % 3][:, q.t, 0:q.vd], psum[:, GEMM, 3 * P - q.vd:3 * P], ACT.Copy
                                             ).then_inc(act_read, 1)

                    def stack_his(q):
                        act.wait_ge(roped, q.g + 1)
                        if q.g:
                            last = preps[q.g - 1]
                            act.wait_ge(turned, last.use0 + len(last.uses))
                        if q.q:
                            nc.scalar.activation(st[:, 0:q.nq, 0:HD], rc[:, 0:q.nq], ACT.Copy)
                        k0 = q.nq
                        src = rc[:, q.nq:q.g1].rearrange("p g (o d) -> p g o d", o=1).broadcast_to([P, q.nk, 2, HD])
                        nc.scalar.activation(st[:, k0:k0 + q.nk].rearrange("p s (o d) -> p s o d", o=2), src, ACT.Copy
                                             ).then_inc(stack_hi, 1)

                    def keep_stacks(q):
                        for u, group in enumerate(q.uses):
                            act.wait_ge(turned, q.use0 + u + 1)
                            nc.scalar.activation(qk[q.p % 2][:, group[0]:group[-1] + 1, q.t * P:(q.t + 1) * P],
                                                 psum[:, TR + (q.use0 + u) % NTR, 0:len(group) * P]
                                                 .rearrange("p (s n) -> p s n", n=P), ACT.Copy).then_inc(stacks_in, 1)

                    def exps(it):
                        for s, n in enumerate(it.scores):
                            act.wait_ge(negmax, n + 1)
                            src = psum[:, SBANK + 2 * (n % 2):SBANK + 2 * (n % 2) + 2, 0:384]
                            dst = e[it.i % 2][s][:].rearrange("p (c w) -> p c w", c=2)
                            if it.keys < T:
                                src, dst = psum[:, SBANK + 2 * (n % 2), 0:it.keys], e[it.i % 2][s][:, 0:it.keys]
                            nc.scalar.activation(dst, src, ACT.Exp, bias=nmx[:, it.i % 2, s:s + 1], scale=SCALE,
                                                 accum_out=esum[:, it.i % 2, s:s + 1]).then_inc(exped, 1)

                    def keep_probs(it):
                        for u, kts in enumerate(it.ptuses):
                            act.wait_ge(turned, it.use0 + u + 1)
                            nc.scalar.activation(pth[it.i % 2][:, kts[0]:kts[-1] + 1, :],
                                                 psum[:, TR + (it.use0 + u) % NTR, 0:len(kts) * P]
                                                 .rearrange("p (s n) -> p s n", n=P), ACT.Copy).then_inc(pt_hi, 1)

                    def square_output(it):
                        act.wait_ge(o_read, it.i + 1)
                        if it.dsq:
                            act.wait_ge(o_var, it.dsq)
                        nc.scalar.activation(osq[:], osb[:, it.i % 2], ACT.Square, accum_out=oss[:]
                                             ).then_inc(o_sq, 1)

                    for n in range(3):
                        weight_hi(n)
                    for sl in slots:
                        if sl["weighed"] is not None and sl["weighed"].diff:
                            square_output(sl["weighed"])
                        if sl["preps"]:
                            read_projection(sl["preps"][0])
                        if len(sl["preps"]) == 1:
                            for n in sl["at_once"][:2]:
                                weight_hi(n)
                        if sl["turn"] is not None:
                            keep_probs(sl["turn"])
                        if len(sl["preps"]) == 1:
                            for n in sl["at_once"][2:]:
                                weight_hi(n)
                        if sl["score"] is not None:
                            exps(sl["score"])
                        for q in sl["late"]:
                            keep_stacks(q)
                        if len(sl["preps"]) > 1:
                            stack_his(sl["preps"][0])
                            read_projection(sl["preps"][1])
                            for n in sl["at_once"]:
                                weight_hi(n)
                            keep_stacks(sl["preps"][0])
                        if sl["finish"] is not None:
                            stack_his(sl["finish"])
                        for n in sl["between"]:
                            weight_hi(n)

                @block.vector
                def _(dve):
                    steps = [0]

                    def link(ins):
                        steps[0] += 1
                        ins.then_inc(dchain, 1)
                        dve.wait_ge(dchain, steps[0])

                    def weight_lo(n):
                        dve.wait_ge(hi_ready, ph.base + n + 1)
                        nc.vector.tensor_tensor(wlo3[:, n % 3].rearrange("p k n -> p (k n)"), raw[ph.raws[n]][:],
                                                whi3[:, n % 3].rearrange("p k n -> p (k n)").bitcast(F32),
                                                ALU.subtract).then_inc(lo_ready, 1)

                    def head_vars(q):
                        dve.wait_ge(sq_done, q.hn + 1)
                        link(nc.vector.tensor_reduce(hss[:, q.g0:q.g1], hsq[:, q.g0:q.g1], AX.X, ALU.add))
                        nc.vector.tensor_scalar(hvar[:, q.g0:q.g1], hss[:, q.g0:q.g1], 1.0 / HD, EPS, ALU.mult, ALU.add
                                                ).then_inc(head_var, 1)

                    def rotate(q, x, between):
                        g0, g1 = q.g0, q.g1

                        def table(tab, first, step):
                            y = tab[:, q.t - CTX_TILES, first::step].rearrange("p (o d) -> p o d", o=1)
                            return y.broadcast_to([P, g1 - g0, HD // step])

                        nc.vector.tensor_tensor(ra[:, g0:g1], x, table(cosT, 0, 1), ALU.mult)
                        nc.vector.tensor_tensor(rd[:, g0:g1, 0::2], x[:, :, 1::2], table(sinT, 0, 2), ALU.mult)
                        sw = nc.vector.tensor_tensor(rd[:, g0:g1, 1::2], x[:, :, 0::2], table(sinT, 1, 2), ALU.mult)
                        if between is not None:
                            between()
                            dve.wait_ge(dve_read, q.g + 1)
                        else:
                            link(sw)
                        nc.vector.tensor_tensor(rc[:, g0:g1], ra[:, g0:g1], rd[:, g0:g1], ALU.add).then_inc(roped, 1)

                    def finish_heads(q):
                        if not q.diff and q.rope:
                            dve.wait_ge(normed, q.roped_before + 1)
                            rotate(q, rc[:, q.g0:q.g1], None)
                        stack_los(q)

                    def shape_heads(q):
                        dve.wait_ge(act_read, q.g + 1)
                        if q.g:
                            dve.wait_ge(stack_lo, q.g)
                        g0, g1 = q.g0, q.g1
                        ng = g1 - g0

                        def values_lo():
                            lo = vlo[q.p % 3][:, q.t, :] if q.diff else vhi[q.p % 3][:, q.t, HD:2 * HD]
                            nc.vector.tensor_tensor(lo, psum[:, GEMM, 3 * P - q.vd:3 * P],
                                                    vhi[q.p % 3][:, q.t, 0:q.vd].bitcast(F32), ALU.subtract
                                                    ).then_inc(dve_read, 1)

                        x = psum[:, GEMM, g0 * HD:g1 * HD].rearrange("p (g d) -> p g d", d=HD)
                        if q.diff and q.rope:
                            rotate(q, x, values_lo)
                        elif q.diff:
                            nc.vector.tensor_copy(rc[:, g0:g1], x).then_inc(roped, 1)
                            values_lo()
                        else:
                            dve.wait_ge(head_pow, q.hn + 1)
                            r = hpow[:, g0:g1].rearrange("p (g o) -> p g o", o=1).broadcast_to([P, ng, HD])
                            nc.vector.tensor_tensor(ra[:, g0:g1], x, r, ALU.mult)
                            values_lo()
                            dve.wait_ge(dve_read, q.g + 1)
                            if q.rope:
                                nc.vector.tensor_tensor(rc[:, g0:g1], ra[:, g0:g1], headG[:, g0:g1], ALU.mult
                                                        ).then_inc(normed, 1)
                            else:
                                nc.vector.tensor_tensor(rc[:, g0:g1], ra[:, g0:g1], headG[:, g0:g1], ALU.mult
                                                        ).then_inc(roped, 1)

                    def stack_los(q):
                        dve.wait_ge(stack_hi, q.g + 1)
                        if q.q:
                            nc.vector.tensor_tensor(st[:, 0:q.nq, HD:2 * HD], rc[:, 0:q.nq],
                                                    st[:, 0:q.nq, 0:HD].bitcast(F32), ALU.subtract)
                        ka, kb = q.nq, q.nq + q.nk
                        src = rc[:, q.nq:q.g1].rearrange("p g (o d) -> p g o d", o=1).broadcast_to([P, q.nk, 2, HD])
                        nc.vector.tensor_tensor(st[:, kb:kb + q.nk].rearrange("p s (o d) -> p s o d", o=2), src,
                                                st[:, ka:ka + q.nk].bitcast(F32)
                                                .rearrange("p s (o d) -> p s o d", o=2), ALU.subtract
                                                ).then_inc(stack_lo, 1)

                    def maxima(it):
                        for s, n in enumerate(it.scores):
                            dve.wait_ge(scores, n + 1)
                            if it.keys < T:
                                link(nc.vector.tensor_reduce(mx[:, s:s + 1], psum[:, SBANK + 2 * (n % 2), 0:it.keys],
                                                             AX.X, ALU.max))
                            else:
                                link(nc.vector.tensor_reduce(
                                    mx[:, s:s + 1], psum[:, SBANK + 2 * (n % 2):SBANK + 2 * (n % 2) + 2, 0:384],
                                    AX.XY, ALU.max))
                            nc.vector.tensor_scalar(nmx[:, it.i % 2, s:s + 1], mx[:, s:s + 1], -SCALE, None, ALU.mult
                                                    ).then_inc(negmax, 1)

                    def normalise(it):
                        b, r = it.i % 2, it.i % 3
                        ns = len(it.scores)
                        dve.wait_ge(exped, it.scores[-1] + 1)
                        if not it.diff:
                            nc.vector.reciprocal(rec[:, r, 0:1], esum[:, b, 0:1]).then_inc(probs, 1)
                            return
                        link(nc.vector.reciprocal(rec[:, r, 0:ns], esum[:, b, 0:ns]))
                        link(nc.vector.tensor_scalar(rlam[:], rec[:, r, 1:2], lam[:, 0:1], None, ALU.mult))
                        link(nc.vector.tensor_scalar(e[b][1][:, 0:it.keys], e[b][1][:, 0:it.keys], rlam[:, 0:1], None,
                                                     ALU.mult))
                        nc.vector.scalar_tensor_tensor(e[b][0][:, 0:it.keys], e[b][0][:, 0:it.keys], rec[:, r, 0:1],
                                                       e[b][1][:, 0:it.keys], ALU.mult, ALU.subtract
                                                       ).then_inc(probs, 1)

                    def probs_lo(it):
                        for u, kts in enumerate(it.ptuses):
                            dve.wait_ge(pt_hi, it.pt0 + u + 1)
                            sl_ = slice(kts[0], kts[-1] + 1)
                            nc.vector.tensor_tensor(ptl[it.i % 2][:, sl_, :],
                                                    psum[:, TR + (it.use0 + u) % NTR, 0:len(kts) * P]
                                                    .rearrange("p (s n) -> p s n", n=P),
                                                    pth[it.i % 2][:, sl_, :].bitcast(F32), ALU.subtract
                                                    ).then_inc(pt_lo, 1)

                    def read_output(it):
                        dve.wait_ge(pv_done, it.i + 1)
                        if it.diff:
                            nc.vector.tensor_copy(osb[:, it.i % 2], psum[:, OB, 0:P]).then_inc(o_read, 1)
                        else:
                            if it.j == 0 and it.before is not None:
                                dve.wait_ge(turned, it.before.ouse + 1)
                            inv = rec[:, it.i % 3, 0:1]
                            part = osb[:, it.i % 2, 0:HD]
                            link(nc.vector.tensor_scalar(part, psum[:, OB, HD:2 * HD], inv, None,
                                                         ALU.mult))
                            nc.vector.scalar_tensor_tensor(onrm[:, it.nrm % 2, it.j * HD:(it.j + 1) * HD],
                                                           psum[:, OB, 0:HD], inv, part, ALU.mult, ALU.add
                                                           ).then_inc(o_read, 1)

                    def output_var(it):
                        dve.wait_ge(o_sq, it.dsq + 1)
                        if it.dsq:
                            dve.wait_ge(o_pow, it.dsq)
                        nc.vector.tensor_scalar(ovar[:], oss[:], 1.0 / (2 * HD), EPS, ALU.mult, ALU.add
                                                ).then_inc(o_var, 1)

                    def output_norm(it):
                        dve.wait_ge(o_pow, it.dsq + 1)
                        if it.before is not None:
                            dve.wait_ge(turned, it.before.ouse + 1)
                        nc.vector.tensor_scalar(onrm[:, it.nrm % 2, 0:P], osb[:, it.i % 2], opow[:, 0:1], None,
                                                ALU.mult).then_inc(o_norm, 1)

                    def keep_output(it):
                        dve.wait_ge(turned, it.ouse + 1)
                        b = psum[:, TR + it.ouse % NTR]
                        tok = slice(it.t * P, (it.t + 1) * P)
                        if it.diff:
                            nc.vector.tensor_scalar(A[:, it.p, tok], b[:, 0:P], subg[:, 0:1], None, ALU.mult
                                                    ).then_inc(o_out, 1)
                        else:
                            f = DIFF_HEADS + 2 * (it.p - DIFF_HEADS)
                            nc.vector.tensor_copy(A[:, f:f + 2, tok], b[:, 0:2 * P].rearrange("p (s n) -> p s n", n=P)
                                                  ).then_inc(o_out, 1)

                    for n in range(3):
                        weight_lo(n)
                    for sl in slots:
                        done = sl["weighed"] if sl["weighed"] is not None and sl["weighed"].diff else None
                        if done is not None:
                            output_var(done)
                        q, more = (sl["preps"] + [None, None])[:2]
                        one = more is None
                        if q is not None and q.diff:
                            shape_heads(q)
                        elif q is not None:
                            head_vars(q)
                        for o in sl["outs"]:
                            keep_output(o)
                        for n in sl["at_once"][:1] if one else []:
                            weight_lo(n)
                        for what in ((probs_lo, maxima) if q is not None and q.diff else (maxima, probs_lo)):
                            it = sl["turn" if what is probs_lo else "score"]
                            if it is not None:
                                what(it)
                            for n in sl["at_once"][1:] if one and what is probs_lo else []:
                                weight_lo(n)
                        if sl["score"] is not None:
                            normalise(sl["score"])
                        if done is not None:
                            output_norm(done)
                        if sl["weigh"] is not None:
                            read_output(sl["weigh"])
                        if q is not None and not q.diff:
                            shape_heads(q)
                        if more is not None:
                            finish_heads(q)
                            if not more.diff:
                                head_vars(more)
                            shape_heads(more)
                            for n in sl["at_once"]:
                                weight_lo(n)
                        if sl["finish"] is not None:
                            finish_heads(sl["finish"])
                        for n in sl["between"]:
                            weight_lo(n)

                @block.gpsimd
                def _(pool):
                    for n, sl in enumerate(slots):
                        it = sl["weighed"]
                        if it is not None and it.diff:
                            pool.wait_ge(o_var, it.dsq + 1)
                            if it.dsq:
                                pool.wait_ge(o_norm, it.dsq)
                            nc.gpsimd.tensor_tensor(opow[:], ovar[:], mhalf[:, 0:1], ALU.pow).then_inc(o_pow, 1)
                        for q in sl["preps"]:
                            if not q.diff:
                                pool.wait_ge(head_var, q.hn + 1)
                                if q.g:
                                    pool.wait_ge(dve_read, q.g)
                                nc.gpsimd.tensor_tensor(hpow[:, q.g0:q.g1], hvar[:, q.g0:q.g1],
                                                        mhalf[:, q.g0:q.g1], ALU.pow).then_inc(head_pow, 1)

        def wide(layer):
            if layer < DEPTH - 1:
                return [(0, 0, 384), (1, 384, 384)], 0
            return [(0, CTX, SEQ)], CTX

        def grid(ap, layer):
            chunks, t0 = wide(layer)
            return ap[:, t0:T].rearrange("p (c w) -> p c w", c=len(chunks))

        def pair(u, layer):
            chunks, _ = wide(layer)
            return psum[:, 2 * (u % 4):2 * (u % 4) + len(chunks), 0:chunks[0][2]]

        po_step, po_hi, po_lo, po_mm, po_out, po_table, o_hi, o_lo = (
            sem(n) for n in ("po_step", "po_hi", "po_lo", "po_mm", "po_out", "po_table", "o_hi", "o_lo"))
        gate_done, z_done, sig_done, z_read, mix_step, me_hi, me_lo, y_kept = (
            sem(n) for n in ("gate_done", "z_done", "sig_done", "z_read", "mix_step", "me_hi", "me_lo", "y_kept"))
        relu_done, hid_hi, hid_sq, hid_lo, y_done, y_added = (
            sem(n) for n in ("relu_done", "hid_hi", "hid_sq", "hid_lo", "y_done", "y_added"))

        def pooling(layer, Ohi, Olo):
            chunks, t0 = wide(layer)
            w_in = a["w_in"][layer].rearrange("(k p) n -> p k n", p=P)
            grp = a["w_pool_grp"][layer].rearrange("g c d -> c g d")
            G, W2 = len(POOL_WINDOWS), T + 4 * ZPAD
            parts = [(o, q, n) for o, q, n in ((ZPAD, 0, CTX), (CTX + 3 * ZPAD, CTX, SEQ)) if q + n > t0]
            per_layer = 1 + sum(g + 4 for g in range(G))

            def step(g):
                return layer * per_layer + 1 + sum(q + 4 for q in range(g))

            ph = units.phase([0, 1, 2, 0, 1], [2, 3, 0, 1, 2])
            with ExitStack() as z:
                zp = sb(f"zp{layer}", [P, W2], F32, z)
                sums = [sb(f"sum{b}_{layer}", [P, W2], F32, z) for b in range(2)]
                inv = sb(f"inv{layer}", [P, T], F32, z)
                block = z.enter_context(nc.Block())

                @block.sync
                def _(sp):
                    for j in range(G):
                        sp.dma_start(slot_view(ph.raws[j]), w_in[:, :, j * P:(j + 1) * P]).then_inc(landed[ph.raws[j]], 16)
                    sp.wait_ge(lo_ready, ph.base + 1)
                    sp.dma_start(slot_view(ph.raws[G])[:, 0:G], grp).then_inc(landed[ph.raws[G]], 16)
                    for g in range(G):
                        if g:
                            sp.wait_ge(po_step, step(g) - 1)
                        sp.dma_start(inv[:], a["inv_count"][g:g + 1, :].broadcast_to([P, T])).then_inc(po_table, 16)

                @block.scalar
                def _(act):
                    for j in range(G + 1):
                        act.wait_ge(landed[ph.raws[j]], ph.landed(j, 0))
                        if j >= 3:
                            act.wait_ge(unit_used, ph.used0 + j - 2)
                        n = UNIT if j < G else G * P
                        dst = whi(ph.slots[j]).rearrange("p k n -> p (k n)")
                        nc.scalar.activation(dst[:, 0:n], raw[ph.raws[j]][:, 0:n], ACT.Copy).then_inc(hi_ready, 1)
                        for k in ((), (0, 1), (2, 3), (4, 5), (6, 7))[j]:
                            nc.scalar.activation(Ohi[:, 4 + k, t0:T], A[:, k, t0:T], ACT.Copy).then_inc(o_hi, 1)
                    for g in range(G):
                        act.wait_ge(po_step, step(g + 1))
                        nc.scalar.activation(Ohi[:, g, t0:T], A[:, 4 + g, t0:T], ACT.Copy).then_inc(po_hi, 1)
                    for g in range(G):
                        act.wait_ge(*((po_mm, layer * (G - 1) + g + 1) if g < G - 1 else (unit_used, ph.used0 + G + 1)))
                        nc.scalar.activation(grid(A[:, g], layer), pair(g, layer), ACT.Identity,
                                             scale=vec[:, R_PSC + g:R_PSC + g + 1]).then_inc(po_out, 1)
                        act.wait_ge(po_out, layer * G + g + 1)
                        nc.scalar.activation(Ohi[:, g, t0:T], A[:, g, t0:T], ACT.Copy).then_inc(po_hi, 1)

                @block.tensor
                def _(pe):
                    for g in range(G):
                        pe.wait_ge(lo_ready, ph.base + g + 1)
                        s = ph.slots[g]
                        for k in range(KT):
                            mm = three_terms(pair(g, layer), whi(s)[:, k], wlo(s)[:, k], Hhi[:, k], Hlo[:, k],
                                             chunks, k == 0, k == KT - 1)
                        mm.then_inc(unit_used, 1)
                    pe.wait_ge(lo_ready, ph.base + G + 1)
                    s = ph.slots[G]
                    for g in range(G):
                        pe.wait_ge(po_lo, layer * 2 * G + g + 1)
                        mm = three_terms(pair(g, layer), whi(s)[:, g], wlo(s)[:, g], Ohi[:, g], Olo[:, g],
                                         chunks, True, True)
                        mm.then_inc(po_mm if g < G - 1 else unit_used, 1)

                @block.vector
                def _(dve):
                    nc.vector.memset(zp[:], 0.0).then_inc(po_step, 1)
                    for j in range(G + 1):
                        dve.wait_ge(hi_ready, ph.index(j, 0) + 1)
                        n = UNIT if j < G else G * P
                        dst = wlo(ph.slots[j]).rearrange("p k n -> p (k n)")
                        hi = whi(ph.slots[j]).rearrange("p k n -> p (k n)").bitcast(F32)
                        nc.vector.tensor_tensor(dst[:, 0:n], raw[ph.raws[j]][:, 0:n], hi[:, 0:n], ALU.subtract
                                                ).then_inc(lo_ready, 1)
                        for k in ((), (0, 1), (2, 3), (4, 5), (6, 7))[j]:
                            dve.wait_ge(o_hi, 8 * layer + k + 1)
                            nc.vector.tensor_tensor(Olo[:, 4 + k, t0:T], A[:, k, t0:T],
                                                    Ohi[:, 4 + k, t0:T].bitcast(F32), ALU.subtract).then_inc(o_lo, 1)
                    for g in range(G):
                        n = step(g)
                        dve.wait_ge(po_step, n)
                        dve.wait_ge(unit_used, ph.used0 + g + 1)
                        for o, q, ln in parts:
                            for bank, c0, cn in chunks:
                                u, v = max(q, c0), min(q + ln, c0 + cn)
                                if u < v:
                                    ins = nc.vector.tensor_copy(zp[:, o + u - q:o + v - q],
                                                                pair(g, layer)[:, bank, u - c0:v - c0])
                        ins.then_inc(po_step, 1)
                        dve.wait_ge(po_step, n + 1)
                        src, left, right = zp, 0, 0
                        for m in range(g + 1):
                            back, ahead = (1, 0) if m == 0 else (2 ** (m - 1), 2 ** (m - 1))
                            left, right = left + back, right + ahead
                            nc.vector.tensor_tensor(sums[m % 2][:, left:W2 - right],
                                                    src[:, left - back:W2 - right - back],
                                                    src[:, left + ahead:W2 - right + ahead], ALU.add
                                                    ).then_inc(po_step, 1)
                            dve.wait_ge(po_step, n + 2 + m)
                            src = sums[m % 2]
                        mean = sums[(g + 1) % 2]
                        dve.wait_ge(po_table, 16 * (layer * G + g + 1))
                        for o, q, ln in parts:
                            ins = nc.vector.tensor_tensor(mean[:, o:o + ln], src[:, o:o + ln], inv[:, q:q + ln], ALU.mult)
                        ins.then_inc(po_step, 1)
                        dve.wait_ge(po_step, n + 3 + g)
                        dve.wait_ge(o_lo, 8 * layer + 8)
                        for o, q, ln in parts:
                            ins = nc.vector.tensor_tensor(A[:, 4 + g, q:q + ln], mean[:, o:o + ln], zp[:, o:o + ln],
                                                          ALU.subtract)
                        ins.then_inc(po_step, 1)
                        dve.wait_ge(po_hi, layer * 2 * G + g + 1)
                        nc.vector.tensor_tensor(Olo[:, g, t0:T], A[:, 4 + g, t0:T], Ohi[:, g, t0:T].bitcast(F32),
                                                ALU.subtract).then_inc(po_lo, 1)
                    for g in range(G):
                        dve.wait_ge(po_hi, layer * 2 * G + G + g + 1)
                        nc.vector.tensor_tensor(Olo[:, g, t0:T], A[:, g, t0:T], Ohi[:, g, t0:T].bitcast(F32),
                                                ALU.subtract).then_inc(po_lo, 1)

        def merge(layer, Ohi, Olo):
            chunks, t0 = wide(layer)
            w_in = a["w_in"][layer].rearrange("(k p) n -> p k n", p=P)
            w_out = [a[n][layer].rearrange("(k p) n -> p k n", p=P) for n in ("w_pool_out", "w_diff_out", "w_gqa_out")]
            w_o = a["w_o"][layer].rearrange("(k p) n -> p k n", p=P)
            HK = KT // 2
            pg = units.phase([0, 1, 2, 3, 0, 1, 2, 3, 0, 1], [3, 0, 1, 2, 3, 0, 1, 2, 3, 0], KT // 2,
                             [1, 1, 1, 2, 1] * 2)
            po = units.phase([0, 1, 2, 3] * 2, [3, 0, 1, 2] * 2)
            m0 = KT * layer

            with ExitStack() as z:
                fourth_slot(z, f"mix{layer}")
                sig = [sb(f"sig{b}_{layer}", [P, T], F32, z) for b in range(3)]
                block = z.enter_context(nc.Block())

                def pg_used(j, i):
                    return i * pg.B + (pg.used0 + j + 1)

                def A_tile(i, mm):
                    flat = A[:].rearrange("p k t -> p (k t)")
                    n = T - t0
                    ap = flat[:, bass.ds(i * (2 * T) + (mm * T + t0), n)]
                    return ap.rearrange("p (c w) -> p c w", c=len(chunks))

                @block.sync
                def _(sp):
                    with sp.Fori(0, KT // 2) as i:
                        for j in range(pg.B):
                            mm, u = j // 5, j % 5
                            v = slot_view(pg.raws[j])
                            if u < 3:
                                src = [(v, w_in, GATE_OFF + u * D + mm * P)]
                            elif u == 3:
                                src = [(v[:, 0:HK], w_out[0], mm * P), (v[:, HK:KT], w_out[1], mm * P)]
                            else:
                                src = [(v[:, 0:HK], w_out[2], mm * P)]
                            sp.wait_ge(lo_ready, pg.raw_free(j, i))
                            for dst, w, c in src:
                                off = (i * 2 + mm) * P + (c - mm * P) if u < 3 else (i * P + mm * (P // 2)) * 2
                                sp.dma_start(dst, w[:, :, bass.ds(off, P)]).then_inc(landed[pg.raws[j]], 16)
                    for j in range(KT):
                        sp.wait_ge(lo_ready, po.raw_free(j, 0))
                        sp.dma_start(slot_view(po.raws[j]), w_o[:, :, j * P:(j + 1) * P]).then_inc(landed[po.raws[j]], 16)

                @block.tensor
                def _(pe):
                    def branch(b, slot, half, u):
                        for k in range(HK):
                            mm_ = three_terms(pair(u, layer), whi(slot)[:, half * HK + k], wlo(slot)[:, half * HK + k],
                                              Ohi[:, 4 * b + k], Olo[:, 4 * b + k], chunks, k == 0, k == HK - 1)
                        return mm_

                    with pe.Fori(0, KT // 2) as i:
                        for j in range(pg.B):
                            mm, u = j // 5, j % 5
                            s = pg.slots[j]
                            pe.wait_ge(lo_ready, pg.index(j, i) + 1)
                            if u == 0:
                                pe.wait_ge(sig_done, i * 6 + (3 * m0 + 3 * mm))
                            elif u == 1:
                                pe.wait_ge(z_read, i * 6 + (3 * m0 + 3 * mm))
                            elif u == 3:
                                pe.wait_ge(sig_done, i * 6 + (3 * m0 + 3 * mm + 2))
                            if u < 3:
                                for k in range(KT):
                                    last = three_terms(pair(mm * 6 + u, layer), whi(s)[:, k], wlo(s)[:, k], Hhi[:, k],
                                                       Hlo[:, k], chunks, k == 0, k == KT - 1)
                                last.then_inc(unit_used, 1)
                            elif u == 3:
                                branch(0, s, 0, mm * 6 + 3).then_inc(z_done, 1)
                                branch(1, s, 1, mm * 6 + 4).then_inc(unit_used, 1)
                            else:
                                branch(2, s, 0, mm * 6 + 5).then_inc(unit_used, 1)
                    pe.wait_ge(z_read, 3 * (m0 + KT))
                    for j in range(KT):
                        s = po.slots[j]
                        pe.wait_ge(lo_ready, po.base + j + 1)
                        if j >= 4:
                            pe.wait_ge(y_kept, m0 + j - 3)
                        for k in range(KT):
                            if j == 0:
                                pe.wait_ge(me_lo, m0 + k + 1)
                            mm_ = three_terms(pair(j, layer), whi(s)[:, k], wlo(s)[:, k], Hhi[:, k], Hlo[:, k],
                                              chunks, k == 0, k == KT - 1)
                        mm_.then_inc(unit_used, 1)

                @block.scalar
                def _(act):
                    split_hi(act, pg, 0, 0, wait_slot=False)
                    with act.Fori(0, KT // 2) as i:
                        for j in range(pg.B):
                            mm, u = j // 5, j % 5
                            split_hi(act, pg, (j + 1) % pg.B, i + (j + 1) // pg.B if j + 1 == pg.B else i)
                            if u < 3:
                                act.wait_ge(unit_used, pg_used(j, i))
                                act.wait_ge(z_read, i * 6 + (3 * m0 + 3 * mm))
                                act.wait_ge(mix_step, i * 4 + (2 * m0 + 2 * mm))
                                nc.scalar.activation(grid(sig[u], layer), pair(mm * 6 + u, layer), ACT.Sigmoid
                                                     ).then_inc(sig_done, 1)
                    act.wait_ge(unit_used, po.used0)
                    for k in range(KT):
                        act.wait_ge(mix_step, 2 * (m0 + k + 1))
                        nc.scalar.activation(Hhi[:, k, t0:T], A[:, k, t0:T], ACT.Copy).then_inc(me_hi, 1)
                    for j in range(KT):
                        if j + 1 < KT:
                            split_hi(act, po, j + 1, 0)
                        act.wait_ge(unit_used, po.used0 + j + 1)
                        if j == 0:
                            act.wait_ge(me_lo, m0 + KT)
                        nc.scalar.activation(grid(A[:, j], layer), pair(j, layer), ACT.Copy).then_inc(y_kept, 1)

                @block.vector
                def _(dve):
                    split_lo(dve, pg, 0, 0)
                    with dve.Fori(0, KT // 2) as i:
                        for j in range(pg.B):
                            mm, u = j // 5, j % 5
                            split_lo(dve, pg, (j + 1) % pg.B, i + (j + 1) // pg.B if j + 1 == pg.B else i)
                            if u < 3:
                                continue
                            n3, n2 = i * 6 + (3 * m0 + 3 * mm), i * 4 + (2 * m0 + 2 * mm)
                            dst = A_tile(i, mm)
                            for b in ((0, 1) if u == 3 else (2,)):
                                src = pair(mm * 6 + 3 + b, layer)
                                if b == 0:
                                    dve.wait_ge(z_done, i * 2 + (m0 + mm + 1))
                                else:
                                    dve.wait_ge(unit_used, pg_used(j, i))
                                dve.wait_ge(sig_done, n3 + (b + 1))
                                g = grid(sig[b], layer)
                                nc.vector.tensor_tensor(dst if b == 0 else g, src, g, ALU.mult).then_inc(z_read, 1)
                                if b:
                                    dve.wait_ge(z_read, n3 + (b + 1))
                                    if b == 2:
                                        dve.wait_ge(mix_step, n2 + 1)
                                    nc.vector.tensor_tensor(dst, dst, g, ALU.add).then_inc(mix_step, 1)
                    for k in range(KT):
                        dve.wait_ge(me_hi, m0 + k + 1)
                        nc.vector.tensor_tensor(Hlo[:, k, t0:T], A[:, k, t0:T], Hhi[:, k, t0:T].bitcast(F32),
                                                ALU.subtract).then_inc(me_lo, 1)
                    for j in range(KT - 1):
                        split_lo(dve, po, j + 1, 0)

        def mlp(layer):
            chunks, t0 = wide(layer)
            w1 = a["w_ff1"][layer].rearrange("(k p) n -> p k n", p=P)
            w2 = a["w_ff2"][layer].rearrange("(r p) n -> p r n", p=P)
            MB = FB // P
            HK = MB
            ring = [0, 1, 2, 3]
            rr = [3, 0, 1, 2]
            pa = units.phase(ring, rr)
            pb = units.phase(ring * 4, rr * 4, NB // 2 - 1)
            pc = units.phase(ring * 3, rr * 3)
            h0, y0 = NB * MB * layer, (NB + 1) * KT * layer

            with ExitStack() as z:
                fourth_slot(z, f"mlp{layer}")
                hhi = [sb(f"hhi{b}_{layer}", [P, MB, T], F32R, z) for b in range(2)]
                hlo = [sb(f"hlo{b}_{layer}", [P, MB, T], F32R, z) for b in range(2)]
                rt = [sb(f"rt{b}_{layer}", [P, T], F32, z) for b in range(2)]
                h2 = sb(f"h2_{layer}", [P, T], F32, z)
                block = z.enter_context(nc.Block())

                def up(ph, j0, blk):
                    return [(ph, j0 + m, "up", blk, m) for m in range(MB)]

                def down(ph, j0, blk):
                    return [(ph, j0 + m, "down", blk, m) for m in range(KT // 2)]

                plan_a = up(pa, 0, (0, 0))
                plan_b = up(pb, 0, (2, 1)) + down(pb, 4, (2, 0)) + up(pb, 8, (2, 2)) + down(pb, 12, (2, 1))
                plan_c = up(pc, 0, (0, NB - 1)) + down(pc, 4, (0, NB - 2)) + down(pc, 8, (0, NB - 1))

                def run(eng, body):
                    body(0, plan_a, (pb, 0, 0))
                    with eng.Fori(0, NB // 2 - 1) as i:
                        body(i, plan_b, (pb, 0, 1))
                    body(0, plan_c, None)

                def at(i, lin):
                    return i * lin[0] + lin[1] if lin[0] else lin[1]

                def parity(blk):
                    return blk[1] % 2

                def pair_uses(plan):
                    n, got = 0, []
                    for _, _, kind, _, _ in plan:
                        got.append(n)
                        n += 1 if kind == "up" else 2
                    return got

                @block.sync
                def _(sp):
                    def body(i, plan, _):
                        for ph, j, kind, blk, m in plan:
                            s = ph.raws[j]
                            if kind == "up":
                                off, dst, src, n = at(i, (blk[0] * FB, blk[1] * FB + m * P)), slot_view(s), w1, P
                            else:
                                off, dst, src, n = at(i, (blk[0] * HK, blk[1] * HK)), slot_view(s, HK), w2, HK
                            sp.wait_ge(lo_ready, ph.raw_free(j, i))
                            src = src[:, :, bass.ds(off, P)] if kind == "up" else \
                                src[:, bass.ds(off, HK), m * 2 * P:(m + 1) * 2 * P]
                            sp.dma_start(dst, src).then_inc(landed[s], 16)
                    run(sp, body)

                @block.tensor
                def _(pe):
                    def body(i, plan, _):
                        for (ph, j, kind, blk, m), u in zip(plan, pair_uses(plan)):
                            s = ph.slots[j]
                            pe.wait_ge(lo_ready, ph.index(j, i) + 1)
                            if kind == "up":
                                if blk != (0, 0):
                                    pe.wait_ge(relu_done, at(i, (blk[0] * MB, h0 + (blk[1] - 1) * MB + m + 1)))
                                    pe.wait_ge(y_added, at(i, (blk[0] * KT, y0 + (blk[1] - 1) * KT + KT // 2 + m + 1)))
                                for k in range(KT):
                                    mm = three_terms(pair(u, layer), whi(s)[:, k], wlo(s)[:, k], Hhi[:, k], Hlo[:, k],
                                                     chunks, k == 0, k == KT - 1)
                                mm.then_inc(unit_used, 1)
                                continue
                            hh, hl = hhi[parity(blk)], hlo[parity(blk)]
                            if m == 0:
                                pe.wait_ge(hid_lo, at(i, (blk[0] * MB, h0 + (blk[1] + 1) * MB)))
                            w_h = whi(s).rearrange("p k n -> p (k n)").rearrange("p (k n) -> p k n", k=HK)
                            w_l = wlo(s).rearrange("p k n -> p (k n)").rearrange("p (k n) -> p k n", k=HK)
                            for q in range(2):
                                n = 2 * m + q
                                if m < 2 and blk != (0, NB - 1):
                                    pe.wait_ge(relu_done, at(i, (blk[0] * MB, h0 + (blk[1] + 1) * MB + n + 1)))
                                else:
                                    pe.wait_ge(y_added, at(i, (blk[0] * KT, y0 + (blk[1] + 1) * KT + n - 3)))
                                for k in range(HK):
                                    mm = three_terms(pair(u + q, layer), w_h[:, k, q * P:(q + 1) * P],
                                                     w_l[:, k, q * P:(q + 1) * P], hh[:, k], hl[:, k], chunks,
                                                     k == 0, k == HK - 1)
                                mm.then_inc(y_done if q == 0 else unit_used, 1)
                    run(pe, body)

                def prefetch(i, plan, n, follow):
                    if n + 1 < len(plan):
                        return plan[n + 1][0], plan[n + 1][1], i
                    if follow is None:
                        return None
                    ph, j, ahead = follow
                    return ph, j, i + 1 if ahead else 0

                @block.scalar
                def _(act):
                    def body(i, plan, follow):
                        for n, ((ph, j, kind, blk, m), u) in enumerate(zip(plan, pair_uses(plan))):
                            nxt = prefetch(i, plan, n, follow)
                            if nxt is not None:
                                split_hi(act, *nxt)
                            if kind == "down":
                                continue
                            h = at(i, (blk[0] * MB, h0 + blk[1] * MB + m))
                            r = rt[m % 2]
                            act.wait_ge(unit_used, i * ph.B + (ph.used0 + j + 1))
                            if m >= 2 or blk != (0, 0):
                                act.wait_ge(hid_sq, at(i, (blk[0] * MB, h0 + blk[1] * MB + m - 1)))
                            nc.scalar.activation(grid(r, layer), pair(u, layer), ACT.Relu).then_inc(relu_done, 1)
                            act.wait_ge(relu_done, h + 1)
                            nc.scalar.activation(hhi[parity(blk)][:, m, t0:T], r[:, t0:T], ACT.Square
                                                 ).then_inc(hid_hi, 1)
                    split_hi(act, pa, 0, 0)
                    run(act, body)

                @block.vector
                def _(dve):
                    def body(i, plan, follow):
                        for n, ((ph, j, kind, blk, m), u) in enumerate(zip(plan, pair_uses(plan))):
                            nxt = prefetch(i, plan, n, follow)
                            if nxt is not None:
                                split_lo(dve, *nxt)
                            if kind == "up":
                                r = rt[m % 2]
                                h = at(i, (blk[0] * MB, h0 + blk[1] * MB + m))
                                dve.wait_ge(relu_done, h + 1)
                                if m or blk != (0, 0):
                                    dve.wait_ge(hid_lo, h)
                                nc.vector.tensor_tensor(h2[:, t0:T], r[:, t0:T], r[:, t0:T], ALU.mult
                                                        ).then_inc(hid_sq, 1)
                                dve.wait_ge(hid_sq, h + 1)
                                dve.wait_ge(hid_hi, h + 1)
                                nc.vector.tensor_tensor(hlo[parity(blk)][:, m, t0:T], h2[:, t0:T],
                                                        hhi[parity(blk)][:, m, t0:T].bitcast(F32), ALU.subtract
                                                        ).then_inc(hid_lo, 1)
                                continue
                            for q in range(2):
                                k = 2 * m + q
                                if q == 0:
                                    dve.wait_ge(y_done, at(i, (blk[0] * KT // 2, y_done0 + blk[1] * (KT // 2) + m + 1)))
                                else:
                                    dve.wait_ge(unit_used, i * ph.B + (ph.used0 + j + 1))
                                dve.wait_ge(y_added, at(i, (blk[0] * KT, y0 + blk[1] * KT + k + 1)))
                                dst = grid(A[:, k], layer)
                                nc.vector.tensor_tensor(dst, pair(u + q, layer), dst, ALU.add).then_inc(y_added, 1)
                    y_done0 = NB * (KT // 2) * layer
                    split_lo(dve, pa, 0, 0)
                    for k in range(KT):
                        nc.vector.memset(A[:, k, t0:T], 0.0).then_inc(y_added, 1)
                    run(dve, body)

        for layer in range(DEPTH):
            tiles = range(NCH) if layer < DEPTH - 1 else range(CTX // CH, NCH)
            modulation(layer)
            norms(f"pre{layer}", range(NCH), A, preA, 0, spill=True)
            attention(layer)
            with ExitStack() as outs:
                Ohi = sb(f"Ohi{layer}", [P, 12, T], F32R, outs)
                Olo = sb(f"Olo{layer}", [P, 12, T], F32R, outs)
                pooling(layer, Ohi, Olo)
                merge(layer, Ohi, Olo)
            with ExitStack() as xs:
                B = sb(f"B{layer}", [P, KT, T], F32, xs)
                norms(f"mid{layer}", tiles, B, preF, 3 * KT, Y=A, post=postA, reload=True)
                mlp(layer)
                norms(f"end{layer}", tiles, B, Y=A, post=postF, X_out=A)

        with ExitStack() as z:
            rows = sb("out_rows", [P, SEQ // P, D], F32, z)
            out_turned, out_kept, out_left = sem("out_turned"), sem("out_kept"), sem("out_left")
            block = z.enter_context(nc.Block())

            @block.tensor
            def _(pe):
                for t in range(SEQ // P):
                    for h in range(2):
                        g = 2 * t + h
                        for k in range(4):
                            f = 4 * h + k
                            mm = nc.tensor.transpose(psum[:, g, k * P:(k + 1) * P],
                                                     A[:, f, CTX + t * P:CTX + (t + 1) * P], ident[:])
                        mm.then_inc(out_turned, 1)

            @block.vector
            def _(dve):
                for g in range(2 * SEQ // P):
                    dve.wait_ge(out_turned, g + 1)
                    nc.vector.tensor_copy(rows[:, g // 2, (g % 2) * 512:(g % 2 + 1) * 512], psum[:, g]
                                          ).then_inc(out_kept, 1)

            @block.sync
            def _(sp):
                dst = out.rearrange("b (t p) d -> p (b t) d", p=P)
                for t in range(SEQ // P):
                    sp.wait_ge(out_kept, 2 * t + 2)
                    sp.dma_start(dst[:, t], rows[:, t]).then_inc(out_left, 16)
                sp.wait_ge(out_left, 16 * (SEQ // P))


_INS = ["x", "c", "ctx", "c_ctx", "w_mod", "b_mod", "g_pre_mix", "g_post_mix", "g_pre_ffn", "g_post_ffn", "w_in",
        "w_pool_grp", "pool_scale", "lambda_q1", "lambda_k1", "lambda_q2", "lambda_k2", "diff_subln", "gqa_q_norm",
        "gqa_k_norm", "w_pool_out", "w_diff_out", "w_gqa_out", "w_o", "w_ff1", "w_ff2"]


def _constants():
    import numpy as np
    grid_w, pairs = 64, HD // 4
    row = np.repeat(np.arange(SEQ // grid_w), grid_w).astype(np.float32)
    col = np.tile(np.arange(grid_w), SEQ // grid_w).astype(np.float32)
    inv = (1.0 / (np.float32(10000.0) ** (np.arange(pairs, dtype=np.float32) * np.float32(2.0) / np.float32(HD // 2)))
           ).astype(np.float32)
    ang = np.concatenate([row[:, None] * inv, col[:, None] * inv], axis=-1).astype(np.float32)
    cos, sin = np.cos(ang), np.sin(ang)
    inv_count = np.zeros((len(POOL_WINDOWS), T), np.float32)
    for g, w in enumerate(POOL_WINDOWS):
        at = 0
        for n in (CTX, SEQ):
            t = np.arange(n)
            count = np.clip(t + w // 2, 0, n) - np.clip(t - w // 2, 0, n)
            inv_count[g, at:at + n] = 1.0 / count
            at += n
    return {"cos": np.repeat(cos, 2, axis=1).astype(np.float32),
            "sin": np.stack([-sin, sin], axis=-1).reshape(SEQ, HD).astype(np.float32),
            "inv_count": inv_count, "identity": np.eye(P, dtype=np.float32)}


def kernel(**inputs):
    import numpy as _np
    import concourse.bacc as _bacc
    from concourse import mybir as _mybir
    from concourse.bass_utils import run_bass_kernel_spmd as _run

    nc = _bacc.Bacc("TRN2", target_bir_lowering=False, num_devices=1)
    arrays, args = {}, {}
    data = {name: inputs[name] for name in _INS}
    data.update(_constants())
    for name, value in data.items():
        v = _np.ascontiguousarray(value)
        arrays[f"in_{name}"] = v
        args[name] = nc.dram_tensor(f"in_{name}", v.shape, _mybir.dt.from_np(v.dtype), kind="ExternalInput").ap()
    out = nc.dram_tensor("out_0", (1, SEQ, D), _mybir.dt.float32, kind="ExternalOutput").ap()
    build(nc, args, out)
    r = _run(nc, [arrays], core_ids=[0])
    return r.results[0]["out_0"]
```

```python
import math
from contextlib import ExitStack

import concourse.bass as bass
from concourse import mybir

F32 = mybir.dt.float32
F32R = mybir.dt.float32r
ALU = mybir.AluOpType
ACT = mybir.ActivationFunctionType
AX = mybir.AxisListType

P = 128
D = 1024
KT = D // P
SEQ, CTX = 512, 256
T = SEQ + CTX
TT = T // P
CTX_TILES = CTX // P
DEPTH = 2
HD = 64
SCALE = HD ** -0.5
EPS = 1e-6
POOL_WINDOWS = (2, 4, 8, 16)
POOL_W = DIFF_W = GQA_W = 512
DIFF_HEADS, GQA_HEADS, KV_HEADS = 4, 8, 2
GROUP = GQA_HEADS // KV_HEADS
GATE_OFF = POOL_W + DIFF_W + GQA_W
KV_OFF = GATE_OFF + 3 * D
DK_OFF, DV_OFF = KV_OFF, KV_OFF + DIFF_W
GK_OFF = KV_OFF + 2 * DIFF_W
GV_OFF = GK_OFF + KV_HEADS * HD
D_FF = 4 * D
FB = 512
NB = D_FF // FB
NPANEL = DIFF_HEADS + KV_HEADS
RING, RAW = 4, 4
UNIT = KT * P
CH = 256
NCH = T // CH
ZPAD = 8
R_C, R_CC, R_GPM, R_GQM, R_GPF, R_GQF = range(0, 48, 8)
R_BMOD, R_PSC, R_SUB, ROWS = 48, 96, 100, 101


def lambda_init(layer):
    return 0.8 - 0.6 * math.exp(-0.3 * layer)


class Units:

    def __init__(self):
        self.n = 0
        self.used = 0
        self.landed = [0] * RAW
        self.in_slot, self.in_raw = {}, {}

    def phase(self, slots, raws, iters=1, dmas=None):
        return Phase(self, slots, raws, iters, dmas or [1] * len(slots))


class Phase:

    def __init__(self, units, slots, raws, iters, dmas):
        self.slots, self.raws, self.B = slots, raws, len(slots)
        self.base, self.used0 = units.n, units.used
        self.land0 = list(units.landed)
        self.per = [sum(16 * d for r, d in zip(raws, dmas) if r == q) for q in range(RAW)]
        seen = [0] * RAW
        self.rank = []
        for r, d in zip(raws, dmas):
            seen[r] += 16 * d
            self.rank.append(seen[r])
        self.first_slot, self.first_raw = dict(units.in_slot), dict(units.in_raw)
        for j in range(self.B):
            units.in_slot[slots[j]] = units.used + self.B * (iters - 1) + j + 1
            units.in_raw[raws[j]] = units.n + self.B * (iters - 1) + j + 1
        self.iters = iters
        units.n += self.B * iters
        units.used += self.B * iters
        for q in range(RAW):
            units.landed[q] += self.per[q] * iters

    def landed(self, j, i):
        r = self.raws[j]
        return i * self.per[r] + (self.land0[r] + self.rank[j])

    def index(self, j, i):
        return i * self.B + (self.base + j)

    def _free(self, slots, first, base, j, i):
        earlier = [q for q in range(j) if slots[q] == slots[j]]
        if earlier:
            return i * self.B + (base + earlier[-1] + 1)
        if self.iters == 1:
            return first[slots[j]]
        return i * self.B + (base + 1 - self.B + max(q for q in range(self.B) if slots[q] == slots[j]))

    def raw_free(self, j, i):
        return self._free(self.raws, self.first_raw, self.base, j, i)

    def slot_free(self, j, i):
        return self._free(self.slots, self.first_slot, self.used0, j, i)


def build(nc, a, out):
    top = ExitStack()
    with top:
        def sb(name, shape, dt=F32, ctx=top):
            return ctx.enter_context(nc.sbuf_tensor(name, shape, dt))

        def sem(name):
            return top.enter_context(nc.semaphore(name))

        raw = [sb(f"raw{s}", [P, UNIT]) for s in range(RAW)]
        whi3 = sb("whi3", [P, 3, KT, P], F32R)
        wlo3 = sb("wlo3", [P, 3, KT, P], F32R)
        Hhi = sb("Hhi", [P, KT, T], F32R)
        Hlo = sb("Hlo", [P, KT, T], F32R)
        A = sb("A", [P, KT, T])
        ident = sb("ident", [P, P])
        ones = sb("ones", [P, P])
        cosT = sb("cosT", [P, SEQ // P, HD])
        sinT = sb("sinT", [P, SEQ // P, HD])
        vec = sb("vec", [P, ROWS])
        mod = sb("mod", [P, 6 * KT, 2])
        csil = sb("csil", [P, KT, 2])
        preA = sb("preA", [P, KT, 2])
        postA = sb("postA", [P, KT, 2])
        preF = sb("preF", [P, KT, 2])
        postF = sb("postF", [P, KT, 2])
        headG = sb("headG", [P, GROUP + 1, HD])
        subg = sb("subg", [P, 1])
        lams = sb("lams", [P, 2])
        lame = sb("lame", [P, 2])
        lam = sb("lam", [P, 1])
        mhalf = sb("mhalf", [P, 8])
        xdram = nc.dram_tensor("x_spill", [P, KT * T], F32, kind="Internal").ap()

        psum = top.enter_context(nc.psum_tensor("psum", [P, 8, 512], F32))

        landed = [sem(f"landed{s}") for s in range(RAW)]
        hi_ready, lo_ready, unit_used = sem("hi_ready"), sem("lo_ready"), sem("unit_used")
        setup_in, setup_step, setup_pool = sem("setup_in"), sem("setup_step"), sem("setup_pool")
        units = Units()

        def whi(j):
            return whi3[:, j] if j < 3 else whi_x[0][:]

        def wlo(j):
            return wlo3[:, j] if j < 3 else wlo_x[0][:]

        whi_x, wlo_x = [None], [None]

        def fourth_slot(ctx, tag):
            whi_x[0] = sb(f"whi_{tag}", [P, KT, P], F32R, ctx)
            wlo_x[0] = sb(f"wlo_{tag}", [P, KT, P], F32R, ctx)

        def split_hi(act, ph, j, i, wait_slot=True):
            act.wait_ge(landed[ph.raws[j]], ph.landed(j, i))
            if wait_slot:
                act.wait_ge(unit_used, ph.slot_free(j, i))
            dst = whi(ph.slots[j]).rearrange("p k n -> p (k n)")
            nc.scalar.activation(dst, raw[ph.raws[j]][:], ACT.Copy).then_inc(hi_ready, 1)

        def split_lo(dve, ph, j, i):
            dve.wait_ge(hi_ready, ph.index(j, i) + 1)
            dst = wlo(ph.slots[j]).rearrange("p k n -> p (k n)")
            hi = whi(ph.slots[j]).rearrange("p k n -> p (k n)").bitcast(F32)
            nc.vector.tensor_tensor(dst, raw[ph.raws[j]][:], hi, ALU.subtract).then_inc(lo_ready, 1)

        def load_unit(sp, ph, j, i, pieces):
            sp.wait_ge(lo_ready, ph.raw_free(j, i))
            for dst, src in pieces:
                sp.dma_start(dst, src).then_inc(landed[ph.raws[j]], 16)

        def slot_view(s, k=KT):
            return raw[s][:].rearrange("p (k n) -> p k n", k=k)

        def three_terms(out_ap, w_h, w_l, x_h, x_l, chunks, first, last):
            mm = None
            for n, (w, x) in enumerate(((w_h, x_h), (w_h, x_l), (w_l, x_h))):
                for bank, c0, cn in chunks:
                    mm = nc.tensor.matmul(out_ap[:, bank, 0:cn], w, x[:, c0:c0 + cn],
                                          start=first and n == 0, stop=last and n == 2)
            return mm

        n_sq, n_acc, n_ss, n_var, n_pow, n_diag, n_bc, n_sc, n_x, n_aff, n_hi, n_lo = (
            sem(n) for n in ("n_sq", "n_acc", "n_ss", "n_var", "n_pow", "n_diag", "n_bc", "n_sc", "n_x", "n_aff",
                             "n_hi", "n_lo"))
        n_spill, n_reload = sem("n_spill"), sem("n_reload")
        count = {"r": 0, "x": 0, "h": 0, "spill": 0, "reload": 0}
        NSUM, NBC = 3, 4

        def cols(c):
            return slice(c * CH, (c + 1) * CH)

        def stream(c):
            return 1 if c * CH < CTX else 0

        class Norms:

            def __init__(s, ctx, tag, passes, X, gains=None, shift_at=0, Y=None, post=None, X_out=None):
                s.passes, s.X, s.gains, s.shift_at, s.Y, s.post = passes, X, gains, shift_at, Y, post
                s.X_out = X if X_out is None else X_out
                s.reloaded = None
                s.sq = sb(f"sq_{tag}", [P, KT, CH], F32, ctx)
                s.t1 = sb(f"t1_{tag}", [P, KT, CH], F32, ctx)
                s.t2 = sb(f"t2_{tag}", [P, KT, CH], F32, ctx) if gains is not None else None
                s.acc = sb(f"acc_{tag}", [P, CH], F32, ctx)
                s.var = sb(f"var_{tag}", [P, len(passes), 2], F32, ctx)
                s.rstd = sb(f"rstd_{tag}", [P, len(passes), 2], F32, ctx)
                s.diag = sb(f"diag_{tag}", [P, 2, P], F32, ctx)
                s.r0, s.x0, s.h0 = count["r"], count["x"], count["h"]
                s.nx = [s.x0 + sum(w == "Y" for w, _ in passes[:n]) for n in range(len(passes) + 1)]
                s.nh = [s.h0 + sum(w == "x" for w, _ in passes[:n]) for n in range(len(passes) + 1)]
                count["r"] += len(passes)
                count["x"], count["h"] = s.nx[-1], s.nh[-1]

            def src(s, n):
                return s.Y if s.passes[n][0] == "Y" else s.X_out

            def updated(s, c):
                return s.nx[s.passes.index(("Y", c))] + 1

            def act_square(s, act, n, ready=None):
                what, c = s.passes[n]
                if ready is not None:
                    act.wait_ge(*ready)
                elif what == "x" and s.Y is not None:
                    act.wait_ge(n_x, s.updated(c))
                if n:
                    act.wait_ge(n_acc, s.r0 + n)
                nc.scalar.activation(s.sq[:], s.src(n)[:, :, cols(c)], ACT.Square).then_inc(n_sq, 1)

            def dve_square(s, dve, n):
                dve.wait_ge(n_sq, s.r0 + n + 1)
                if n:
                    dve.wait_ge(n_ss, s.r0 + n)
                nc.vector.tensor_reduce(s.acc[:], s.sq[:].rearrange("p k t -> p t k"), AX.X, ALU.add
                                        ).then_inc(n_acc, 1)

            def pe_root(s, pe, n):
                pe.wait_ge(n_acc, s.r0 + n + 1)
                if n:
                    pe.wait_ge(n_var, s.r0 + n)
                for t in range(2):
                    mm = nc.tensor.matmul(psum[:, NSUM, 2 * t:2 * t + 2], s.acc[:, t * P:(t + 1) * P],
                                          ones[:, 0:2], start=True, stop=True)
                mm.then_inc(n_ss, 1)

            def dve_root(s, dve, n):
                dve.wait_ge(n_ss, s.r0 + n + 1)
                nc.vector.tensor_scalar(s.var[:, n], psum[:, NSUM, 0:4].rearrange("p (t o) -> p t o", o=2)[:, :, 0],
                                        1.0 / D, EPS, ALU.mult, ALU.add).then_inc(n_var, 1)

            def pool_root(s, pool, n):
                pool.wait_ge(n_var, s.r0 + n + 1)
                nc.gpsimd.tensor_tensor(s.rstd[:, n], s.var[:, n], mhalf[:, 0:2], ALU.pow).then_inc(n_pow, 1)

            def dve_spread(s, dve, n):
                dve.wait_ge(n_pow, s.r0 + n + 1)
                if n:
                    dve.wait_ge(n_bc, s.r0 + n)
                for t in range(2):
                    dg = nc.vector.tensor_scalar(s.diag[:, t], ident[:], s.rstd[:, n, t:t + 1], None, ALU.mult)
                dg.then_inc(n_diag, 1)

            def pe_spread(s, pe, n):
                pe.wait_ge(n_diag, s.r0 + n + 1)
                if n:
                    pe.wait_ge(n_sc, s.r0 + n)
                nc.tensor.matmul(psum[:, NBC, 0:CH], ones[:], s.diag[:].rearrange("p t n -> p (t n)"),
                                 start=True, stop=True).then_inc(n_bc, 1)

            def dve_apply(s, dve, n):
                what, c = s.passes[n]
                dve.wait_ge(n_bc, s.r0 + n + 1)
                if n:
                    dve.wait_ge(*((n_aff, s.nh[n]) if s.passes[n - 1][0] == "x" else (n_x, s.nx[n])))
                nc.vector.tensor_tensor(s.t1[:], s.src(n)[:, :, cols(c)],
                                        psum[:, NBC, 0:CH].rearrange("p (o t) -> p o t", o=1)
                                        .broadcast_to([P, KT, CH]), ALU.mult).then_inc(n_sc, 1)
                if what == "Y":
                    st_ = stream(c)
                    dve.wait_ge(n_sc, s.r0 + n + 1)
                    if n == 0 and s.reloaded is not None:
                        dve.wait_ge(*s.reloaded)
                    for k in range(KT):
                        up = nc.vector.scalar_tensor_tensor(s.X_out[:, k, cols(c)], s.t1[:, k],
                                                            s.post[:, k, st_:st_ + 1], s.X[:, k, cols(c)], ALU.mult,
                                                            ALU.add)
                    up.then_inc(n_x, 1)

            def dve_split(s, dve, n):
                what, c = s.passes[n]
                if what == "x":
                    dve.wait_ge(n_hi, s.nh[n] + 1)
                    nc.vector.tensor_tensor(Hlo[:, :, cols(c)], s.t2[:], Hhi[:, :, cols(c)].bitcast(F32),
                                            ALU.subtract).then_inc(n_lo, 1)

            def act_apply(s, act, n):
                what, c = s.passes[n]
                if what != "x":
                    return
                h, st_ = s.nh[n], stream(c)
                act.wait_ge(n_sc, s.r0 + n + 1)
                if h > s.h0:
                    act.wait_ge(n_lo, h)
                for k in range(KT):
                    aff = nc.scalar.activation(s.t2[:, k], s.t1[:, k], ACT.Identity,
                                               bias=mod[:, s.shift_at + k, st_:st_ + 1],
                                               scale=s.gains[:, k, st_:st_ + 1])
                aff.then_inc(n_aff, 1)
                act.wait_ge(n_aff, h + 1)
                nc.scalar.activation(Hhi[:, :, cols(c)], s.t2[:], ACT.Copy).then_inc(n_hi, 1)

        def norm_steps(nm, block, ph_next):
            N = len(nm.passes)

            @block.scalar
            def _(act):
                nm.act_square(act, 0)
                for n in range(N):
                    if n + 1 < N:
                        nm.act_square(act, n + 1)
                    nm.act_apply(act, n)
                    if n >= N - 3:
                        split_hi(act, ph_next, n - (N - 3), 0, wait_slot=False)

            @block.vector
            def _(dve):
                nm.dve_square(dve, 0)
                nm.dve_root(dve, 0)
                for n in range(N):
                    if n + 1 < N:
                        nm.dve_square(dve, n + 1)
                    nm.dve_spread(dve, n)
                    nm.dve_apply(dve, n)
                    if n + 1 < N:
                        nm.dve_root(dve, n + 1)
                    if n >= N - 3:
                        split_lo(dve, ph_next, n - (N - 3), 0)
                    nm.dve_split(dve, n)

            @block.gpsimd
            def _(pool):
                for n in range(N):
                    nm.pool_root(pool, n)

            @block.tensor
            def _(pe):
                nm.pe_root(pe, 0)
                for n in range(N):
                    nm.pe_spread(pe, n)
                    if n + 1 < N:
                        nm.pe_root(pe, n + 1)

        def w_in_of(layer):
            return a["w_in"][layer].rearrange("(k p) n -> p k n", p=P)

        def attention_phase(layer):
            ph = units.phase([0, 1, 2] * NPANEL, [n % RAW for n in range(3 * NPANEL)], 1,
                             [1, 1, 1] * DIFF_HEADS + [1, 1, 2] * KV_HEADS)
            units.used -= 3 * NPANEL
            units.in_slot = {s: units.used for s in range(RING)}
            return ph

        def load_attention(sp, ph, layer, n):
            w_in, v = w_in_of(layer), slot_view(ph.raws[n])
            p, m = n // 3, n % 3
            if p < DIFF_HEADS:
                c = (POOL_W, DK_OFF, DV_OFF)[m] + p * 2 * HD
                pieces = [(v, w_in[:, :, c:c + P])]
            elif m < 2:
                c = POOL_W + DIFF_W + (p - DIFF_HEADS) * GROUP * HD + m * P
                pieces = [(v, w_in[:, :, c:c + P])]
            else:
                ck, cv = GK_OFF + (p - DIFF_HEADS) * HD, GV_OFF + (p - DIFF_HEADS) * HD
                pieces = [(v[:, :, 0:HD], w_in[:, :, ck:ck + HD]), (v[:, :, HD:P], w_in[:, :, cv:cv + HD])]
            for dst, src in pieces:
                sp.dma_start(dst, src).then_inc(landed[ph.raws[n]], 16)

        def pooling_phase():
            return units.phase([0, 1, 2, 0, 1], [2, 3, 0, 1, 2])

        def load_pooling(sp, ph, layer, j):
            G = len(POOL_WINDOWS)
            if j < G:
                sp.dma_start(slot_view(ph.raws[j]), w_in_of(layer)[:, :, j * P:(j + 1) * P]
                             ).then_inc(landed[ph.raws[j]], 16)
            else:
                sp.dma_start(slot_view(ph.raws[j])[:, 0:G], a["w_pool_grp"][layer].rearrange("g c d -> c g d")
                             ).then_inc(landed[ph.raws[j]], 16)

        def merge_phase():
            return units.phase([0, 1, 2, 3, 0, 1, 2, 3, 0, 1], [3, 0, 1, 2, 3, 0, 1, 2, 3, 0], KT // 2,
                               [1, 1, 1, 2, 1] * 2)

        def load_merge(sp, ph, layer, j, i, ahead=0):
            w_in, HK = w_in_of(layer), KT // 2
            w_out = [a[n][layer].rearrange("(k p) n -> p k n", p=P) for n in ("w_pool_out", "w_diff_out", "w_gqa_out")]
            mm, u = j // 5 + 2 * ahead, j % 5
            v = slot_view(ph.raws[j])
            if u < 3:
                pieces = [(v, w_in, GATE_OFF + u * D)]
            elif u == 3:
                pieces = [(v[:, 0:HK], w_out[0], 0), (v[:, HK:KT], w_out[1], 0)]
            else:
                pieces = [(v[:, 0:HK], w_out[2], 0)]
            for dst, w, c in pieces:
                off = (i * 2 + mm) * P + c if u < 3 else (i * P + mm * (P // 2)) * 2
                src = w[:, :, off:off + P] if isinstance(off, int) else w[:, :, bass.ds(off, P)]
                sp.dma_start(dst, src).then_inc(landed[ph.raws[j]], 16)

        def mlp_phase():
            return units.phase([0, 1, 2, 3], [3, 0, 1, 2])

        def load_first_hidden(sp, ph, layer, j):
            sp.dma_start(slot_view(ph.raws[j]), a["w_ff1"][layer].rearrange("(k p) n -> p k n", p=P)
                         [:, :, j * P:(j + 1) * P]).then_inc(landed[ph.raws[j]], 16)

        MU, MS = 12, 2
        MOUT = 2
        XBANK = 5
        m_in, m_vec, m_loaded = sem("m_in"), sem("m_vec"), [sem(f"m_loaded{s}") for s in range(MS)]
        m_turned, m_step, m_sig, m_exp = sem("m_turned"), sem("m_step"), sem("m_sig"), sem("m_exp")
        m_rows, m_placed = sem("m_rows"), sem("m_placed")
        ident_in, x_in, x_turned, x_kept = sem("ident_in"), [sem("ctx_in"), sem("x_in")], sem("x_turned"), sem("x_kept")

        def modulation(layer, ph, B=None):
            NX = NCH
            ys = [("Y", c) for c in range(NCH)] if layer else []
            y = len(ys)
            if layer:
                order = [("square", 0), ("unit", 0), ("root", 0), ("square", 1), ("spread", 0), ("apply", 0),
                         ("unit", 1), ("root", 1), ("square", 2), ("spread", 1), ("apply", 1),
                         ("unit", 2), ("root", 2), ("square", 3), ("spread", 2), ("apply", 2),
                         ("unit", 3), ("root", 3), ("square", 4), ("unit", 4), ("root", 4), ("square", 5),
                         ("gains", 0)]
            else:
                order = [("turn", 0), ("unit", 0), ("turn", 1), ("square", 0), ("unit", 1), ("root", 0),
                         ("square", 1), ("unit", 2), ("root", 1), ("square", 2), ("unit", 3),
                         ("unit", 4), ("gains", 0)]
            order += [("spread", y), ("apply", y), ("root", y + 2), ("unit", 5), ("split", y),
                      ("spread", y + 1), ("apply", y + 1), ("unit", 6), ("split", y + 1),
                      ("spread", y + 2), ("apply", y + 2), ("unit", 7), ("split", y + 2)]
            order += [("unit", u) for u in range(8, MU)] + [("stored", 0), ("gains", 1), ("weights", 0)]

            with ExitStack() as z:
                rows = sb(f"rows{layer}", [P, P], F32, z)
                lamv = sb(f"lamv{layer}", [P, 4, HD], F32, z)
                lamp = sb(f"lamp{layer}", [P, 2, HD], F32, z)
                sg = sb(f"sg{layer}", [P, 2 * KT], F32, z)
                wm = [sb(f"wm{layer}_{s}", [P, KT, 512], F32, z) for s in range(MS)]
                mrow = [sb(f"mrow{layer}_{b}", [2, 512], F32, z) for b in range(2)]
                xt = None if layer else sb("x_rows", [P, TT, D], F32, z)
                nm = Norms(z, f"pre{layer}", ys + [("x", c) for c in range(NX)], A if B is None else B, preA, 0,
                           Y=A if ys else None, post=postF, X_out=A)
                sp0 = count["spill"]
                count["spill"] += 16
                block = z.enter_context(nc.Block())
                lin = 16 * 9 * (layer + 1)
                l0 = MU // MS * 16 * layer
                used0 = units.used - MU
                NSTEP = 12

                @block.sync
                def _(sp):
                    if layer == 0:
                        sp.dma_start(ident[:], a["identity"]).then_inc(ident_in, 16)
                    for r, src in ((R_C, a["c"].rearrange("b (k p) -> (b k) p", p=P)),
                                   (R_CC, a["c_ctx"].rearrange("(k p) -> k p", p=P)),
                                   (R_GPM, a["g_pre_mix"][layer].rearrange("(k p) -> k p", p=P)),
                                   (R_GQM, a["g_post_mix"][layer].rearrange("(k p) -> k p", p=P)),
                                   (R_GPF, a["g_pre_ffn"][layer].rearrange("(k p) -> k p", p=P)),
                                   (R_GQF, a["g_post_ffn"][layer].rearrange("(k p) -> k p", p=P)),
                                   (R_BMOD, a["b_mod"][layer].rearrange("(k p) -> k p", p=P)),
                                   (R_PSC, a["pool_scale"][layer].rearrange("(k p) -> k p", p=P)),
                                   (R_SUB, a["diff_subln"][layer].rearrange("(k p) -> k p", p=P))):
                        sp.dma_start(rows[r:r + src.shape[0], :], src).then_inc(m_vec, 16)
                    if layer == 0:
                        sp.dma_start(xt[:, 0:CTX_TILES], a["ctx"].rearrange("b (t p) d -> p (b t) d", p=P)
                                     ).then_inc(x_in[0], 16)
                    src = a["w_mod"][layer].rearrange("(k p) n -> p k n", p=P)
                    for u in range(MU):
                        if u >= MS:
                            sp.wait_ge(unit_used, used0 + u + 1 - MS)
                        sp.dma_start(wm[u % MS][:], src[:, :, u * 512:(u + 1) * 512]).then_inc(m_loaded[u % MS], 16)
                        if layer == 0 and u == 0:
                            sp.dma_start(xt[:, CTX_TILES:TT], a["x"].rearrange("b (t p) d -> p (b t) d", p=P)
                                         ).then_inc(x_in[1], 16)
                    for n in range(RAW):
                        load_attention(sp, ph, layer, n)
                    if layer == 0:
                        sp.dma_start(cosT[:], a["cos"].rearrange("(t p) d -> p t d", p=P)).then_inc(setup_in, 16)
                        sp.dma_start(sinT[:], a["sin"].rearrange("(t p) d -> p t d", p=P)).then_inc(setup_in, 16)
                        sp.wait_ge(setup_in, 32)

                @block.gpsimd
                def _(pool):
                    if layer == 0:
                        nc.gpsimd.memset(ones[:], 1.0).then_inc(setup_pool, 1)
                        nc.gpsimd.memset(mhalf[:], -0.5).then_inc(setup_pool, 1)
                        pool.wait_ge(setup_pool, 2)
                    for g in range(GROUP + 1):
                        g_dram = a["gqa_q_norm" if g < GROUP else "gqa_k_norm"][layer]
                        pool.dma_start(headG[:, g, :], g_dram.rearrange("(o d) -> o d", o=1).broadcast_to([P, HD])
                                       ).then_inc(m_in, 16)
                    for n, name in enumerate(("lambda_q1", "lambda_k1", "lambda_q2", "lambda_k2")):
                        pool.dma_start(lamv[:, n, :], a[name][layer].rearrange("(o d) -> o d", o=1)
                                       .broadcast_to([P, HD])).then_inc(m_in, 16)
                    for step, n in order:
                        if step == "root":
                            nm.pool_root(pool, n)
                        elif step == "stored":
                            pool.wait_ge(*((n_x, nm.nx[-1]) if layer else (x_kept, 2 * TT)))
                            pool.dma_start(xdram, A[:].rearrange("p k t -> p (k t)")).then_inc(n_spill, 16)
                    pool.wait_ge(n_spill, sp0 + 16)

                @block.scalar
                def _(act):
                    act.wait_ge(m_step, NSTEP * layer + 1)
                    nc.scalar.activation(sg[:], vec[:, 0:2 * KT], ACT.Sigmoid).then_inc(m_sig, 1)
                    act.wait_ge(m_step, NSTEP * layer + 4)
                    nc.scalar.activation(lame[:], lams[:], ACT.Exp).then_inc(m_exp, 1)
                    for step, n in order:
                        if step == "square":
                            nm.act_square(act, n, None if layer else (x_kept, 4 * (n + 1)))
                        elif step == "gains" and n == 0:
                            act.wait_ge(m_step, NSTEP * layer + 8)
                        elif step == "apply":
                            nm.act_apply(act, n)
                        elif step == "weights":
                            for j in range(3):
                                split_hi(act, ph, j, 0, wait_slot=False)

                @block.tensor
                def _(pe):
                    if layer == 0:
                        pe.wait_ge(ident_in, 16)
                        pe.wait_ge(setup_pool, 2)
                    pe.wait_ge(m_vec, 16 * 9 * (layer + 1))
                    nc.tensor.transpose(psum[:, MOUT, 0:ROWS], rows[0:ROWS, :], ident[0:ROWS, 0:ROWS]).then_inc(m_turned, 1)
                    def turn(part):
                        pe.wait_ge(x_in[part], 16)
                        for g in range(2 * CTX_TILES, 2 * TT) if part else range(2 * CTX_TILES):
                            t, h = g // 2, g % 2
                            if g >= 3:
                                pe.wait_ge(x_kept, g - 2)
                            for k in range(4):
                                f = 4 * h + k
                                mm = nc.tensor.transpose(psum[:, XBANK + g % 3, k * P:(k + 1) * P],
                                                         xt[:, t, f * P:(f + 1) * P], ident[:])
                            mm.then_inc(x_turned, 1)
                    pe.wait_ge(m_step, NSTEP * layer + 2)

                    def place(u):
                        pe.wait_ge(m_rows, MU * layer + u + 1)
                        if u == 4:
                            pe.wait_ge(m_step, NSTEP * layer + 7)
                        for q in range(4):
                            mm = nc.tensor.transpose(psum[:, MOUT, u * 8 + q * 2:u * 8 + q * 2 + 2],
                                                     mrow[u % 2][:, q * P:(q + 1) * P], ident[0:2, 0:2])
                        mm.then_inc(m_placed, 1)

                    for step, n in order:
                        if step == "turn":
                            turn(n)
                        elif step == "root":
                            nm.pe_root(pe, n)
                        elif step == "spread":
                            nm.pe_spread(pe, n)
                        elif step == "unit":
                            pe.wait_ge(m_loaded[n % MS], l0 + 16 * (n // MS + 1))
                            for k in range(KT):
                                mm = nc.tensor.matmul(psum[0:2, n % 2, :], csil[:, k, :], wm[n % MS][:, k, :],
                                                      start=k == 0, stop=k == KT - 1)
                            mm.then_inc(unit_used, 1)
                            if n:
                                place(n - 1)
                        elif step == "gains" and n == 1:
                            place(MU - 1)

                @block.vector
                def _(dve):
                    s0 = NSTEP * layer
                    dve.wait_ge(m_turned, layer + 1)
                    nc.vector.tensor_copy(vec[:], psum[:, MOUT, 0:ROWS]).then_inc(m_step, 1)
                    dve.wait_ge(m_sig, layer + 1)
                    nc.vector.tensor_tensor(csil[:].rearrange("p k s -> p s k"),
                                            vec[:, 0:2 * KT].rearrange("p (s k) -> p s k", s=2),
                                            sg[:].rearrange("p (s k) -> p s k", s=2), ALU.mult).then_inc(m_step, 1)
                    dve.wait_ge(m_in, lin)
                    nc.vector.tensor_tensor(lamp[:], lamv[:].rearrange("p (n q) d -> p q n d", q=2)[:, 0],
                                            lamv[:].rearrange("p (n q) d -> p q n d", q=2)[:, 1],
                                            ALU.mult).then_inc(m_step, 1)
                    dve.wait_ge(m_step, s0 + 3)
                    nc.vector.tensor_reduce(lams[:], lamp[:], AX.X, ALU.add).then_inc(m_step, 1)
                    dve.wait_ge(m_exp, layer + 1)
                    nc.vector.scalar_tensor_tensor(lam[:], lame[:, 0:1], lambda_init(layer), lame[:, 1:2],
                                                   ALU.add, ALU.subtract).then_inc(m_step, 1)
                    nc.vector.tensor_scalar(subg[:], vec[:, R_SUB:R_SUB + 1], 1.0 - lambda_init(layer), None,
                                            ALU.mult).then_inc(m_step, 1)
                    def keep_turned(part):
                        for g in range(2 * CTX_TILES, 2 * TT) if part else range(2 * CTX_TILES):
                            t, h = g // 2, g % 2
                            dve.wait_ge(x_turned, g + 1)
                            nc.vector.tensor_copy(A[:, 4 * h:4 * h + 4, t * P:(t + 1) * P],
                                                  psum[:, XBANK + g % 3].rearrange("p (k n) -> p k n", k=4)
                                                  ).then_inc(x_kept, 1)

                    def gain(r):
                        return vec[:, r:r + KT].rearrange("p (k o) -> p k o", o=1).broadcast_to([P, KT, 2])

                    def add_bias(k0, k1):
                        nc.vector.tensor_tensor(mod[:, k0:k1], psum[:, MOUT, 2 * k0:2 * k1]
                                                .rearrange("p (k s) -> p k s", s=2),
                                                vec[:, R_BMOD + k0:R_BMOD + k1].rearrange("p (k o) -> p k o", o=1)
                                                .broadcast_to([P, k1 - k0, 2]), ALU.add).then_inc(m_step, 1)

                    for step, n in order:
                        if step == "turn":
                            keep_turned(n)
                        elif step == "square":
                            nm.dve_square(dve, n)
                        elif step == "root":
                            nm.dve_root(dve, n)
                        elif step == "spread":
                            nm.dve_spread(dve, n)
                        elif step == "apply":
                            nm.dve_apply(dve, n)
                        elif step == "split":
                            nm.dve_split(dve, n)
                        elif step == "unit":
                            dve.wait_ge(unit_used, used0 + n + 1)
                            nc.vector.tensor_copy(mrow[n % 2][:], psum[0:2, n % 2, :]).then_inc(m_rows, 1)
                        elif step == "gains" and n == 0:
                            dve.wait_ge(m_placed, MU * layer + 4)
                            add_bias(0, 2 * KT)
                            dve.wait_ge(m_step, s0 + 7)
                            nc.vector.scalar_tensor_tensor(preA[:], mod[:, KT:2 * KT], 1.0, gain(R_GPM), ALU.add,
                                                           ALU.mult).then_inc(m_step, 1)
                        elif step == "gains":
                            dve.wait_ge(m_placed, MU * (layer + 1))
                            add_bias(2 * KT, 6 * KT)
                            dve.wait_ge(m_step, s0 + 9)
                            nc.vector.tensor_tensor(postA[:], mod[:, 2 * KT:3 * KT], gain(R_GQM), ALU.mult
                                                    ).then_inc(m_step, 1)
                            nc.vector.scalar_tensor_tensor(preF[:], mod[:, 4 * KT:5 * KT], 1.0, gain(R_GPF),
                                                           ALU.add, ALU.mult).then_inc(m_step, 1)
                            nc.vector.tensor_tensor(postF[:], mod[:, 5 * KT:6 * KT], gain(R_GQF), ALU.mult
                                                    ).then_inc(m_step, 1)
                        elif step == "weights":
                            for j in range(3):
                                split_lo(dve, ph, j, 0)

        GEMM, SBANK, TR, NTR, OB = 0, 1, 5, 2, 7

        def attention(layer, ph, ph_next):
            q_tiles = range(TT) if layer < DEPTH - 1 else range(CTX_TILES, TT)
            def sm(n):
                return sem(f"{n}_{layer}")

            gemm_done, act_read, dve_read = sm("gemm_done"), sm("act_read"), sm("dve_read")
            sq_done, head_var, head_pow = sm("sq_done"), sm("head_var"), sm("head_pow")
            normed, roped, stack_hi, stack_lo, stacks_in = sm("normed"), sm("roped"), sm("stack_hi"), sm("stack_lo"), sm("stacks_in")
            scores, negmax, exped, probs = sm("scores"), sm("negmax"), sm("exped"), sm("probs")
            turned, pt_hi, pt_lo, pv_done = sm("turned"), sm("pt_hi"), sm("pt_lo"), sm("pv_done")
            o_read, o_sq, o_var, o_pow, o_norm, o_out = (sm("o_read"), sm("o_sq"), sm("o_var"), sm("o_pow"),
                                                         sm("o_norm"), sm("o_out"))
            dchain = sm("dchain")

            class Prep:

                def __init__(s, g):
                    s.g, s.p, s.t = g, g // TT, g % TT
                    s.diff = s.p < DIFF_HEADS
                    s.q = s.t in q_tiles
                    s.nq = 2 if s.diff else GROUP
                    s.nk = 2 if s.diff else 1
                    s.vd = 2 * HD if s.diff else HD
                    s.g0 = 0 if s.q else s.nq
                    s.g1 = s.nq + s.nk
                    s.stacks = list(range(s.g0, 6))
                    s.uses = [s.stacks[i:i + 3] for i in range(0, len(s.stacks), 3)]
                    s.rope = s.t >= CTX_TILES
                    s.bank = OB if g < TT and g % 2 else GEMM
                    s.bank_free = g if g > TT else max(0, g - 1)

            class Item:

                def __init__(s, p, t, j):
                    s.p, s.t, s.j = p, t, j
                    s.diff = p < DIFF_HEADS
                    s.nkt = CTX_TILES if t < CTX_TILES else TT
                    s.keys = s.nkt * P
                    s.last = s.diff or j == GROUP - 1

            preps = [Prep(g) for g in range(NPANEL * TT)]
            items = [Item(p, t, j) for p in range(NPANEL) for t in q_tiles
                     for j in range(1 if p < DIFF_HEADS else GROUP)]
            lead = TT + 1
            slots = [dict(preps=[], late=[], outs=[], finish=None) for _ in range(lead + len(items) + 4)]
            for t in range(TT):
                slots[t]["preps"] = [preps[t]]
            for p in range(NPANEL - 1):
                first = lead + sum(it.p < p for it in items)
                count = sum(it.p == p for it in items)
                for t in range(TT):
                    at = (t * count // TT - 1) if count <= TT else max(0, (t + 1) * count // TT - 4)
                    slots[first + at]["preps"].append(preps[(p + 1) * TT + t])
            for n, sl in enumerate(slots):
                if sl["preps"]:
                    q = sl["preps"][-1]
                    scored = lead + sum(it.p < q.p for it in items)
                    lag = 1
                    if not q.diff:
                        while lag < 3 and not slots[n + lag]["preps"] and n + lag + 1 < scored:
                            lag += 1
                    slots[n + lag]["late"] = [q]
                    slots[n + (lag > 1)]["finish"] = q
            for sl in slots:
                sl["at_once"], sl["between"] = [], []
            for j in range(3):
                slots[len(slots) - 10 + j]["between"].append(3 * NPANEL + j)
            for p in range(1, NPANEL):
                end = [n for n, sl in enumerate(slots) if any(q.p == p - 1 for q in sl["preps"])][-1]
                start = [n for n, sl in enumerate(slots) if any(q.p == p for q in sl["preps"])][0]
                for u in range(3):
                    if start == end + 1:
                        slots[end]["at_once"].append(3 * p + u)
                    else:
                        slots[end + u * (start - end) // 3]["between"].append(3 * p + u)

            def nth(n):
                return items[n] if 0 <= n < len(items) else None

            for n, sl in enumerate(slots):
                sl["score"], sl["turn"], sl["weigh"], sl["weighed"] = (nth(n - lead - lag) for lag in range(4))
                if sl["weigh"] is not None and sl["weigh"].last:
                    slots[n + 2]["outs"].append(sl["weigh"])
            n_score = n_use = n_ptuse = n_stuse = n_out = n_norm = n_dsq = 0
            readers = []
            for i, it in enumerate(items):
                it.i, it.scores = i, []
                for _ in range(2 if it.diff else 1):
                    it.scores.append(n_score)
                    n_score += 1
            for sl in slots:
                for o in sl["outs"]:
                    o.ouse = n_use
                    n_out += 1
                    readers.append((o_out, n_out))
                    n_use += 1
                it = sl["turn"]
                if it is not None:
                    it.use0, it.pt0 = n_use, n_ptuse
                    it.ptuses = [list(range(k, min(k + 3, it.nkt))) for k in range(0, it.nkt, 3)]
                    for _ in it.ptuses:
                        n_ptuse += 1
                        readers.append((pt_lo, n_ptuse))
                        n_use += 1
                for q in sl["late"] + sl["preps"][:-1]:
                    q.use0, q.st0 = n_use, n_stuse
                    for _ in q.uses:
                        n_stuse += 1
                        readers.append((stacks_in, n_stuse))
                        n_use += 1
            kept = []
            for it in items:
                it.before = kept[n_norm - 2] if n_norm >= 2 else None
                if it.last:
                    kept.append(it)
                it.nrm = n_norm
                n_norm += it.last
                if it.diff:
                    it.dsq = n_dsq
                    n_dsq += 1
            gq = [q for q in preps if not q.diff]
            for n, q in enumerate(gq):
                q.hn, q.roped_before = n, sum(x.rope for x in gq[:n])

            with ExitStack() as z:
                qk = [sb(f"qk{b}_{layer}", [P, 6, T], F32R, z) for b in range(2)]
                vhi = [sb(f"vhi{b}_{layer}", [P, TT, 2 * HD], F32R, z) for b in range(3)]
                vlo = [sb(f"vlo{b}_{layer}", [P, TT, 2 * HD], F32R, z) for b in range(3)]
                e = [[sb(f"e{b}{s}_{layer}", [P, T], F32, z) for s in range(2)] for b in range(2)]
                pth = [sb(f"pth{b}_{layer}", [P, TT, P], F32R, z) for b in range(2)]
                ptl = [sb(f"ptl{b}_{layer}", [P, TT, P], F32R, z) for b in range(2)]
                ra = sb(f"ra_{layer}", [P, 5, HD], F32, z)
                rc = sb(f"rc_{layer}", [P, 5, HD], F32, z)
                st = sb(f"st_{layer}", [P, 6, 2 * HD], F32R, z)
                hsq = sb(f"hsq_{layer}", [P, 5, HD], F32, z)
                rd = sb(f"rd_{layer}", [P, 5, HD], F32, z)
                hss = sb(f"hss_{layer}", [P, 5], F32, z)
                hvar = sb(f"hvar_{layer}", [P, 5], F32, z)
                hpow = sb(f"hpow_{layer}", [P, 5], F32, z)
                mx = sb(f"mx_{layer}", [P, 2], F32, z)
                nmx = sb(f"nmx_{layer}", [P, 2, 2], F32, z)
                esum = sb(f"esum_{layer}", [P, 2, 2], F32, z)
                rec = sb(f"rec_{layer}", [P, 3, 2], F32, z)
                rlam = sb(f"rlam_{layer}", [P, 1], F32, z)
                osb = sb(f"osb_{layer}", [P, 2, P], F32, z)
                osq = sb(f"osq_{layer}", [P, P], F32, z)
                oss = sb(f"oss_{layer}", [P, 1], F32, z)
                ovar = sb(f"ovar_{layer}", [P, 1], F32, z)
                opow = sb(f"opow_{layer}", [P, 1], F32, z)
                onrm = sb(f"onrm_{layer}", [P, 2, 2 * P], F32, z)
                block = z.enter_context(nc.Block())

                @block.sync
                def _(sp):
                    for n in range(RAW, 3 * NPANEL):
                        sp.wait_ge(lo_ready, ph.base + n - RAW + 1)
                        load_attention(sp, ph, layer, n)
                    for j in range(RAW):
                        sp.wait_ge(lo_ready, ph_next.first_raw[ph_next.raws[j]])
                        load_pooling(sp, ph_next, layer, j)

                @block.tensor
                def _(pe):
                    def gemm(q):
                        pe.wait_ge(lo_ready, ph.base + 3 * q.p + 3)
                        if q.bank_free:
                            pe.wait_ge(act_read, q.bank_free)
                            pe.wait_ge(dve_read, q.bank_free)
                        u0 = 0 if q.q else (1 if q.diff else 2)
                        o = psum[:, q.bank, u0 * P:3 * P]
                        tok = slice(q.t * P, (q.t + 1) * P)
                        for k in range(KT):
                            for n, (x, w) in enumerate(((Hhi, whi3), (Hhi, wlo3), (Hlo, whi3))):
                                mm = nc.tensor.matmul(o, x[:, k, tok], w[:, u0:3, k, :],
                                                      start=k == 0 and n == 0, stop=k == KT - 1 and n == 2)
                        mm.then_inc(gemm_done, 1)

                    def bank(use):
                        if use >= NTR:
                            pe.wait_ge(*readers[use - NTR])
                        return psum[:, TR + use % NTR]

                    def turn_stacks(q):
                        pe.wait_ge(stack_hi, q.g + 1)
                        pe.wait_ge(stack_lo, q.g + 1)
                        for u, group in enumerate(q.uses):
                            b = bank(q.use0 + u)
                            for n, sx in enumerate(group):
                                mm = nc.tensor.transpose(b[:, n * P:(n + 1) * P], st[:, sx, :].bitcast(F32), ident[:])
                            mm.then_inc(turned, 1)

                    def score(it):
                        b = qk[it.p % 2]
                        pe.wait_ge(stacks_in, preps[it.p * TT + TT - 1].st0 + len(preps[it.p * TT + TT - 1].uses))
                        tok = slice(it.t * P, (it.t + 1) * P)
                        for s, n in enumerate(it.scores):
                            if n >= 2:
                                pe.wait_ge(exped, n - 1)
                            qs = s if it.diff else it.j
                            ks = (2 + s, 4 + s) if it.diff else (4, 5)
                            for c in range((it.keys + 383) // 384):
                                w = min(384, it.keys)
                                for m in range(2):
                                    mm = nc.tensor.matmul(psum[:, SBANK + 2 * (n % 2) + c, 0:w], b[:, qs, tok],
                                                          b[:, ks[m], c * 384:c * 384 + w], start=m == 0, stop=m == 1)
                            mm.then_inc(scores, 1)

                    def turn_probs(it):
                        pe.wait_ge(probs, it.i + 1)
                        for u, kts in enumerate(it.ptuses):
                            b = bank(it.use0 + u)
                            for n, kt in enumerate(kts):
                                mm = nc.tensor.transpose(b[:, n * P:(n + 1) * P],
                                                         e[it.i % 2][0][:, kt * P:(kt + 1) * P], ident[:])
                            mm.then_inc(turned, 1)

                    def weigh(it):
                        pe.wait_ge(pt_hi, it.pt0 + len(it.ptuses))
                        pe.wait_ge(pt_lo, it.pt0 + len(it.ptuses))
                        if it.i:
                            pe.wait_ge(o_read, it.i)
                        x, y = pth[it.i % 2], ptl[it.i % 2]
                        vh, vl = vhi[it.p % 3], vlo[it.p % 3]
                        for kt in range(it.nkt):
                            terms = (((x, vh, 2 * HD), (x, vl, 2 * HD), (y, vh, 2 * HD)) if it.diff else
                                     ((x, vh, 2 * HD), (y, vh, HD)))
                            for n, (w, v, wd) in enumerate(terms):
                                mm = nc.tensor.matmul(psum[:, OB, 0:wd], w[:, kt, :], v[:, kt, 0:wd],
                                                      start=kt == 0 and n == 0,
                                                      stop=kt == it.nkt - 1 and n == len(terms) - 1)
                        mm.then_inc(pv_done, 1)

                    def turn_out(it):
                        if it.diff:
                            pe.wait_ge(o_norm, it.dsq + 1)
                        else:
                            pe.wait_ge(o_read, it.i + 1)
                        b = bank(it.ouse)
                        for n in range(1 if it.diff else 2):
                            mm = nc.tensor.transpose(b[:, n * P:(n + 1) * P], onrm[:, it.nrm % 2, n * P:(n + 1) * P],
                                                     ident[:])
                        mm.then_inc(turned, 1)

                    for sl in slots:
                        if sl["preps"]:
                            gemm(sl["preps"][0])
                        for o in sl["outs"]:
                            turn_out(o)
                        if sl["score"] is not None:
                            score(sl["score"])
                        if sl["turn"] is not None:
                            turn_probs(sl["turn"])
                        if sl["weigh"] is not None:
                            weigh(sl["weigh"])
                        for q in sl["late"]:
                            turn_stacks(q)
                        if len(sl["preps"]) > 1:
                            gemm(sl["preps"][1])
                            turn_stacks(sl["preps"][0])

                @block.scalar
                def _(act):
                    def weight_hi(n):
                        if n >= 3 * NPANEL:
                            act.wait_ge(gemm_done, TT * NPANEL)
                            return split_hi(act, ph_next, n - 3 * NPANEL, 0, wait_slot=False)
                        act.wait_ge(landed[ph.raws[n]], ph.landed(n, 0))
                        if n >= 3:
                            act.wait_ge(gemm_done, TT * (n // 3))
                        nc.scalar.activation(whi3[:, n % 3].rearrange("p k n -> p (k n)"), raw[ph.raws[n]][:],
                                             ACT.Copy).then_inc(hi_ready, 1)

                    def read_projection(q):
                        act.wait_ge(gemm_done, q.g + 1)
                        if not q.diff:
                            if q.hn:
                                act.wait_ge(head_var, q.hn)
                            nc.scalar.activation(hsq[:, q.g0:q.g1].rearrange("p g d -> p (g d)"),
                                                 psum[:, q.bank, q.g0 * HD:q.g1 * HD], ACT.Square).then_inc(sq_done, 1)
                        nc.scalar.activation(vhi[q.p % 3][:, q.t, 0:q.vd], psum[:, q.bank, 3 * P - q.vd:3 * P], ACT.Copy
                                             ).then_inc(act_read, 1)

                    def stack_his(q):
                        act.wait_ge(roped, q.g + 1)
                        if q.g:
                            last = preps[q.g - 1]
                            act.wait_ge(turned, last.use0 + len(last.uses))
                        if q.q:
                            nc.scalar.activation(st[:, 0:q.nq, 0:HD], rc[:, 0:q.nq], ACT.Copy)
                        k0 = q.nq
                        src = rc[:, q.nq:q.g1].rearrange("p g (o d) -> p g o d", o=1).broadcast_to([P, q.nk, 2, HD])
                        nc.scalar.activation(st[:, k0:k0 + q.nk].rearrange("p s (o d) -> p s o d", o=2), src, ACT.Copy
                                             ).then_inc(stack_hi, 1)

                    def keep_stacks(q):
                        for u, group in enumerate(q.uses):
                            act.wait_ge(turned, q.use0 + u + 1)
                            nc.scalar.activation(qk[q.p % 2][:, group[0]:group[-1] + 1, q.t * P:(q.t + 1) * P],
                                                 psum[:, TR + (q.use0 + u) % NTR, 0:len(group) * P]
                                                 .rearrange("p (s n) -> p s n", n=P), ACT.Copy).then_inc(stacks_in, 1)

                    def exps(it):
                        for s, n in enumerate(it.scores):
                            act.wait_ge(negmax, n + 1)
                            src = psum[:, SBANK + 2 * (n % 2):SBANK + 2 * (n % 2) + 2, 0:384]
                            dst = e[it.i % 2][s][:].rearrange("p (c w) -> p c w", c=2)
                            if it.keys < T:
                                src, dst = psum[:, SBANK + 2 * (n % 2), 0:it.keys], e[it.i % 2][s][:, 0:it.keys]
                            nc.scalar.activation(dst, src, ACT.Exp, bias=nmx[:, it.i % 2, s:s + 1], scale=SCALE,
                                                 accum_out=esum[:, it.i % 2, s:s + 1]).then_inc(exped, 1)

                    def keep_probs(it):
                        for u, kts in enumerate(it.ptuses):
                            act.wait_ge(turned, it.use0 + u + 1)
                            nc.scalar.activation(pth[it.i % 2][:, kts[0]:kts[-1] + 1, :],
                                                 psum[:, TR + (it.use0 + u) % NTR, 0:len(kts) * P]
                                                 .rearrange("p (s n) -> p s n", n=P), ACT.Copy).then_inc(pt_hi, 1)

                    def keep_output(it):
                        act.wait_ge(turned, it.ouse + 1)
                        b = psum[:, TR + it.ouse % NTR]
                        tok = slice(it.t * P, (it.t + 1) * P)
                        if it.diff:
                            nc.scalar.activation(A[:, it.p, tok], b[:, 0:P], ACT.Copy, scale=subg[:, 0:1]
                                                 ).then_inc(o_out, 1)
                        else:
                            f = DIFF_HEADS + 2 * (it.p - DIFF_HEADS)
                            nc.scalar.activation(A[:, f:f + 2, tok], b[:, 0:2 * P].rearrange("p (s n) -> p s n", n=P),
                                                 ACT.Copy).then_inc(o_out, 1)

                    def square_output(it):
                        act.wait_ge(o_read, it.i + 1)
                        if it.dsq:
                            act.wait_ge(o_var, it.dsq)
                        nc.scalar.activation(osq[:], osb[:, it.i % 2], ACT.Square, accum_out=oss[:]
                                             ).then_inc(o_sq, 1)

                    for sl in slots:
                        if sl["weighed"] is not None and sl["weighed"].diff:
                            square_output(sl["weighed"])
                        if sl["preps"]:
                            read_projection(sl["preps"][0])
                        for o in sl["outs"]:
                            keep_output(o)
                        if len(sl["preps"]) == 1:
                            for n in sl["at_once"][:2]:
                                weight_hi(n)
                        if sl["turn"] is not None:
                            keep_probs(sl["turn"])
                        if len(sl["preps"]) == 1:
                            for n in sl["at_once"][2:]:
                                weight_hi(n)
                        if sl["score"] is not None:
                            exps(sl["score"])
                        for q in sl["late"]:
                            keep_stacks(q)
                        if len(sl["preps"]) > 1:
                            stack_his(sl["preps"][0])
                            read_projection(sl["preps"][1])
                            for n in sl["at_once"]:
                                weight_hi(n)
                            keep_stacks(sl["preps"][0])
                        if sl["finish"] is not None:
                            stack_his(sl["finish"])
                        for n in sl["between"]:
                            weight_hi(n)

                @block.vector
                def _(dve):
                    steps = [0]

                    def link(ins):
                        steps[0] += 1
                        ins.then_inc(dchain, 1)
                        dve.wait_ge(dchain, steps[0])

                    def weight_lo(n):
                        if n >= 3 * NPANEL:
                            return split_lo(dve, ph_next, n - 3 * NPANEL, 0)
                        dve.wait_ge(hi_ready, ph.base + n + 1)
                        nc.vector.tensor_tensor(wlo3[:, n % 3].rearrange("p k n -> p (k n)"), raw[ph.raws[n]][:],
                                                whi3[:, n % 3].rearrange("p k n -> p (k n)").bitcast(F32),
                                                ALU.subtract).then_inc(lo_ready, 1)

                    def head_vars(q):
                        dve.wait_ge(sq_done, q.hn + 1)
                        link(nc.vector.tensor_reduce(hss[:, q.g0:q.g1], hsq[:, q.g0:q.g1], AX.X, ALU.add))
                        nc.vector.tensor_scalar(hvar[:, q.g0:q.g1], hss[:, q.g0:q.g1], 1.0 / HD, EPS, ALU.mult, ALU.add
                                                ).then_inc(head_var, 1)

                    def rotate(q, x, between):
                        g0, g1 = q.g0, q.g1

                        def table(tab, first, step):
                            y = tab[:, q.t - CTX_TILES, first::step].rearrange("p (o d) -> p o d", o=1)
                            return y.broadcast_to([P, g1 - g0, HD // step])

                        nc.vector.tensor_tensor(ra[:, g0:g1], x, table(cosT, 0, 1), ALU.mult)
                        nc.vector.tensor_tensor(rd[:, g0:g1, 0::2], x[:, :, 1::2], table(sinT, 0, 2), ALU.mult)
                        sw = nc.vector.tensor_tensor(rd[:, g0:g1, 1::2], x[:, :, 0::2], table(sinT, 1, 2), ALU.mult)
                        if between is not None:
                            between()
                            dve.wait_ge(dve_read, q.g + 1)
                        else:
                            link(sw)
                        nc.vector.tensor_tensor(rc[:, g0:g1], ra[:, g0:g1], rd[:, g0:g1], ALU.add).then_inc(roped, 1)

                    def finish_heads(q):
                        if not q.diff and q.rope:
                            dve.wait_ge(normed, q.roped_before + 1)
                            rotate(q, rc[:, q.g0:q.g1], None)
                        stack_los(q)

                    def shape_heads(q):
                        dve.wait_ge(act_read, q.g + 1)
                        if q.g:
                            dve.wait_ge(stack_lo, q.g)
                        g0, g1 = q.g0, q.g1
                        ng = g1 - g0

                        def values_lo():
                            lo = vlo[q.p % 3][:, q.t, :] if q.diff else vhi[q.p % 3][:, q.t, HD:2 * HD]
                            nc.vector.tensor_tensor(lo, psum[:, q.bank, 3 * P - q.vd:3 * P],
                                                    vhi[q.p % 3][:, q.t, 0:q.vd].bitcast(F32), ALU.subtract
                                                    ).then_inc(dve_read, 1)

                        x = psum[:, q.bank, g0 * HD:g1 * HD].rearrange("p (g d) -> p g d", d=HD)
                        if q.diff and q.rope:
                            rotate(q, x, values_lo)
                        elif q.diff:
                            nc.vector.tensor_copy(rc[:, g0:g1], x).then_inc(roped, 1)
                            values_lo()
                        else:
                            dve.wait_ge(head_pow, q.hn + 1)
                            r = hpow[:, g0:g1].rearrange("p (g o) -> p g o", o=1).broadcast_to([P, ng, HD])
                            nc.vector.tensor_tensor(ra[:, g0:g1], x, r, ALU.mult)
                            values_lo()
                            dve.wait_ge(dve_read, q.g + 1)
                            if q.rope:
                                nc.vector.tensor_tensor(rc[:, g0:g1], ra[:, g0:g1], headG[:, g0:g1], ALU.mult
                                                        ).then_inc(normed, 1)
                            else:
                                nc.vector.tensor_tensor(rc[:, g0:g1], ra[:, g0:g1], headG[:, g0:g1], ALU.mult
                                                        ).then_inc(roped, 1)

                    def stack_los(q):
                        dve.wait_ge(stack_hi, q.g + 1)
                        if q.q:
                            nc.vector.tensor_tensor(st[:, 0:q.nq, HD:2 * HD], rc[:, 0:q.nq],
                                                    st[:, 0:q.nq, 0:HD].bitcast(F32), ALU.subtract)
                        ka, kb = q.nq, q.nq + q.nk
                        src = rc[:, q.nq:q.g1].rearrange("p g (o d) -> p g o d", o=1).broadcast_to([P, q.nk, 2, HD])
                        nc.vector.tensor_tensor(st[:, kb:kb + q.nk].rearrange("p s (o d) -> p s o d", o=2), src,
                                                st[:, ka:ka + q.nk].bitcast(F32)
                                                .rearrange("p s (o d) -> p s o d", o=2), ALU.subtract
                                                ).then_inc(stack_lo, 1)

                    def maxima(it):
                        for s, n in enumerate(it.scores):
                            dve.wait_ge(scores, n + 1)
                            if it.keys < T:
                                link(nc.vector.tensor_reduce(mx[:, s:s + 1], psum[:, SBANK + 2 * (n % 2), 0:it.keys],
                                                             AX.X, ALU.max))
                            else:
                                link(nc.vector.tensor_reduce(
                                    mx[:, s:s + 1], psum[:, SBANK + 2 * (n % 2):SBANK + 2 * (n % 2) + 2, 0:384],
                                    AX.XY, ALU.max))
                            nc.vector.tensor_scalar(nmx[:, it.i % 2, s:s + 1], mx[:, s:s + 1], -SCALE, None, ALU.mult
                                                    ).then_inc(negmax, 1)

                    def normalise(it):
                        b, r = it.i % 2, it.i % 3
                        ns = len(it.scores)
                        dve.wait_ge(exped, it.scores[-1] + 1)
                        if not it.diff:
                            nc.vector.reciprocal(rec[:, r, 0:1], esum[:, b, 0:1]).then_inc(probs, 1)
                            return
                        link(nc.vector.reciprocal(rec[:, r, 0:ns], esum[:, b, 0:ns]))
                        link(nc.vector.tensor_scalar(rlam[:], rec[:, r, 1:2], lam[:, 0:1], None, ALU.mult))
                        link(nc.vector.tensor_scalar(e[b][1][:, 0:it.keys], e[b][1][:, 0:it.keys], rlam[:, 0:1], None,
                                                     ALU.mult))
                        nc.vector.scalar_tensor_tensor(e[b][0][:, 0:it.keys], e[b][0][:, 0:it.keys], rec[:, r, 0:1],
                                                       e[b][1][:, 0:it.keys], ALU.mult, ALU.subtract
                                                       ).then_inc(probs, 1)

                    def probs_lo(it):
                        for u, kts in enumerate(it.ptuses):
                            dve.wait_ge(pt_hi, it.pt0 + u + 1)
                            sl_ = slice(kts[0], kts[-1] + 1)
                            nc.vector.tensor_tensor(ptl[it.i % 2][:, sl_, :],
                                                    psum[:, TR + (it.use0 + u) % NTR, 0:len(kts) * P]
                                                    .rearrange("p (s n) -> p s n", n=P),
                                                    pth[it.i % 2][:, sl_, :].bitcast(F32), ALU.subtract
                                                    ).then_inc(pt_lo, 1)

                    def read_output(it):
                        dve.wait_ge(pv_done, it.i + 1)
                        if it.diff:
                            nc.vector.tensor_copy(osb[:, it.i % 2], psum[:, OB, 0:P]).then_inc(o_read, 1)
                        else:
                            if it.j == 0 and it.before is not None:
                                dve.wait_ge(turned, it.before.ouse + 1)
                            inv = rec[:, it.i % 3, 0:1]
                            part = osb[:, it.i % 2, 0:HD]
                            link(nc.vector.tensor_scalar(part, psum[:, OB, HD:2 * HD], inv, None,
                                                         ALU.mult))
                            nc.vector.scalar_tensor_tensor(onrm[:, it.nrm % 2, it.j * HD:(it.j + 1) * HD],
                                                           psum[:, OB, 0:HD], inv, part, ALU.mult, ALU.add
                                                           ).then_inc(o_read, 1)

                    def output_var(it):
                        dve.wait_ge(o_sq, it.dsq + 1)
                        if it.dsq:
                            dve.wait_ge(o_pow, it.dsq)
                        nc.vector.tensor_scalar(ovar[:], oss[:], 1.0 / (2 * HD), EPS, ALU.mult, ALU.add
                                                ).then_inc(o_var, 1)

                    def output_norm(it):
                        dve.wait_ge(o_pow, it.dsq + 1)
                        if it.before is not None:
                            dve.wait_ge(turned, it.before.ouse + 1)
                        nc.vector.tensor_scalar(onrm[:, it.nrm % 2, 0:P], osb[:, it.i % 2], opow[:, 0:1], None,
                                                ALU.mult).then_inc(o_norm, 1)

                    for sl in slots:
                        done = sl["weighed"] if sl["weighed"] is not None and sl["weighed"].diff else None
                        if done is not None:
                            output_var(done)
                        q, more = (sl["preps"] + [None, None])[:2]
                        one = more is None
                        if q is not None and q.diff:
                            shape_heads(q)
                        elif q is not None:
                            head_vars(q)
                        for n in sl["at_once"][:1] if one else []:
                            weight_lo(n)
                        for what in ((probs_lo, maxima) if q is not None and q.diff else (maxima, probs_lo)):
                            it = sl["turn" if what is probs_lo else "score"]
                            if it is not None:
                                what(it)
                            for n in sl["at_once"][1:] if one and what is probs_lo else []:
                                weight_lo(n)
                        if sl["score"] is not None:
                            normalise(sl["score"])
                        if done is not None:
                            output_norm(done)
                        if sl["weigh"] is not None:
                            read_output(sl["weigh"])
                        if q is not None and not q.diff:
                            shape_heads(q)
                        if more is not None:
                            finish_heads(q)
                            if not more.diff:
                                head_vars(more)
                            shape_heads(more)
                            for n in sl["at_once"]:
                                weight_lo(n)
                        if sl["finish"] is not None:
                            finish_heads(sl["finish"])
                        for n in sl["between"]:
                            weight_lo(n)

                @block.gpsimd
                def _(pool):
                    for n, sl in enumerate(slots):
                        it = sl["weighed"]
                        if it is not None and it.diff:
                            pool.wait_ge(o_var, it.dsq + 1)
                            if it.dsq:
                                pool.wait_ge(o_norm, it.dsq)
                            nc.gpsimd.tensor_tensor(opow[:], ovar[:], mhalf[:, 0:1], ALU.pow).then_inc(o_pow, 1)
                        for q in sl["preps"]:
                            if not q.diff:
                                pool.wait_ge(head_var, q.hn + 1)
                                if q.g:
                                    pool.wait_ge(dve_read, q.g)
                                nc.gpsimd.tensor_tensor(hpow[:, q.g0:q.g1], hvar[:, q.g0:q.g1],
                                                        mhalf[:, q.g0:q.g1], ALU.pow).then_inc(head_pow, 1)

        def wide(layer):
            if layer < DEPTH - 1:
                return [(0, 0, 384), (1, 384, 384)], 0
            return [(0, CTX, SEQ)], CTX

        def grid(ap, layer):
            chunks, t0 = wide(layer)
            return ap[:, t0:T].rearrange("p (c w) -> p c w", c=len(chunks))

        def pair(u, layer):
            chunks, _ = wide(layer)
            return psum[:, 2 * (u % 4):2 * (u % 4) + len(chunks), 0:chunks[0][2]]

        po_step, po_hi, po_lo, po_mm, po_out, po_table, o_hi, o_lo = (
            sem(n) for n in ("po_step", "po_hi", "po_lo", "po_mm", "po_out", "po_table", "o_hi", "o_lo"))
        gate_done, z_done, sig_done, z_read, mix_step, me_hi, me_lo, y_kept = (
            sem(n) for n in ("gate_done", "z_done", "sig_done", "z_read", "mix_step", "me_hi", "me_lo", "y_kept"))
        relu_done, hid_hi, hid_sq, hid_lo, y_done, y_added = (
            sem(n) for n in ("relu_done", "hid_hi", "hid_sq", "hid_lo", "y_done", "y_added"))

        def pooling(layer, Ohi, Olo, ph, ph_next):
            chunks, t0 = wide(layer)
            w_in = a["w_in"][layer].rearrange("(k p) n -> p k n", p=P)
            G, W2 = len(POOL_WINDOWS), T + 4 * ZPAD
            parts = [(o, q, n) for o, q, n in ((ZPAD, 0, CTX), (CTX + 3 * ZPAD, CTX, SEQ)) if q + n > t0]
            per_layer = 1 + sum(g + 4 for g in range(G))

            def step(g):
                return layer * per_layer + 1 + sum(q + 4 for q in range(g))

            with ExitStack() as z:
                zp = sb(f"zp{layer}", [P, W2], F32, z)
                sums = [sb(f"sum{b}_{layer}", [P, W2], F32, z) for b in range(2)]
                inv = sb(f"inv{layer}", [P, T], F32, z)
                block = z.enter_context(nc.Block())

                @block.sync
                def _(sp):
                    sp.wait_ge(lo_ready, ph.base + 1)
                    load_pooling(sp, ph, layer, G)
                    for g in range(G):
                        if g:
                            sp.wait_ge(po_step, step(g) - 1)
                        sp.dma_start(inv[:], a["inv_count"][g:g + 1, :].broadcast_to([P, T])).then_inc(po_table, 16)
                    for j in range(RAW):
                        sp.wait_ge(lo_ready, ph_next.first_raw[ph_next.raws[j]])
                        load_merge(sp, ph_next, layer, j, 0)

                @block.scalar
                def _(act):
                    for j in range(G + 1):
                        if j >= 3:
                            act.wait_ge(landed[ph.raws[j]], ph.landed(j, 0))
                            act.wait_ge(unit_used, ph.used0 + j - 2)
                            n = UNIT if j < G else G * P
                            dst = whi(ph.slots[j]).rearrange("p k n -> p (k n)")
                            nc.scalar.activation(dst[:, 0:n], raw[ph.raws[j]][:, 0:n], ACT.Copy).then_inc(hi_ready, 1)
                        for k in ((), (0, 1), (2, 3), (4, 5), (6, 7))[j]:
                            nc.scalar.activation(Ohi[:, 4 + k, t0:T], A[:, k, t0:T], ACT.Copy).then_inc(o_hi, 1)
                    for g in range(G):
                        act.wait_ge(po_step, step(g + 1))
                        nc.scalar.activation(Ohi[:, g, t0:T], A[:, 4 + g, t0:T], ACT.Copy).then_inc(po_hi, 1)
                    for g in range(G):
                        act.wait_ge(*((po_mm, layer * (G - 1) + g + 1) if g < G - 1 else (unit_used, ph.used0 + G + 1)))
                        nc.scalar.activation(grid(A[:, g], layer), pair(g, layer), ACT.Identity,
                                             scale=vec[:, R_PSC + g:R_PSC + g + 1]).then_inc(po_out, 1)
                        if g == 0:
                            act.wait_ge(unit_used, ph.used0 + G)
                            split_hi(act, ph_next, 0, 0, wait_slot=False)
                        act.wait_ge(po_out, layer * G + g + 1)
                        nc.scalar.activation(Ohi[:, g, t0:T], A[:, g, t0:T], ACT.Copy).then_inc(po_hi, 1)

                @block.tensor
                def _(pe):
                    for g in range(G):
                        pe.wait_ge(lo_ready, ph.base + g + 1)
                        s = ph.slots[g]
                        for k in range(KT):
                            mm = three_terms(pair(g, layer), whi(s)[:, k], wlo(s)[:, k], Hhi[:, k], Hlo[:, k],
                                             chunks, k == 0, k == KT - 1)
                        mm.then_inc(unit_used, 1)
                    pe.wait_ge(lo_ready, ph.base + G + 1)
                    s = ph.slots[G]
                    for g in range(G):
                        pe.wait_ge(po_lo, layer * 2 * G + g + 1)
                        mm = three_terms(pair(g, layer), whi(s)[:, g], wlo(s)[:, g], Ohi[:, g], Olo[:, g],
                                         chunks, True, True)
                        mm.then_inc(po_mm if g < G - 1 else unit_used, 1)

                @block.vector
                def _(dve):
                    nc.vector.memset(zp[:], 0.0).then_inc(po_step, 1)
                    for j in range(G + 1):
                        if j >= 3:
                            dve.wait_ge(hi_ready, ph.index(j, 0) + 1)
                            n = UNIT if j < G else G * P
                            dst = wlo(ph.slots[j]).rearrange("p k n -> p (k n)")
                            hi = whi(ph.slots[j]).rearrange("p k n -> p (k n)").bitcast(F32)
                            nc.vector.tensor_tensor(dst[:, 0:n], raw[ph.raws[j]][:, 0:n], hi[:, 0:n], ALU.subtract
                                                    ).then_inc(lo_ready, 1)
                        for k in ((), (0, 1), (2, 3), (4, 5), (6, 7))[j]:
                            dve.wait_ge(o_hi, 8 * layer + k + 1)
                            nc.vector.tensor_tensor(Olo[:, 4 + k, t0:T], A[:, k, t0:T],
                                                    Ohi[:, 4 + k, t0:T].bitcast(F32), ALU.subtract).then_inc(o_lo, 1)
                    for g in range(G):
                        n = step(g)
                        dve.wait_ge(po_step, n)
                        dve.wait_ge(unit_used, ph.used0 + g + 1)
                        for o, q, ln in parts:
                            for bank, c0, cn in chunks:
                                u, v = max(q, c0), min(q + ln, c0 + cn)
                                if u < v:
                                    ins = nc.vector.tensor_copy(zp[:, o + u - q:o + v - q],
                                                                pair(g, layer)[:, bank, u - c0:v - c0])
                        ins.then_inc(po_step, 1)
                        dve.wait_ge(po_step, n + 1)
                        src, left, right = zp, 0, 0
                        for m in range(g + 1):
                            back, ahead = (1, 0) if m == 0 else (2 ** (m - 1), 2 ** (m - 1))
                            left, right = left + back, right + ahead
                            nc.vector.tensor_tensor(sums[m % 2][:, left:W2 - right],
                                                    src[:, left - back:W2 - right - back],
                                                    src[:, left + ahead:W2 - right + ahead], ALU.add
                                                    ).then_inc(po_step, 1)
                            dve.wait_ge(po_step, n + 2 + m)
                            src = sums[m % 2]
                        mean = sums[(g + 1) % 2]
                        dve.wait_ge(po_table, 16 * (layer * G + g + 1))
                        for o, q, ln in parts:
                            ins = nc.vector.tensor_tensor(mean[:, o:o + ln], src[:, o:o + ln], inv[:, q:q + ln], ALU.mult)
                        ins.then_inc(po_step, 1)
                        dve.wait_ge(po_step, n + 3 + g)
                        dve.wait_ge(o_lo, 8 * layer + 8)
                        for o, q, ln in parts:
                            ins = nc.vector.tensor_tensor(A[:, 4 + g, q:q + ln], mean[:, o:o + ln], zp[:, o:o + ln],
                                                          ALU.subtract)
                        ins.then_inc(po_step, 1)
                        dve.wait_ge(po_hi, layer * 2 * G + g + 1)
                        nc.vector.tensor_tensor(Olo[:, g, t0:T], A[:, 4 + g, t0:T], Ohi[:, g, t0:T].bitcast(F32),
                                                ALU.subtract).then_inc(po_lo, 1)
                    split_lo(dve, ph_next, 0, 0)
                    for g in range(G):
                        dve.wait_ge(po_hi, layer * 2 * G + G + g + 1)
                        nc.vector.tensor_tensor(Olo[:, g, t0:T], A[:, g, t0:T], Ohi[:, g, t0:T].bitcast(F32),
                                                ALU.subtract).then_inc(po_lo, 1)

        def merge(layer, Ohi, Olo, pg):
            chunks, t0 = wide(layer)
            w_in = a["w_in"][layer].rearrange("(k p) n -> p k n", p=P)
            w_out = [a[n][layer].rearrange("(k p) n -> p k n", p=P) for n in ("w_pool_out", "w_diff_out", "w_gqa_out")]
            w_o = a["w_o"][layer].rearrange("(k p) n -> p k n", p=P)
            HK = KT // 2
            po = units.phase([0, 1, 2, 3] * 2, [3, 0, 1, 2] * 2)
            m0 = KT * layer

            with ExitStack() as z:
                fourth_slot(z, f"mix{layer}")
                sig = [sb(f"sig{b}_{layer}", [P, T], F32, z) for b in range(3)]
                block = z.enter_context(nc.Block())

                def pg_used(j, i):
                    return i * pg.B + (pg.used0 + j + 1)

                def A_tile(i, mm):
                    flat = A[:].rearrange("p k t -> p (k t)")
                    n = T - t0
                    ap = flat[:, bass.ds(i * (2 * T) + (mm * T + t0), n)]
                    return ap.rearrange("p (c w) -> p c w", c=len(chunks))

                @block.sync
                def _(sp):
                    with sp.Fori(0, KT // 2 - 1) as i:
                        for j in range(RAW, pg.B + RAW):
                            jj, ahead = j % pg.B, j // pg.B
                            sp.wait_ge(lo_ready, pg.raw_free(jj, i) + pg.B * ahead)
                            load_merge(sp, pg, layer, jj, i, ahead)
                    for j in range(RAW, pg.B):
                        sp.wait_ge(lo_ready, pg.raw_free(j, KT // 2 - 1))
                        load_merge(sp, pg, layer, j, KT // 2 - 1)
                    for j in range(KT):
                        sp.wait_ge(lo_ready, po.raw_free(j, 0))
                        sp.dma_start(slot_view(po.raws[j]), w_o[:, :, j * P:(j + 1) * P]).then_inc(landed[po.raws[j]], 16)

                @block.tensor
                def _(pe):
                    def branch(b, slot, half, u):
                        for k in range(HK):
                            mm_ = three_terms(pair(u, layer), whi(slot)[:, half * HK + k], wlo(slot)[:, half * HK + k],
                                              Ohi[:, 4 * b + k], Olo[:, 4 * b + k], chunks, k == 0, k == HK - 1)
                        return mm_

                    with pe.Fori(0, KT // 2) as i:
                        for j in range(pg.B):
                            mm, u = j // 5, j % 5
                            s = pg.slots[j]
                            pe.wait_ge(lo_ready, pg.index(j, i) + 1)
                            if u == 0:
                                pe.wait_ge(sig_done, i * 6 + (3 * m0 + 3 * mm))
                            elif u == 1:
                                pe.wait_ge(z_read, i * 6 + (3 * m0 + 3 * mm))
                            elif u == 3:
                                pe.wait_ge(sig_done, i * 6 + (3 * m0 + 3 * mm + 2))
                            if u < 3:
                                for k in range(KT):
                                    last = three_terms(pair(mm * 6 + u, layer), whi(s)[:, k], wlo(s)[:, k], Hhi[:, k],
                                                       Hlo[:, k], chunks, k == 0, k == KT - 1)
                                last.then_inc(unit_used, 1)
                            elif u == 3:
                                branch(0, s, 0, mm * 6 + 3).then_inc(z_done, 1)
                                branch(1, s, 1, mm * 6 + 4).then_inc(unit_used, 1)
                            else:
                                branch(2, s, 0, mm * 6 + 5).then_inc(unit_used, 1)
                    pe.wait_ge(z_read, 3 * (m0 + KT))
                    for j in range(KT):
                        s = po.slots[j]
                        pe.wait_ge(lo_ready, po.base + j + 1)
                        if j >= 4:
                            pe.wait_ge(y_kept, m0 + j - 3)
                        for k in range(KT):
                            if j == 0:
                                pe.wait_ge(me_lo, m0 + k + 1)
                            mm_ = three_terms(pair(j, layer), whi(s)[:, k], wlo(s)[:, k], Hhi[:, k], Hlo[:, k],
                                              chunks, k == 0, k == KT - 1)
                        mm_.then_inc(unit_used, 1)

                @block.scalar
                def _(act):
                    with act.Fori(0, KT // 2) as i:
                        for j in range(pg.B):
                            mm, u = j // 5, j % 5
                            split_hi(act, pg, (j + 1) % pg.B, i + (j + 1) // pg.B if j + 1 == pg.B else i)
                            if u < 3:
                                act.wait_ge(unit_used, pg_used(j, i))
                                act.wait_ge(z_read, i * 6 + (3 * m0 + 3 * mm))
                                act.wait_ge(mix_step, i * 4 + (2 * m0 + 2 * mm))
                                nc.scalar.activation(grid(sig[u], layer), pair(mm * 6 + u, layer), ACT.Sigmoid
                                                     ).then_inc(sig_done, 1)
                    act.wait_ge(unit_used, po.used0)
                    for k in range(KT):
                        act.wait_ge(mix_step, 2 * (m0 + k + 1))
                        nc.scalar.activation(Hhi[:, k, t0:T], A[:, k, t0:T], ACT.Copy).then_inc(me_hi, 1)
                    for j in range(KT):
                        if j + 1 < KT:
                            split_hi(act, po, j + 1, 0)
                        act.wait_ge(unit_used, po.used0 + j + 1)
                        if j == 0:
                            act.wait_ge(me_lo, m0 + KT)
                        nc.scalar.activation(grid(A[:, j], layer), pair(j, layer), ACT.Copy).then_inc(y_kept, 1)

                @block.vector
                def _(dve):
                    with dve.Fori(0, KT // 2) as i:
                        for j in range(pg.B):
                            mm, u = j // 5, j % 5
                            split_lo(dve, pg, (j + 1) % pg.B, i + (j + 1) // pg.B if j + 1 == pg.B else i)
                            if u < 3:
                                continue
                            n3, n2 = i * 6 + (3 * m0 + 3 * mm), i * 4 + (2 * m0 + 2 * mm)
                            dst = A_tile(i, mm)
                            for b in ((0, 1) if u == 3 else (2,)):
                                src = pair(mm * 6 + 3 + b, layer)
                                if b == 0:
                                    dve.wait_ge(z_done, i * 2 + (m0 + mm + 1))
                                else:
                                    dve.wait_ge(unit_used, pg_used(j, i))
                                dve.wait_ge(sig_done, n3 + (b + 1))
                                g = grid(sig[b], layer)
                                nc.vector.tensor_tensor(dst if b == 0 else g, src, g, ALU.mult).then_inc(z_read, 1)
                                if b:
                                    dve.wait_ge(z_read, n3 + (b + 1))
                                    if b == 2:
                                        dve.wait_ge(mix_step, n2 + 1)
                                    nc.vector.tensor_tensor(dst, dst, g, ALU.add).then_inc(mix_step, 1)
                    for k in range(KT):
                        dve.wait_ge(me_hi, m0 + k + 1)
                        nc.vector.tensor_tensor(Hlo[:, k, t0:T], A[:, k, t0:T], Hhi[:, k, t0:T].bitcast(F32),
                                                ALU.subtract).then_inc(me_lo, 1)
                    for j in range(KT - 1):
                        split_lo(dve, po, j + 1, 0)

        def mlp(layer, pa):
            chunks, t0 = wide(layer)
            w1 = a["w_ff1"][layer].rearrange("(k p) n -> p k n", p=P)
            w2 = a["w_ff2"][layer].rearrange("(r p) n -> p r n", p=P)
            MB = FB // P
            HK = MB
            ring = [0, 1, 2, 3]
            rr = [3, 0, 1, 2]
            pb = units.phase(ring * 4, rr * 4, NB // 2 - 1)
            pc = units.phase(ring * 3, rr * 3)
            h0, y0 = NB * MB * layer, (NB + 1) * KT * layer

            with ExitStack() as z:
                fourth_slot(z, f"mlp{layer}")
                hhi = [sb(f"hhi{b}_{layer}", [P, MB, T], F32R, z) for b in range(2)]
                hlo = [sb(f"hlo{b}_{layer}", [P, MB, T], F32R, z) for b in range(2)]
                rt = [sb(f"rt{b}_{layer}", [P, T], F32, z) for b in range(2)]
                h2 = sb(f"h2_{layer}", [P, T], F32, z)
                block = z.enter_context(nc.Block())

                def up(ph, j0, blk):
                    return [(ph, j0 + m, "up", blk, m) for m in range(MB)]

                def down(ph, j0, blk):
                    return [(ph, j0 + m, "down", blk, m) for m in range(KT // 2)]

                plan_a = up(pa, 0, (0, 0))
                plan_b = up(pb, 0, (2, 1)) + down(pb, 4, (2, 0)) + up(pb, 8, (2, 2)) + down(pb, 12, (2, 1))
                plan_c = up(pc, 0, (0, NB - 1)) + down(pc, 4, (0, NB - 2)) + down(pc, 8, (0, NB - 1))

                def run(eng, body):
                    body(0, plan_a, (pb, 0, 0))
                    with eng.Fori(0, NB // 2 - 1) as i:
                        body(i, plan_b, (pb, 0, 1))
                    body(0, plan_c, None)

                def at(i, lin):
                    return i * lin[0] + lin[1] if lin[0] else lin[1]

                def parity(blk):
                    return blk[1] % 2

                def pair_uses(plan):
                    n, got = 0, []
                    for _, _, kind, _, _ in plan:
                        got.append(n)
                        n += 1 if kind == "up" else 2
                    return got

                @block.sync
                def _(sp):
                    def body(i, plan, _):
                        for ph, j, kind, blk, m in plan:
                            if ph is pa:
                                continue
                            s = ph.raws[j]
                            if kind == "up":
                                off, dst, src, n = at(i, (blk[0] * FB, blk[1] * FB + m * P)), slot_view(s), w1, P
                            else:
                                off, dst, src, n = at(i, (blk[0] * HK, blk[1] * HK)), slot_view(s, HK), w2, HK
                            sp.wait_ge(lo_ready, ph.raw_free(j, i))
                            src = src[:, :, bass.ds(off, P)] if kind == "up" else \
                                src[:, bass.ds(off, HK), m * 2 * P:(m + 1) * 2 * P]
                            sp.dma_start(dst, src).then_inc(landed[s], 16)
                    run(sp, body)

                @block.tensor
                def _(pe):
                    def body(i, plan, _):
                        for (ph, j, kind, blk, m), u in zip(plan, pair_uses(plan)):
                            s = ph.slots[j]
                            pe.wait_ge(lo_ready, ph.index(j, i) + 1)
                            if kind == "up":
                                if blk != (0, 0):
                                    pe.wait_ge(relu_done, at(i, (blk[0] * MB, h0 + (blk[1] - 1) * MB + m + 1)))
                                    pe.wait_ge(y_added, at(i, (blk[0] * KT, y0 + (blk[1] - 1) * KT + KT // 2 + m + 1)))
                                for k in range(KT):
                                    mm = three_terms(pair(u, layer), whi(s)[:, k], wlo(s)[:, k], Hhi[:, k], Hlo[:, k],
                                                     chunks, k == 0, k == KT - 1)
                                mm.then_inc(unit_used, 1)
                                continue
                            hh, hl = hhi[parity(blk)], hlo[parity(blk)]
                            if m == 0:
                                pe.wait_ge(hid_lo, at(i, (blk[0] * MB, h0 + (blk[1] + 1) * MB)))
                            w_h = whi(s).rearrange("p k n -> p (k n)").rearrange("p (k n) -> p k n", k=HK)
                            w_l = wlo(s).rearrange("p k n -> p (k n)").rearrange("p (k n) -> p k n", k=HK)
                            for q in range(2):
                                n = 2 * m + q
                                if m < 2 and blk != (0, NB - 1):
                                    pe.wait_ge(relu_done, at(i, (blk[0] * MB, h0 + (blk[1] + 1) * MB + n + 1)))
                                else:
                                    pe.wait_ge(y_added, at(i, (blk[0] * KT, y0 + (blk[1] + 1) * KT + n - 3)))
                                for k in range(HK):
                                    mm = three_terms(pair(u + q, layer), w_h[:, k, q * P:(q + 1) * P],
                                                     w_l[:, k, q * P:(q + 1) * P], hh[:, k], hl[:, k], chunks,
                                                     k == 0, k == HK - 1)
                                mm.then_inc(y_done if q == 0 else unit_used, 1)
                    run(pe, body)

                def prefetch(i, plan, n, follow):
                    if n + 1 < len(plan):
                        return plan[n + 1][0], plan[n + 1][1], i
                    if follow is None:
                        return None
                    ph, j, ahead = follow
                    return ph, j, i + 1 if ahead else 0

                @block.scalar
                def _(act):
                    def body(i, plan, follow):
                        for n, ((ph, j, kind, blk, m), u) in enumerate(zip(plan, pair_uses(plan))):
                            nxt = prefetch(i, plan, n, follow)
                            if nxt is not None and (nxt[0] is not pa or nxt[1] >= 3):
                                split_hi(act, *nxt)
                            if kind == "down":
                                continue
                            h = at(i, (blk[0] * MB, h0 + blk[1] * MB + m))
                            r = rt[m % 2]
                            act.wait_ge(unit_used, i * ph.B + (ph.used0 + j + 1))
                            if m >= 2 or blk != (0, 0):
                                act.wait_ge(hid_sq, at(i, (blk[0] * MB, h0 + blk[1] * MB + m - 1)))
                            nc.scalar.activation(grid(r, layer), pair(u, layer), ACT.Relu).then_inc(relu_done, 1)
                            act.wait_ge(relu_done, h + 1)
                            nc.scalar.activation(hhi[parity(blk)][:, m, t0:T], r[:, t0:T], ACT.Square
                                                 ).then_inc(hid_hi, 1)
                    run(act, body)

                @block.vector
                def _(dve):
                    def body(i, plan, follow):
                        for n, ((ph, j, kind, blk, m), u) in enumerate(zip(plan, pair_uses(plan))):
                            nxt = prefetch(i, plan, n, follow)
                            if nxt is not None and (nxt[0] is not pa or nxt[1] >= 3):
                                split_lo(dve, *nxt)
                            if kind == "up":
                                r = rt[m % 2]
                                h = at(i, (blk[0] * MB, h0 + blk[1] * MB + m))
                                dve.wait_ge(relu_done, h + 1)
                                if m or blk != (0, 0):
                                    dve.wait_ge(hid_lo, h)
                                nc.vector.tensor_tensor(h2[:, t0:T], r[:, t0:T], r[:, t0:T], ALU.mult
                                                        ).then_inc(hid_sq, 1)
                                dve.wait_ge(hid_sq, h + 1)
                                dve.wait_ge(hid_hi, h + 1)
                                nc.vector.tensor_tensor(hlo[parity(blk)][:, m, t0:T], h2[:, t0:T],
                                                        hhi[parity(blk)][:, m, t0:T].bitcast(F32), ALU.subtract
                                                        ).then_inc(hid_lo, 1)
                                continue
                            for q in range(2):
                                k = 2 * m + q
                                if q == 0:
                                    dve.wait_ge(y_done, at(i, (blk[0] * KT // 2, y_done0 + blk[1] * (KT // 2) + m + 1)))
                                else:
                                    dve.wait_ge(unit_used, i * ph.B + (ph.used0 + j + 1))
                                dve.wait_ge(y_added, at(i, (blk[0] * KT, y0 + blk[1] * KT + k + 1)))
                                dst = grid(A[:, k], layer)
                                nc.vector.tensor_tensor(dst, pair(u + q, layer), dst, ALU.add).then_inc(y_added, 1)
                    y_done0 = NB * (KT // 2) * layer
                    for k in range(KT):
                        nc.vector.memset(A[:, k, t0:T], 0.0).then_inc(y_added, 1)
                    run(dve, body)

        def middle(layer, tiles, B, ph_next):
            tiles = list(tiles)
            passes = [("Y", tiles[0])]
            for n in range(1, len(tiles)):
                passes += [("Y", tiles[n]), ("x", tiles[n - 1])]
            passes.append(("x", tiles[-1]))
            with ExitStack() as z:
                nm = Norms(z, f"mid{layer}", passes, B, preF, 3 * KT, Y=A, post=postA)
                rl0 = count["reload"]
                count["reload"] += 16
                block = z.enter_context(nc.Block())
                nm.reloaded = (n_reload, rl0 + 16)

                @block.sync
                def _(sp):
                    sp.dma_start(B[:].rearrange("p k t -> p (k t)"), xdram).then_inc(n_reload, 16)
                    for j in range(RAW):
                        load_first_hidden(sp, ph_next, layer, j)
                    sp.wait_ge(*nm.reloaded)
                norm_steps(nm, block, ph_next)

        def ending(layer, tiles, B):
            tiles = list(tiles)
            out_turned, out_kept, out_left = sem("out_turned"), sem("out_kept"), sem("out_left")
            with ExitStack() as z:
                rows = sb("out_rows", [P, SEQ // P, D], F32, z)
                nm = Norms(z, f"end{layer}", [("Y", c) for c in tiles], B, Y=A, post=postF, X_out=A)
                block = z.enter_context(nc.Block())
                blocks = [(g % 3, t, g % 2) for g, t in ((g, g // 2) for g in range(2 * SEQ // P))]
                per_chunk = 2 * CH // P

                @block.scalar
                def _(act):
                    for n in range(len(tiles)):
                        nm.act_square(act, n)

                @block.gpsimd
                def _(pool):
                    for n in range(len(tiles)):
                        nm.pool_root(pool, n)

                @block.tensor
                def _(pe):
                    for n in range(len(tiles)):
                        nm.pe_root(pe, n)
                    for n in range(len(tiles)):
                        nm.pe_spread(pe, n)
                        pe.wait_ge(n_x, nm.nx[n + 1])
                        for g in range(n * per_chunk, (n + 1) * per_chunk):
                            bank, t, h = blocks[g]
                            if g >= 3:
                                pe.wait_ge(out_kept, g - 2)
                            for k in range(4):
                                mm = nc.tensor.transpose(psum[:, XBANK + bank, k * P:(k + 1) * P],
                                                         A[:, 4 * h + k, CTX + t * P:CTX + (t + 1) * P], ident[:])
                            mm.then_inc(out_turned, 1)

                @block.vector
                def _(dve):
                    for n in range(len(tiles)):
                        nm.dve_square(dve, n)
                        nm.dve_root(dve, n)
                    for n in range(len(tiles)):
                        nm.dve_spread(dve, n)
                        nm.dve_apply(dve, n)
                        for g in range(n * per_chunk, (n + 1) * per_chunk):
                            bank, t, h = blocks[g]
                            dve.wait_ge(out_turned, g + 1)
                            nc.vector.tensor_copy(rows[:, t, h * 512:(h + 1) * 512], psum[:, XBANK + bank]
                                                  ).then_inc(out_kept, 1)

                @block.sync
                def _(sp):
                    dst = out.rearrange("b (t p) d -> p (b t) d", p=P)
                    for t in range(SEQ // P):
                        sp.wait_ge(out_kept, 2 * t + 2)
                        sp.dma_start(dst[:, t], rows[:, t]).then_inc(out_left, 16)
                    sp.wait_ge(out_left, 16 * (SEQ // P))

        units.used += MU
        ph_attention = attention_phase(0)
        modulation(0, ph_attention)
        for layer in range(DEPTH):
            tiles = range(NCH) if layer < DEPTH - 1 else range(CTX // CH, NCH)
            ph_pooling = pooling_phase()
            attention(layer, ph_attention, ph_pooling)
            with ExitStack() as outs:
                Ohi = sb(f"Ohi{layer}", [P, 12, T], F32R, outs)
                Olo = sb(f"Olo{layer}", [P, 12, T], F32R, outs)
                ph_merge = merge_phase()
                pooling(layer, Ohi, Olo, ph_pooling, ph_merge)
                merge(layer, Ohi, Olo, ph_merge)
            with ExitStack() as xs:
                B = sb(f"B{layer}", [P, KT, T], F32, xs)
                ph_mlp = mlp_phase()
                middle(layer, tiles, B, ph_mlp)
                mlp(layer, ph_mlp)
                if layer < DEPTH - 1:
                    units.used += MU
                    ph_attention = attention_phase(layer + 1)
                    modulation(layer + 1, ph_attention, B)
                else:
                    ending(layer, tiles, B)


_INS = ["x", "c", "ctx", "c_ctx", "w_mod", "b_mod", "g_pre_mix", "g_post_mix", "g_pre_ffn", "g_post_ffn", "w_in",
        "w_pool_grp", "pool_scale", "lambda_q1", "lambda_k1", "lambda_q2", "lambda_k2", "diff_subln", "gqa_q_norm",
        "gqa_k_norm", "w_pool_out", "w_diff_out", "w_gqa_out", "w_o", "w_ff1", "w_ff2"]


def _constants():
    import numpy as np
    grid_w, pairs = 64, HD // 4
    row = np.repeat(np.arange(SEQ // grid_w), grid_w).astype(np.float32)
    col = np.tile(np.arange(grid_w), SEQ // grid_w).astype(np.float32)
    inv = (1.0 / (np.float32(10000.0) ** (np.arange(pairs, dtype=np.float32) * np.float32(2.0) / np.float32(HD // 2)))
           ).astype(np.float32)
    ang = np.concatenate([row[:, None] * inv, col[:, None] * inv], axis=-1).astype(np.float32)
    cos, sin = np.cos(ang), np.sin(ang)
    inv_count = np.zeros((len(POOL_WINDOWS), T), np.float32)
    for g, w in enumerate(POOL_WINDOWS):
        at = 0
        for n in (CTX, SEQ):
            t = np.arange(n)
            count = np.clip(t + w // 2, 0, n) - np.clip(t - w // 2, 0, n)
            inv_count[g, at:at + n] = 1.0 / count
            at += n
    return {"cos": np.repeat(cos, 2, axis=1).astype(np.float32),
            "sin": np.stack([-sin, sin], axis=-1).reshape(SEQ, HD).astype(np.float32),
            "inv_count": inv_count, "identity": np.eye(P, dtype=np.float32)}


def kernel(**inputs):
    import numpy as _np
    import concourse.bacc as _bacc
    from concourse import mybir as _mybir
    from concourse.bass_utils import run_bass_kernel_spmd as _run

    nc = _bacc.Bacc("TRN2", target_bir_lowering=False, num_devices=1)
    arrays, args = {}, {}
    data = {name: inputs[name] for name in _INS}
    data.update(_constants())
    for name, value in data.items():
        v = _np.ascontiguousarray(value)
        arrays[f"in_{name}"] = v
        args[name] = nc.dram_tensor(f"in_{name}", v.shape, _mybir.dt.from_np(v.dtype), kind="ExternalInput").ap()
    out = nc.dram_tensor("out_0", (1, SEQ, D), _mybir.dt.float32, kind="ExternalOutput").ap()
    build(nc, args, out)
    r = _run(nc, [arrays], core_ids=[0])
    return r.results[0]["out_0"]
```
